# Optimizing a Trainium2 kernel written in Bass

```python
import math
import jax, jax.numpy as jnp
from jax import lax
import numpy as np

D_MODEL = 1024
BATCH = 1
SEQ = 256
DEPTH = 1

N_META = 16
BLK = 128
META_BLK = BLK

MLA_HEADS = 6
MLA_Q_RANK = 256
MLA_KV_RANK = 128
MLA_NOPE = 64
MLA_ROPE = 32
MLA_V = 64
ROPE_THETA = 10000.0

DIFF_HEADS = 4
DIFF_QK = 32
DIFF_V = 2 * DIFF_QK

SWA_HEADS = 6
SWA_KV_HEADS = 2
SWA_HD = 64
WINDOW = 128

REL_BUCKETS = 32
REL_MAX_DIST = 128
N_BIAS_HEADS = DIFF_HEADS + SWA_HEADS

D_FF = -(-(8 * D_MODEL) // (3 * 256)) * 256
NEG_INF = -1e30

IN_WIDTHS = (MLA_Q_RANK, MLA_KV_RANK, MLA_ROPE,
             DIFF_HEADS * 2 * DIFF_QK, DIFF_HEADS * 2 * DIFF_QK, DIFF_HEADS * DIFF_V,
             SWA_HEADS * SWA_HD, SWA_KV_HEADS * SWA_HD, SWA_KV_HEADS * SWA_HD)
D_IN = sum(IN_WIDTHS)
IN_OFFSETS = tuple(sum(IN_WIDTHS[:i + 1]) for i in range(len(IN_WIDTHS) - 1))
D_MIX = MLA_HEADS * MLA_V + DIFF_HEADS * DIFF_V + SWA_HEADS * SWA_HD


def rms_norm(x, g, eps=1e-6):
    xf = x.astype(jnp.float32)
    y = xf * lax.rsqrt(jnp.mean(xf * xf, axis=-1, keepdims=True) + eps)
    return (y * g.astype(jnp.float32)).astype(x.dtype)

def rotate(x, cos, sin):
    x1, x2 = jnp.split(x, 2, axis=-1)
    return jnp.concatenate([x1 * cos - x2 * sin, x2 * cos + x1 * sin], axis=-1)

def t5_bucket(q_pos, k_pos):
    n = jnp.maximum(q_pos - k_pos, 0)
    max_exact = REL_BUCKETS // 2
    nf = jnp.maximum(n, max_exact).astype(jnp.float32)
    large = max_exact + (jnp.log(nf / max_exact) / math.log(REL_MAX_DIST / max_exact)
                         * (REL_BUCKETS - max_exact)).astype(jnp.int32)
    large = jnp.minimum(large, REL_BUCKETS - 1)
    return jnp.where(n < max_exact, n, large)

def masked_softmax(logits, mask):
    z = jnp.where(mask, logits.astype(jnp.float32), NEG_INF)
    return jax.nn.softmax(z, axis=-1)

def mla_mixer(c_q, c_kv, k_rope, q_norm, w_qb, kv_norm, w_kvb, cos, sin, idx, valid):
    B, L, _ = c_q.shape
    q = (rms_norm(c_q, q_norm) @ w_qb).reshape(B, L, MLA_HEADS, MLA_NOPE + MLA_ROPE)
    q_nope = q[..., :MLA_NOPE]
    q_rot = rotate(q[..., MLA_NOPE:], cos[None, :, None], sin[None, :, None])
    kv = (rms_norm(c_kv, kv_norm) @ w_kvb).reshape(B, L, MLA_HEADS, MLA_NOPE + MLA_V)
    k_nope, v = kv[..., :MLA_NOPE], kv[..., MLA_NOPE:]
    k_rot = rotate(k_rope, cos[None], sin[None])
    scale = (MLA_NOPE + MLA_ROPE) ** -0.5

    def one_block(i):
        s = i * BLK
        qn = lax.dynamic_slice_in_dim(q_nope, s, BLK, axis=1)
        qr = lax.dynamic_slice_in_dim(q_rot, s, BLK, axis=1)
        logits = (jnp.einsum('bqhd,bkhd->bhqk', qn, k_nope)
                  + jnp.einsum('bqhd,bkd->bhqk', qr, k_rot)) * scale
        q_idx = s + jnp.arange(BLK)
        mask = (idx[None, :] <= q_idx[:, None]) & valid[None, :]
        p = masked_softmax(logits, mask).astype(v.dtype)
        return jnp.einsum('bhqk,bkhd->bqhd', p, v)

    out = lax.map(one_block, jnp.arange(L // BLK))
    return out.transpose(1, 0, 2, 3, 4).reshape(B, L, MLA_HEADS * MLA_V)

def diff_mixer(q, k, v, lam_p, sub_g, lam_init, bias_tab, pos, idx, valid):
    B, L, _ = q.shape
    q = q.reshape(B, L, DIFF_HEADS, 2, DIFF_QK)
    k = k.reshape(B, L, DIFF_HEADS, 2, DIFF_QK)
    v = v.reshape(B, L, DIFF_HEADS, DIFF_V)
    lp = lam_p.astype(jnp.float32)
    lam = jnp.exp(jnp.sum(lp[0] * lp[1])) - jnp.exp(jnp.sum(lp[2] * lp[3])) + lam_init
    scale = DIFF_QK ** -0.5

    def one_block(i):
        s = i * BLK
        qb = lax.dynamic_slice_in_dim(q, s, BLK, axis=1)
        q_idx = s + jnp.arange(BLK)
        q_pos = lax.dynamic_slice_in_dim(pos, s, BLK)
        bias = bias_tab[t5_bucket(q_pos[:, None], pos[None, :])]
        bias = bias.transpose(2, 0, 1).astype(jnp.float32)
        logits = jnp.einsum('bqhcd,bkhcd->bchqk', qb, k).astype(jnp.float32) * scale + bias[None, None]
        mask = (idx[None, :] <= q_idx[:, None]) & valid[None, :]
        p = masked_softmax(logits, mask)
        attn = (p[:, 0] - lam * p[:, 1]).astype(v.dtype)
        return jnp.einsum('bhqk,bkhd->bqhd', attn, v)

    out = lax.map(one_block, jnp.arange(L // BLK))
    out = out.transpose(1, 0, 2, 3, 4).reshape(B, L, DIFF_HEADS, DIFF_V)
    out = rms_norm(out, sub_g) * (1.0 - lam_init)
    return out.reshape(B, L, DIFF_HEADS * DIFF_V)

def swa_mixer(q, k, v, sinks, bias_tab, pos, real):
    B, L, _ = q.shape
    nb = L // BLK
    G, R = SWA_KV_HEADS, SWA_HEADS // SWA_KV_HEADS
    qb = q.reshape(B, nb, BLK, G, R, SWA_HD)
    kb = k.reshape(B, nb, BLK, G, SWA_HD)
    vb = v.reshape(B, nb, BLK, G, SWA_HD)

    def band(t, meta):
        prev = jnp.concatenate([t[:, :1], t[:, :-1]], axis=1)
        meta_b = jnp.broadcast_to(meta[:, None], (B, nb) + meta.shape[1:])
        return jnp.concatenate([meta_b, prev, t], axis=2)

    keys = band(kb, k.reshape(B, L, G, SWA_HD)[:, :N_META])
    vals = band(vb, v.reshape(B, L, G, SWA_HD)[:, :N_META])
    K = N_META + 2 * BLK
    blk = jnp.arange(nb)
    ar = jnp.arange(BLK)
    q_idx = blk[:, None] * BLK + ar[None, :]
    prev_idx = jnp.maximum(blk - 1, 0)[:, None] * BLK + ar[None, :]
    k_idx = jnp.concatenate([jnp.broadcast_to(jnp.arange(N_META), (nb, N_META)), prev_idx, q_idx], axis=1)
    in_band = jnp.arange(K) >= N_META
    q_pos, k_pos = pos[q_idx], pos[k_idx]
    causal = k_idx[:, None, :] <= q_idx[:, :, None]
    window_ok = (q_pos[:, :, None] - k_pos[:, None, :]) < WINDOW
    mask = causal & jnp.where(in_band[None, None, :], real[k_idx][:, None, :] & window_ok, True)
    bias = bias_tab[t5_bucket(q_pos[:, :, None], k_pos[:, None, :])]
    bias = bias.transpose(0, 3, 1, 2).reshape(nb, G, R, BLK, K).astype(jnp.float32)
    logits = jnp.einsum('bnqgrd,bnkgd->bngrqk', qb, keys).astype(jnp.float32) * (SWA_HD ** -0.5) + bias[None]
    logits = jnp.where(mask[None, :, None, None], logits, NEG_INF)
    sink = sinks.astype(jnp.float32).reshape(G, R)[None, None, :, :, None, None]
    m = jnp.maximum(jnp.max(logits, axis=-1, keepdims=True), sink)
    p = jnp.exp(logits - m)
    p = p / (jnp.sum(p, axis=-1, keepdims=True) + jnp.exp(sink - m))
    out = jnp.einsum('bngrqk,bnkgd->bnqgrd', p.astype(v.dtype), vals)
    return out.reshape(B, L, SWA_HEADS * SWA_HD)

def first_inputs(seed: int = 0) -> dict:
    key = jax.random.key(seed)
    ks = jax.random.split(key, 20)
    n = jax.random.normal
    f32 = jnp.float32
    return {
        "x": n(ks[0], (BATCH, SEQ, D_MODEL), f32),
        "meta_tokens": n(ks[1], (N_META, D_MODEL), f32),
        "rel_bias": 0.5 * n(ks[2], (REL_BUCKETS, N_BIAS_HEADS), f32),
        "attn_norm": 1.0 + 0.02 * n(ks[3], (DEPTH, D_MODEL), f32),
        "w_in": n(ks[4], (DEPTH, D_MODEL, D_IN), f32) * D_MODEL ** -0.5,
        "mla_q_norm": 1.0 + 0.02 * n(ks[5], (DEPTH, MLA_Q_RANK), f32),
        "mla_w_qb": n(ks[6], (DEPTH, MLA_Q_RANK, MLA_HEADS * (MLA_NOPE + MLA_ROPE)), f32) * MLA_Q_RANK ** -0.5,
        "mla_kv_norm": 1.0 + 0.02 * n(ks[7], (DEPTH, MLA_KV_RANK), f32),
        "mla_w_kvb": n(ks[8], (DEPTH, MLA_KV_RANK, MLA_HEADS * (MLA_NOPE + MLA_V)), f32) * MLA_KV_RANK ** -0.5,
        "diff_lambda": 0.1 * n(ks[9], (DEPTH, 4, DIFF_QK), f32),
        "diff_subln": 1.0 + 0.02 * n(ks[10], (DEPTH, DIFF_V), f32),
        "swa_sinks": n(ks[11], (DEPTH, SWA_HEADS), f32),
        "w_out": n(ks[12], (DEPTH, D_MIX, D_MODEL), f32) * D_MIX ** -0.5,
        "ffn_norm": 1.0 + 0.02 * n(ks[13], (DEPTH, D_MODEL), f32),
        "w_gate": n(ks[14], (DEPTH, D_MODEL, D_FF), f32) * D_MODEL ** -0.5,
        "w_up": n(ks[15], (DEPTH, D_MODEL, D_FF), f32) * D_MODEL ** -0.5,
        "w_down": n(ks[16], (DEPTH, D_FF, D_MODEL), f32) * D_FF ** -0.5,
        "final_norm": 1.0 + 0.02 * n(ks[17], (D_MODEL,), f32),
    }

def first_block(x, meta_tokens, rel_bias, attn_norm, w_in, mla_q_norm, mla_w_qb, mla_kv_norm, mla_w_kvb,
              diff_lambda, diff_subln, swa_sinks, w_out, ffn_norm, w_gate, w_up, w_down, final_norm):
    B = x.shape[0]
    meta = jnp.broadcast_to(meta_tokens.astype(x.dtype)[None], (B, N_META, D_MODEL))
    pad = jnp.zeros((B, META_BLK - N_META, D_MODEL), x.dtype)
    h = jnp.concatenate([meta, pad, x], axis=1)
    L = h.shape[1]
    idx = jnp.arange(L)
    real = idx >= META_BLK
    valid = real | (idx < N_META)
    pos = jnp.where(real, idx - META_BLK + N_META, jnp.minimum(idx, N_META - 1))
    inv_freq = ROPE_THETA ** (-jnp.arange(0, MLA_ROPE, 2, dtype=jnp.float32) / MLA_ROPE)
    ang = pos.astype(jnp.float32)[:, None] * inv_freq[None, :]
    cos, sin = jnp.cos(ang).astype(x.dtype), jnp.sin(ang).astype(x.dtype)
    bias_b, bias_c = rel_bias[:, :DIFF_HEADS], rel_bias[:, DIFF_HEADS:]

    for l in range(DEPTH):
        hn = rms_norm(h, attn_norm[l])
        proj = hn @ w_in[l]
        c_q, c_kv, k_rope, dq, dk, dv, sq, sk, sv = jnp.split(proj, IN_OFFSETS, axis=-1)
        y_a = mla_mixer(c_q, c_kv, k_rope, mla_q_norm[l], mla_w_qb[l], mla_kv_norm[l], mla_w_kvb[l],
                        cos, sin, idx, valid)
        lam_init = 0.8 - 0.6 * math.exp(-0.3 * l)
        y_b = diff_mixer(dq, dk, dv, diff_lambda[l], diff_subln[l], lam_init, bias_b, pos, idx, valid)
        y_c = swa_mixer(sq, sk, sv, swa_sinks[l], bias_c, pos, real)
        h = h + jnp.concatenate([y_a, y_b, y_c], axis=-1) @ w_out[l]
        hn = rms_norm(h, ffn_norm[l])
        h = h + (jax.nn.silu(hn @ w_gate[l]) * (hn @ w_up[l])) @ w_down[l]

    h = rms_norm(h, final_norm)
    return h[:, META_BLK:]


DN_HEADS = 8
DN_HEAD_DIM = 128
DN_W = DN_HEADS * DN_HEAD_DIM
DN_CONV = 4
DN_CHUNK = 64
NSA_HEADS = 16
NSA_GROUPS = 4
NSA_REP = NSA_HEADS // NSA_GROUPS
NSA_HEAD_DIM = 64
NSA_W = NSA_HEADS * NSA_HEAD_DIM
NSA_KV_W = NSA_GROUPS * NSA_HEAD_DIM
CMP_LEN = 32
CMP_STRIDE = 16
CMP_HIDDEN = 2 * NSA_HEAD_DIM
SLC_LEN = 64
SLC_TOPK = 8
WINDOW_2 = 256
ATT_QBLK = 128
SLC_QBLK = 64
D_FF_2 = 4 * D_MODEL
IN_WIDTH = 4 * DN_W + 2 * DN_HEADS + NSA_W + 6 * NSA_KV_W + 3 * NSA_HEADS + 2 * D_MODEL
EPS = 1e-6
NEG = -1e30
FORCE = 1e9


def _in_split_points():
    sizes = [3 * DN_W, DN_W, DN_HEADS, DN_HEADS,
             NSA_W, NSA_KV_W, NSA_KV_W, NSA_KV_W, NSA_KV_W, NSA_KV_W, NSA_KV_W, 3 * NSA_HEADS,
             D_MODEL, D_MODEL]
    return [int(v) for v in np.cumsum(sizes)[:-1]]

def rmsnorm(x, gain):
    xf = x.astype(jnp.float32)
    y = xf * lax.rsqrt(jnp.mean(xf * xf, axis=-1, keepdims=True) + EPS)
    return (y * gain.astype(jnp.float32)).astype(x.dtype)

def l2norm(x):
    xf = x.astype(jnp.float32)
    return (xf * lax.rsqrt(jnp.sum(xf * xf, axis=-1, keepdims=True) + EPS)).astype(x.dtype)

def alibi_slopes(n_heads):
    return jnp.asarray(2.0 ** (-8.0 * np.arange(1, n_heads + 1) / n_heads), jnp.float32)

def causal_depthwise_conv(x, w):
    k, c = w.shape
    return lax.conv_general_dilated(x, w[:, None, :].astype(x.dtype), window_strides=(1,),
                                    padding=[(k - 1, 0)], dimension_numbers=('NWC', 'WIO', 'NWC'),
                                    feature_group_count=c)

def chunk_gated_delta_rule(q, k, v, g, beta):
    B, S, H, dk = q.shape
    dv = v.shape[-1]
    C = DN_CHUNK
    N = S // C
    f32 = jnp.float32

    def chunks(t):
        t = t.astype(f32).reshape((B, N, C, H) + t.shape[3:])
        return jnp.moveaxis(t, (1, 3), (0, 2))

    q = chunks(q) * (dk ** -0.5)
    k = chunks(k)
    v = chunks(v)
    beta = chunks(beta)
    gc = jnp.cumsum(chunks(g), axis=-1)
    kb = k * beta[..., None]
    vb = v * beta[..., None]
    causal = jnp.tril(jnp.ones((C, C), bool))
    strict = jnp.tril(jnp.ones((C, C), bool), -1)
    decay = jnp.exp(jnp.where(causal, gc[..., :, None] - gc[..., None, :], -jnp.inf))
    a = jnp.where(strict, jnp.einsum('nbhid,nbhjd->nbhij', kb, k) * decay, 0.0)
    t_mat = a + jnp.eye(C, dtype=f32)
    u = lax.linalg.triangular_solve(t_mat, vb, left_side=True, lower=True)
    w = lax.linalg.triangular_solve(t_mat, kb * jnp.exp(gc)[..., None], left_side=True, lower=True)
    qk = jnp.einsum('nbhid,nbhjd->nbhij', q, k) * decay
    q_dec = q * jnp.exp(gc)[..., None]
    k_end = k * jnp.exp(gc[..., -1:] - gc)[..., None]
    g_last = jnp.exp(gc[..., -1])

    def step(state, inp):
        qd, ke, u_c, w_c, qk_c, gl = inp
        v_new = u_c - jnp.einsum('bhcd,bhde->bhce', w_c, state)
        o = jnp.einsum('bhcd,bhde->bhce', qd, state) + jnp.einsum('bhij,bhje->bhie', qk_c, v_new)
        state = state * gl[..., None, None] + jnp.einsum('bhcd,bhce->bhde', ke, v_new)
        return state, o

    s0 = jnp.zeros((B, H, dk, dv), f32)
    _, o = lax.scan(step, s0, (q_dec, k_end, u, w, qk, g_last))
    return jnp.moveaxis(o, (0, 2), (1, 3)).reshape(B, S, H, dv)

def gated_deltanet(qkv, z, b_logit, a_logit, conv_w, a_log, dt_bias, out_norm):
    B, S, _ = qkv.shape
    f32 = jnp.float32
    qkv = jax.nn.silu(causal_depthwise_conv(qkv, conv_w))
    q, k, v = jnp.split(qkv, 3, axis=-1)
    q = l2norm(q.reshape(B, S, DN_HEADS, DN_HEAD_DIM))
    k = l2norm(k.reshape(B, S, DN_HEADS, DN_HEAD_DIM))
    v = v.reshape(B, S, DN_HEADS, DN_HEAD_DIM)
    beta = jax.nn.sigmoid(b_logit.astype(f32))
    g = -jnp.exp(a_log.astype(f32)) * jax.nn.softplus(a_logit.astype(f32) + dt_bias.astype(f32))
    o = chunk_gated_delta_rule(q, k, v, g, beta)
    o = rmsnorm(o, out_norm) * jax.nn.silu(z.reshape(B, S, DN_HEADS, DN_HEAD_DIM).astype(f32))
    return o.reshape(B, S, DN_W).astype(qkv.dtype)

def cmp_to_slc_overlap(n_cmp, n_sel):
    c0 = np.arange(n_cmp)[:, None] * CMP_STRIDE
    j0 = np.arange(n_sel)[None, :] * SLC_LEN
    ov = np.clip(np.minimum(c0 + CMP_LEN, j0 + SLC_LEN) - np.maximum(c0, j0), 0, None) / CMP_LEN
    return jnp.asarray(ov, jnp.float32)

def compress_blocks(t, pos_emb, w1, w2, idx):
    B, _, G, d = t.shape
    n_cmp = idx.shape[0]
    blk = t[:, idx] + pos_emb[:, None, :].astype(t.dtype)
    blk = jnp.moveaxis(blk, 3, 2).reshape(B, n_cmp, G, CMP_LEN * d)
    return jax.nn.gelu(blk @ w1) @ w2

def window_branch(q, k, v, slopes):
    B, S, G, R, _ = q.shape
    span = WINDOW_2 + ATT_QBLK
    kp = jnp.pad(k, ((0, 0), (WINDOW_2, 0), (0, 0), (0, 0)))
    vp = jnp.pad(v, ((0, 0), (WINDOW_2, 0), (0, 0), (0, 0)))

    def block(i):
        t0 = i * ATT_QBLK
        qb = lax.dynamic_slice_in_dim(q, t0, ATT_QBLK, axis=1)
        kb = lax.dynamic_slice_in_dim(kp, t0, span, axis=1)
        vb = lax.dynamic_slice_in_dim(vp, t0, span, axis=1)
        qpos = t0 + jnp.arange(ATT_QBLK)
        kpos = t0 - WINDOW_2 + jnp.arange(span)
        dist = qpos[:, None] - kpos[None, :]
        mask = (dist >= 0) & (dist < WINDOW_2) & (kpos[None, :] >= 0)
        s = jnp.einsum('bqgrd,bkgd->bgrqk', qb, kb).astype(jnp.float32) - slopes[:, :, None, None] * dist
        p = jax.nn.softmax(jnp.where(mask, s, NEG), axis=-1).astype(vb.dtype)
        return jnp.einsum('bgrqk,bkge->bqgre', p, vb)

    o = lax.map(block, jnp.arange(S // ATT_QBLK))
    return jnp.moveaxis(o, 0, 1).reshape(B, S, G, R, -1)

def selection_branch(q, k, v, sel_idx, slopes):
    B, S, G, R, dk = q.shape
    dv = v.shape[-1]
    n_sel = S // SLC_LEN
    K = sel_idx.shape[-1]
    kblk = jnp.moveaxis(k.reshape(B, n_sel, SLC_LEN, G, dk), 3, 1).reshape(B, G, n_sel, SLC_LEN * dk)
    vblk = jnp.moveaxis(v.reshape(B, n_sel, SLC_LEN, G, dv), 3, 1).reshape(B, G, n_sel, SLC_LEN * dv)
    gather = jax.vmap(jax.vmap(lambda tab, ix: tab[ix]))

    def block(i):
        t0 = i * SLC_QBLK
        qb = lax.dynamic_slice_in_dim(q, t0, SLC_QBLK, axis=1)
        ib = lax.dynamic_slice_in_dim(sel_idx, t0, SLC_QBLK, axis=2)
        flat = ib.reshape(B, G, SLC_QBLK * K)
        kg = gather(kblk, flat).reshape(B, G, SLC_QBLK, K * SLC_LEN, dk)
        vg = gather(vblk, flat).reshape(B, G, SLC_QBLK, K * SLC_LEN, dv)
        kpos = (ib[..., None] * SLC_LEN + jnp.arange(SLC_LEN)).reshape(B, G, SLC_QBLK, K * SLC_LEN)
        qpos = t0 + jnp.arange(SLC_QBLK)
        dist = (qpos[:, None] - kpos)[:, :, None]
        s = jnp.einsum('bqgrd,bgqkd->bgrqk', qb, kg).astype(jnp.float32) - slopes[None, :, :, None, None] * dist
        p = jax.nn.softmax(jnp.where(dist >= 0, s, NEG), axis=-1).astype(vg.dtype)
        return jnp.einsum('bgrqk,bgqke->bqgre', p, vg)

    o = lax.map(block, jnp.arange(S // SLC_QBLK))
    return jnp.moveaxis(o, 0, 1).reshape(B, S, G, R, dv)

def nsa_mixer(q, k_c, v_c, k_s, v_s, k_w, v_w, gate_logits, q_norm, kn_cmp, kn_slc, kn_win,
              cmp_pos_k, cmp_w1_k, cmp_w2_k, cmp_pos_v, cmp_w1_v, cmp_w2_v):
    B, S, _ = q.shape
    G, R, d = NSA_GROUPS, NSA_REP, NSA_HEAD_DIM
    f32 = jnp.float32
    slopes = alibi_slopes(NSA_HEADS).reshape(G, R)
    pos = jnp.arange(S)
    q = (rmsnorm(q.reshape(B, S, NSA_HEADS, d), q_norm) * (d ** -0.5)).reshape(B, S, G, R, d)
    kv = lambda t: t.reshape(B, S, G, d)

    n_cmp = (S - CMP_LEN) // CMP_STRIDE + 1
    idx = np.arange(n_cmp)[:, None] * CMP_STRIDE + np.arange(CMP_LEN)[None, :]
    kc = rmsnorm(compress_blocks(kv(k_c), cmp_pos_k, cmp_w1_k, cmp_w2_k, idx), kn_cmp)
    vc = compress_blocks(kv(v_c), cmp_pos_v, cmp_w1_v, cmp_w2_v, idx)
    cmp_end = jnp.asarray(idx[:, -1])
    dist_c = pos[:, None] - cmp_end[None, :]
    s_c = jnp.einsum('bsgrd,bcgd->bgrsc', q, kc).astype(f32) - slopes[:, :, None, None] * dist_c
    any_valid = (pos >= CMP_LEN - 1).astype(f32)[:, None]
    p_c = jax.nn.softmax(jnp.where(dist_c >= 0, s_c, NEG), axis=-1) * any_valid
    o_cmp = jnp.einsum('bgrsc,bcgd->bsgrd', p_c.astype(vc.dtype), vc)

    n_sel = S // SLC_LEN
    imp = jnp.einsum('bgrsc,cj->bgsj', p_c, cmp_to_slc_overlap(n_cmp, n_sel))
    j = jnp.arange(n_sel)[None, :]
    blk_t = (pos // SLC_LEN)[:, None]
    imp = jnp.where(j <= blk_t, imp, NEG)
    imp = jnp.where((j == blk_t) | (j == 0), FORCE, imp)
    _, sel_idx = lax.top_k(imp, min(SLC_TOPK, n_sel))
    o_slc = selection_branch(q, rmsnorm(kv(k_s), kn_slc), kv(v_s), sel_idx, slopes)

    o_win = window_branch(q, rmsnorm(kv(k_w), kn_win), kv(v_w), slopes)

    gates = jax.nn.sigmoid(gate_logits.astype(f32)).reshape(B, S, G, R, 3)
    o = gates[..., 0:1] * o_cmp + gates[..., 1:2] * o_slc + gates[..., 2:3] * o_win
    return o.reshape(B, S, NSA_W).astype(q.dtype)

def second_inputs(seed: int = 0) -> dict:
    key = jax.random.key(seed)
    ks = jax.random.split(key, 24)
    f32 = jnp.float32
    L = DEPTH

    def nrm(k, shape, scale):
        return jax.random.normal(k, shape, f32) * scale

    def gain(k, n):
        return 1.0 + 0.02 * jax.random.normal(k, (L, n), f32)

    dt = jnp.exp(jax.random.uniform(ks[4], (L, DN_HEADS), f32, math.log(1e-3), math.log(1e-1)))
    flat = CMP_LEN * NSA_HEAD_DIM
    return {
        "x": nrm(ks[0], (BATCH, SEQ, D_MODEL), 1.0),
        "norm_mix": gain(ks[1], D_MODEL),
        "w_in": nrm(ks[2], (L, D_MODEL, IN_WIDTH), D_MODEL ** -0.5),
        "dn_conv": nrm(ks[3], (L, DN_CONV, 3 * DN_W), DN_CONV ** -0.5),
        "dn_a_log": jnp.log(jax.random.uniform(ks[5], (L, DN_HEADS), f32, 1.0, 16.0)),
        "dn_dt_bias": dt + jnp.log(-jnp.expm1(-dt)),
        "dn_out_norm": gain(ks[6], DN_HEAD_DIM),
        "nsa_q_norm": gain(ks[7], NSA_HEAD_DIM),
        "nsa_k_norm_cmp": gain(ks[8], NSA_HEAD_DIM),
        "nsa_k_norm_slc": gain(ks[9], NSA_HEAD_DIM),
        "nsa_k_norm_win": gain(ks[10], NSA_HEAD_DIM),
        "cmp_pos_k": nrm(ks[11], (L, CMP_LEN, NSA_HEAD_DIM), 0.1),
        "cmp_w1_k": nrm(ks[12], (L, flat, CMP_HIDDEN), flat ** -0.5),
        "cmp_w2_k": nrm(ks[13], (L, CMP_HIDDEN, NSA_HEAD_DIM), CMP_HIDDEN ** -0.5),
        "cmp_pos_v": nrm(ks[14], (L, CMP_LEN, NSA_HEAD_DIM), 0.1),
        "cmp_w1_v": nrm(ks[15], (L, flat, CMP_HIDDEN), flat ** -0.5),
        "cmp_w2_v": nrm(ks[16], (L, CMP_HIDDEN, NSA_HEAD_DIM), CMP_HIDDEN ** -0.5),
        "w_proj_dn": nrm(ks[17], (L, DN_W, D_MODEL), DN_W ** -0.5),
        "w_proj_nsa": nrm(ks[18], (L, NSA_W, D_MODEL), NSA_W ** -0.5),
        "w_out": nrm(ks[19], (L, D_MODEL, D_MODEL), D_MODEL ** -0.5),
        "norm_mlp": gain(ks[20], D_MODEL),
        "w_up": nrm(ks[21], (L, D_MODEL, D_FF_2), D_MODEL ** -0.5),
        "w_down": nrm(ks[22], (L, D_FF_2, D_MODEL), D_FF_2 ** -0.5),
    }

def second_block(x, norm_mix, w_in, dn_conv, dn_a_log, dn_dt_bias, dn_out_norm,
              nsa_q_norm, nsa_k_norm_cmp, nsa_k_norm_slc, nsa_k_norm_win,
              cmp_pos_k, cmp_w1_k, cmp_w2_k, cmp_pos_v, cmp_w1_v, cmp_w2_v,
              w_proj_dn, w_proj_nsa, w_out, norm_mlp, w_up, w_down):
    splits = _in_split_points()
    for l in range(DEPTH):
        h = rmsnorm(x, norm_mix[l])
        (dn_qkv, dn_z, dn_b, dn_a, ns_q, ns_kc, ns_vc, ns_ks, ns_vs, ns_kw, ns_vw, ns_gate,
         gate_dn, gate_nsa) = jnp.split(h @ w_in[l], splits, axis=-1)
        o_dn = gated_deltanet(dn_qkv, dn_z, dn_b, dn_a, dn_conv[l], dn_a_log[l], dn_dt_bias[l], dn_out_norm[l])
        o_ns = nsa_mixer(ns_q, ns_kc, ns_vc, ns_ks, ns_vs, ns_kw, ns_vw, ns_gate,
                         nsa_q_norm[l], nsa_k_norm_cmp[l], nsa_k_norm_slc[l], nsa_k_norm_win[l],
                         cmp_pos_k[l], cmp_w1_k[l], cmp_w2_k[l], cmp_pos_v[l], cmp_w1_v[l], cmp_w2_v[l])
        mix = jax.nn.sigmoid(gate_dn) * (o_dn @ w_proj_dn[l]) + jax.nn.sigmoid(gate_nsa) * (o_ns @ w_proj_nsa[l])
        x = x + mix @ w_out[l]
        h2 = rmsnorm(x, norm_mlp[l])
        x = x + jnp.square(jax.nn.relu(h2 @ w_up[l])) @ w_down[l]
    return x


def setup_inputs(seed=0):
    out = dict(first_inputs(seed))
    for name, value in second_inputs(seed + 1).items():
        if name != "x":
            out[name + "_2"] = value
    return out


def reference(
    x, meta_tokens, rel_bias, attn_norm, w_in, mla_q_norm, mla_w_qb, mla_kv_norm, mla_w_kvb,
    diff_lambda, diff_subln, swa_sinks, w_out, ffn_norm, w_gate, w_up, w_down, final_norm,
    norm_mix_2, w_in_2, dn_conv_2, dn_a_log_2, dn_dt_bias_2, dn_out_norm_2, nsa_q_norm_2,
    nsa_k_norm_cmp_2, nsa_k_norm_slc_2, nsa_k_norm_win_2, cmp_pos_k_2, cmp_w1_k_2, cmp_w2_k_2,
    cmp_pos_v_2, cmp_w1_v_2, cmp_w2_v_2, w_proj_dn_2, w_proj_nsa_2, w_out_2, norm_mlp_2, w_up_2,
    w_down_2,
):
    x = first_block(
        x, meta_tokens, rel_bias, attn_norm, w_in, mla_q_norm, mla_w_qb, mla_kv_norm, mla_w_kvb,
        diff_lambda, diff_subln, swa_sinks, w_out, ffn_norm, w_gate, w_up, w_down, final_norm,
    )
    return second_block(
        x, norm_mix_2, w_in_2, dn_conv_2, dn_a_log_2, dn_dt_bias_2, dn_out_norm_2, nsa_q_norm_2,
        nsa_k_norm_cmp_2, nsa_k_norm_slc_2, nsa_k_norm_win_2, cmp_pos_k_2, cmp_w1_k_2,
        cmp_w2_k_2, cmp_pos_v_2, cmp_w1_v_2, cmp_w2_v_2, w_proj_dn_2, w_proj_nsa_2, w_out_2,
        norm_mlp_2, w_up_2, w_down_2,
    )


_drawn_inputs = setup_inputs


def setup_inputs(seed=0):
    import zlib

    import numpy as np

    out = dict(_drawn_inputs(seed))
    spreads = {}
    factors = {'attn_norm': 3.239,
     'mla_q_norm': 8.0,
     'mla_kv_norm': 8.0,
     'diff_lambda': 4.817,
     'diff_subln': 5.139,
     'swa_sinks': 22.869,
     'ffn_norm': 3.308,
     'norm_mix_2': 4.436,
     'dn_out_norm_2': 8.0,
     'nsa_q_norm_2': 8.0,
     'nsa_k_norm_cmp_2': 200.0,
     'nsa_k_norm_slc_2': 81.737,
     'nsa_k_norm_win_2': 92.607,
     'cmp_pos_k_2': 8.0,
     'cmp_pos_v_2': 29.24,
     'norm_mlp_2': 12.533}
    for name, (base, spread) in spreads.items():
        noise = np.random.default_rng([zlib.crc32(name.encode()), seed]).standard_normal(out[name].shape)
        drawn = base * np.exp(spread * noise) if base else spread * noise
        out[name] = __import__('jax').numpy.asarray(drawn.astype(out[name].dtype))
    for name, factor in factors.items():
        out[name] = (out[name] * factor).astype(out[name].dtype)
    return out
```

```python
import math
from contextlib import ExitStack

import numpy as np

import concourse.bass as bass
from concourse import mybir

F32 = mybir.dt.float32
I32 = mybir.dt.int32
ALU = mybir.AluOpType
ACT = mybir.ActivationFunctionType
AXX = mybir.AxisListType.X

P = 128
D = 1024
KD = D // P
SEQ = 256
TT = SEQ // P
META = 16
ALL = META + SEQ
EPS = 1e-6
NEG = -1e30
MH, MQR, MKR, NOPE, ROPE, MV = 6, 256, 128, 64, 32, 64
DH, DQK, DV = 4, 32, 64
SH, SG, SD, WIN = 6, 2, 64, 128
BUCKETS, BH = 32, 10
FF1 = 2816
FT1 = FF1 // P
LAM0 = 0.8 - 0.6 * math.exp(0.0)
LINE = ALL + P - 1
NH2, GH = 8, 4
NSH, NSG, ND = 16, 4, 64
CL, CS, NC = 32, 16, 15
FF2 = 4096
FT2 = FF2 // P
LEVELS = 7
UNIT = 4096
SLOTS = 4

CONST = {}
PARAM = {}


def _place(table, names):
    at = 0
    for name, width in names:
        table[name] = (at, width)
        at += width
    return at


NCONST = _place(CONST, [("ident", P), ("upper", P), ("level", LEVELS * P), ("negdist", 2 * P),
                        ("cmpbias", TT * NSH * NC), ("valid", TT), ("causal", ALL),
                        ("onehot", 2 * LINE), ("cos", ALL), ("sin", ALL)])
NCHELD = CONST["causal"][0]
NEARLY = CONST["onehot"][0]
NPARAM = _place(PARAM, [("attn_norm", KD), ("ffn_norm", KD), ("norm_mix", KD), ("norm_mlp", KD),
                        ("q_norm", MQR // P), ("kv_norm", 1), ("subln", 1), ("dn_out", 1), ("nsa_q", 1),
                        ("k_cmp", 1), ("k_slc", 1), ("k_win", 1), ("conv", 24 * 4), ("w2k", ND),
                        ("w2v", ND), ("pos_k", CL // 2), ("pos_v", CL // 2), ("rel", BH), ("lam", 4 * DQK),
                        ("sinks", SH), ("a_log", NH2), ("dt", NH2), ("small", KD * 64), ("final", D)])
NHELD = NPARAM - D

WIDTHS = {}
for _n in range(3):
    WIDTHS[f"in1f{_n}"] = UNIT
WIDTHS["in1t"] = KD * 384
WIDTHS["mla"] = MH * 2 * P + 2 * MH * 64
WIDTHS["out1_0"] = WIDTHS["out1_1"] = UNIT
for _n in range(FT1 // 2):
    WIDTHS[f"gu{_n}"] = UNIT
    if _n % 2 == 1 or _n == FT1 // 2 - 1:
        WIDTHS[f"dn1_{_n // 2}"] = (4 if _n % 2 == 1 else 2) * D
for _n in ["qnsa0", "qnsa1", "ksw", "vsw", "kvc", "dk0", "dk1", "cmp", "dv0", "dv1", "dq0", "dq1", "z0", "z1",
           "gn0", "gn1", "pn0", "pn1", "gd0", "gd1", "pd0", "pd1", "out2_0", "out2_1"]:
    WIDTHS[_n] = UNIT
for _n in range(8):
    WIDTHS[f"up{_n}"] = UNIT
    if _n >= 1:
        WIDTHS[f"dn2_{_n - 1}"] = UNIT
WIDTHS["dn2_7"] = UNIT
UNITS = list(WIDTHS)
STARTS = {}
_at = 0
for _n, _w in WIDTHS.items():
    STARTS[_n] = _at
    _at += P * _w
TOTAL = _at


def build(nc, consts, params, weights, x, meta, out, line_dram):
    ctx = ExitStack()
    with ctx:
        def sb(name, shape, dt=F32):
            return ctx.enter_context(nc.sbuf_tensor(name, shape, dt))

        sems = {}

        def sem(name):
            if name not in sems:
                sems[name] = ctx.enter_context(nc.semaphore(name))
            return sems[name]

        psum = ctx.enter_context(nc.psum_tensor("psum", [P, 8, 512], F32))
        ring = sb("ring", [P, SLOTS, UNIT])
        cbuf = sb("cbuf", [P, NCHELD])
        pbuf = sb("pbuf", [P, NHELD])
        X = sb("X", [P, TT, D])
        hT = sb("hT", [P, KD, ALL])
        ones = sb("ones", [P, P])
        st = sb("st", [P, 192])
        ARENA = 27520
        arena = sb("arena", [P, ARENA])

        def cst(name, rows=P):
            a, w = CONST[name]
            if a >= NEARLY:
                return att1["S"][0:rows, a - NEARLY:a - NEARLY + w]
            if a >= NCHELD:
                return att1["causal"][0:rows, :]
            return cbuf[0:rows, a:a + w]

        def par(name, rows=P):
            a, w = PARAM[name]
            return pbuf[0:rows, a:a + w]

        ident = cbuf[:, 0:P]

        def lay(start, names):
            at, got = start, {}
            for name, width in names:
                got[name] = arena[:, at:at + width]
                at += width
            assert at <= ARENA, at
            return got

        KM = 4 * ALL
        one = lay(0, [("Xm", D), ("Xn", TT * D), ("Xnm", D), ("cT", 3 * ALL), ("cnT", 3 * ALL), ("sqT", 3 * ALL),
                      ("rs", 3 * ALL), ("qT", MH * SEQ), ("kT", MH * ALL), ("dqT", 2 * SEQ), ("dkT", 2 * ALL),
                      ("sQT", 3 * SEQ), ("sKT", ALL), ("V", 3 * 768), ("dz", DH * ALL), ("sz0", SH * 144),
                      ("sz1", SH * ALL), ("rot", 4 * ALL)])
        end = sum(w for w in [D, TT * D, D, 12 * ALL, MH * SEQ, MH * ALL, 2 * SEQ, 2 * ALL, 3 * SEQ, ALL, 3 * 768,
                              DH * ALL, SH * 144, SH * ALL, 4 * ALL])
        att1 = lay(end, [("S", 2 * KM), ("E", 2 * KM), ("PTm", 2 * 512), ("final", D), ("causal", ALL)])
        att1 |= lay(0, [("PT", 2 * 4 * SEQ), ("y", TT * D)])
        ffn1 = lay(0, [("yT", KD * SEQ), ("Xn", TT * D), ("sg", 4 * SEQ), ("aT", FT1 * SEQ)])
        two = lay(0, [("Xn", TT * D), ("Q", TT * D)])
        nsa = lay(2048, [("Q", TT * D), ("qT", KD * SEQ), ("ksw", TT * 512), ("KT", 4 * SEQ), ("VV", TT * 512),
                         ("blk", 2 * 16 * 60), ("alibi", NSH * SEQ), ("O", TT * D), ("E", 2 * 4 * SEQ),
                         ("cv", 3 * NH2 * SEQ), ("Z", TT * D)])
        nsa |= lay(0, [("PT", 2 * 4 * SEQ), ("S", 2 * 4 * SEQ)])
        nsa["PTm"] = nsa["ksw"]
        dn = lay(0, [("Kt", 2048), ("KnT", 2048), ("Vb", 2048), ("DT", 2048), ("QKD", 2048), ("LT", 2048), ("Xi", 2048)])
        dn["Yi"] = nsa["E"]
        dn["M"] = nsa["cv"][:, 0:2048]
        dnp = nsa

        bank_full = [sem(f"bank{b}_full") for b in range(8)]
        bank_free = [sem(f"bank{b}_free") for b in range(8)]
        used = [0] * 8
        jobs = {}
        turn = [0, 8]

        def bank_of(name):
            return psum[:, jobs[name][0], :]

        def full(eng, name):
            b, n = jobs[name]
            eng.wait_ge(bank_full[b], n + 1)

        def freed(eng, name):
            b, n = jobs[name]
            eng.wait_ge(bank_free[b], n + 1)

        def release(ins, name):
            ins.then_inc(bank_free[jobs[name][0]], 1)

        counts = {}

        def signal(ins, name, by=1):
            ins.then_inc(sem(name), by)
            counts[name] = counts.get(name, 0) + by
            return counts[name]

        unit_jobs = {}

        def groups_one():
            got = []
            for qt in range(TT):
                keys = META + P * (qt + 1)
                for name, hs in [("mla", range(0, 4)), ("mla", range(4, 6)), ("dif", range(0, 2)), ("dif", range(2, 4)),
                                 ("swa", range(0, 4)), ("swa", range(4, 6))]:
                    got.append(dict(kind=name, qt=qt, hs=list(hs), keys=keys, meta=META, tiles=qt + 1,
                                    name=f"{name}{qt}_{hs[0]}"))
            return got

        def groups_two():
            got = []
            for qt in range(TT):
                for g in range(NSG):
                    hs = list(range(4 * g, 4 * g + 4))
                    got.append(dict(kind="cmp", qt=qt, hs=hs, keys=NC, meta=NC, tiles=0, name=f"cmp{qt}_{g}"))
                    for kind in ("slc", "win"):
                        got.append(dict(kind=kind, qt=qt, hs=hs, keys=P * (qt + 1), meta=0, tiles=qt + 1,
                                        name=f"{kind}{qt}_{g}"))
            return got

        G1, G2 = groups_one(), groups_two()
        FILLERS = [(w, p, first, n) for w, p in (("v", 1), ("q", 2)) for first in (0, 4) for n in range(2)]
        FILLERS += [("z", n, t) for n in range(2) for t in range(TT)]
        FILL = [2 * n for n in range(len(FILLERS))]
        n_maps = 0
        for i, g in enumerate(G1 + G2):
            if i == len(G1):
                n_maps = 0
            g["maps"] = [(h, c) for h in g["hs"] for c in range(2)] if g["kind"] == "dif" else [(h, 0) for h in g["hs"]]
            g["first"] = n_maps
            n_maps += len(g["maps"])
            g["last"] = n_maps
            g["per"] = 1 if g["kind"] == "dif" else min(len(g["maps"]), 512 // g["keys"])
        for G in (G1, G2):
            for i, g in enumerate(G):
                g["i"] = i
                g["difs"] = sum(q["kind"] == "dif" for q in G[:i + 1])
                g["swas"] = sum(q["kind"] == "swa" for q in G[:i + 1])

        def heads_v(g, h):
            if g["kind"] in ("mla", "dif", "swa"):
                V = one["V"].rearrange("p (t n) -> p t n", t=3)
                off = {"mla": 64 * h, "dif": 384 + 64 * h, "swa": 640 + 64 * (h // 3)}[g["kind"]]
                return [V[:, 1 + t, off:off + 64] for t in range(2)], V[0:META, 0, off:off + 64]
            if g["kind"] == "cmp":
                return [], vc[0:NC, 64 * (h // 4):64 * (h // 4) + 64]
            off = {"slc": 0, "win": 256}[g["kind"]] + 64 * (h // 4)
            V = nsa["VV"].rearrange("p (t n) -> p t n", t=TT)
            return [V[:, t, off:off + 64] for t in range(TT)], None

        def heads_qk(g, h, c):
            qs = slice(P * g["qt"], P * g["qt"] + P)
            ks = slice(0, g["keys"])
            if g["kind"] == "mla":
                return (one["qT"].rearrange("p (h n) -> p h n", h=MH)[0:96, h, qs],
                        one["kT"].rearrange("p (h n) -> p h n", h=MH)[0:96, h, ks])
            if g["kind"] == "dif":
                r = 32 * ((2 * h + c) % 4)
                return (one["dqT"].rearrange("p (h n) -> p h n", h=2)[r:r + 32, h // 2, qs],
                        one["dkT"].rearrange("p (h n) -> p h n", h=2)[r:r + 32, h // 2, ks])
            if g["kind"] == "swa":
                r = 64 * (h // 3)
                return (one["sQT"].rearrange("p (h n) -> p h n", h=3)[r:r + 64, h % 3, qs], one["sKT"][r:r + 64, ks])
            r = 64 * (h // 8)
            q = nsa["qT"].rearrange("p (h n) -> p h n", h=KD)[r:r + 64, h % 8, qs]
            if g["kind"] == "cmp":
                return q, kcT[r:r + 64, (h // 4) % 2, 0:NC]
            slot = {"slc": 0, "win": 2}[g["kind"]] + (h // 4) % 2
            return q, nsa["KT"].rearrange("p (h n) -> p h n", h=4)[r:r + 64, slot, ks]

        def map_bias(g, h):
            if g["kind"] == "mla":
                return cst("causal")[:, P * (1 - g["qt"]):ALL]
            if g["kind"] == "dif":
                return one["dz"].rearrange("p (h n) -> p h n", h=DH)[:, h, P * (1 - g["qt"]):ALL]
            if g["kind"] == "swa":
                return one["sz0" if g["qt"] == 0 else "sz1"].rearrange("p (h n) -> p h n", h=SH)[:, h, :]
            if g["kind"] == "cmp":
                return cst("cmpbias").rearrange("p (t h n) -> p t h n", t=TT, h=NSH)[:, g["qt"], h, :]
            return nsa["alibi"].rearrange("p (h n) -> p h n", h=NSH)[:, h, P * (1 - g["qt"]):2 * P]

        def slabs(g):
            own, width = (att1, ALL) if g["kind"] in ("mla", "dif", "swa") else (nsa, SEQ)
            par_ = g["i"] % 2
            S = own["S"].rearrange("p (b m n) -> p b m n", b=2, m=4)[:, par_]
            E = own["E"].rearrange("p (b m n) -> p b m n", b=2, m=4)[:, par_]
            PT = own["PT"].rearrange("p (b m n) -> p b m n", b=2, m=4)[:, par_]
            PTm = own["PTm"].rearrange("p (b n) -> p b n", b=2)[:, par_]
            return S, E, PT, PTm

        sig = sb("sig", [P, 112])
        soft = sb("soft", [P, 96])
        gl = sb("gl", [P, TT, NH2])
        gcb = sb("gcb", [P, 64])
        hid = sb("hid", [P, 2, 60])
        kcT = sb("kcT", [P, 2, 16])
        vc = sb("vc", [16, 256])
        be = sig[:, 0:16].rearrange("p (t h) -> p t h", t=TT)
        sums = sb("sums", [P, 96])
        peaks = sb("peaks", [P, 96])
        npeaks = sb("npeaks", [P, 96])
        scr = sb("scr", [P, 808])
        kcn = scr[0:16, 512:768]
        difsum = sb("difsum", [P, 40])

        def map_slot(g, buf, n):
            return buf[:, n, 0:g["keys"]]

        def probs_slot(g, n):
            return 2 * n if g["kind"] == "dif" else n

        def last_turn(g):
            per = 512 // (P * g["tiles"]) if g["tiles"] else 0
            return f"tt_{g['name']}_{(len(g['hs']) - 1) // per}" if per else f"tm_{g['name']}"

        block = ctx.enter_context(nc.Block())
        order = list(UNITS)
        index = {n: i for i, n in enumerate(order)}

        @block.tensor
        def _(pe):
            mm = nc.tensor.matmul

            def opened(name, bank=None):
                if bank is None:
                    bank = turn[0] % turn[1]
                    turn[0] += 1
                if used[bank]:
                    pe.wait_ge(bank_free[bank], used[bank])
                jobs[name] = (bank, used[bank])
                used[bank] += 1
                return psum[:, bank, :]

            def closed(ins, name):
                ins.then_inc(bank_full[jobs[name][0]], 1)

            def arrived(name):
                i = index[name]
                pe.wait_ge(sem(f"unit_in{i % SLOTS}"), 16 * (i // SLOTS + 1))
                return ring[:, i % SLOTS, 0:WIDTHS[name]]

            def transposes_of(src, name_of, gain_tiles=KD, meta=None):
                for k in range(gain_tiles):
                    name = name_of(k)
                    ps = opened(name)
                    at = 0
                    if meta is not None:
                        nc.tensor.transpose(ps[:, 0:META], meta[0:META, P * k:P * k + P], ident[0:META, 0:META])
                        at = META
                    for t in range(TT):
                        last = nc.tensor.transpose(ps[:, at + P * t:at + P * t + P], src[:, t, P * k:P * k + P], ident)
                    closed(last, name)

            def feature_product(unit, tile, cols, ps, first, rows=P, c0=0, m=P):
                w = unit.rearrange("p (m k n) -> p m k n", k=KD, n=P)
                for k in range(KD):
                    last = mm(ps, w[:, tile, k, c0:c0 + m], hT[:, k, cols], start=(k == 0), stop=(k == KD - 1))
                return last

            def token_product(unit, src, width, name, t, tk=KD, m=P, off=0):
                w = unit.rearrange("p (k n) -> p k n", k=tk)
                ps = opened(name)
                for k in range(tk):
                    last = mm(ps[0:m, 0:width], src(k, t), w[:, k, off:off + width], start=(k == 0), stop=(k == tk - 1))
                closed(last, name)

            def scores(g):
                for n, (h, c) in enumerate(g["maps"]):
                    name = f"qk_{g['name']}_{n // g['per']}"
                    if n % g["per"] == 0:
                        ps = opened(name)
                    q, k = heads_qk(g, h, c)
                    at = g["keys"] * (n % g["per"])
                    last = mm(ps[:, at:at + g["keys"]], q, k, start=True, stop=True)
                    if n % g["per"] == g["per"] - 1 or n == len(g["maps"]) - 1:
                        closed(last, name)

            def turned(g):
                S, E, PT, PTm = slabs(g)
                block_no = "1" if g["kind"] in ("mla", "dif", "swa") else "2"
                if g["kind"] == "dif":
                    pe.wait_ge(sem("differences"), g["difs"])
                else:
                    pe.wait_ge(sem("probs" + block_no), g["last"])
                nm = len(g["hs"])
                if g["meta"]:
                    name = f"tm_{g['name']}"
                    ps = opened(name)
                    for n in range(nm):
                        last = nc.tensor.transpose(ps[0:g["meta"], P * n:P * n + P], E[:, probs_slot(g, n), 0:g["meta"]], ident)
                    closed(last, name)
                per = 512 // (P * g["tiles"]) if g["tiles"] else 0
                for n in range(nm if per else 0):
                    name = f"tt_{g['name']}_{n // per}"
                    if n % per == 0:
                        ps = opened(name)
                    for t in range(g["tiles"]):
                        at = P * ((n % per) * g["tiles"] + t)
                        last = nc.tensor.transpose(ps[:, at:at + P], E[:, probs_slot(g, n), g["meta"] + P * t:g["meta"] + P * t + P],
                                                   ident)
                    if n % per == per - 1 or n == nm - 1:
                        closed(last, name)

            def weighted(g):
                S, E, PT, PTm = slabs(g)
                name = f"pv_{g['name']}"
                nm = len(g["hs"])
                if g["meta"]:
                    freed(pe, f"tm_{g['name']}")
                if g["tiles"]:
                    per = 512 // (P * g["tiles"])
                    for j in range((nm + per - 1) // per):
                        freed(pe, f"tt_{g['name']}_{j}")
                ps = opened(name)
                for n, h in enumerate(g["hs"]):
                    vt, vm = heads_v(g, h)
                    o = ps[:, 64 * n:64 * n + 64]
                    if g["meta"]:
                        last = mm(o, PTm[0:g["meta"], P * n:P * n + P], vm, start=True, stop=g["tiles"] == 0)
                    for t in range(g["tiles"]):
                        at = P * (n * g["tiles"] + t)
                        flat = PT.rearrange("p m n -> p (m n)")
                        last = mm(o, flat[:, at:at + P], vt[t], start=(t == 0 and not g["meta"]),
                                  stop=(t == g["tiles"] - 1))
                closed(last, name)

            def attention(G, between):
                scores(G[0])
                for i, g in enumerate(G):
                    if i + 1 < len(G):
                        scores(G[i + 1])
                    turned(g)
                    if i >= 1:
                        weighted(G[i - 1])
                    for step in between.get(i, ()):
                        step()
                weighted(G[-1])

            pe.wait_ge(sem("const_in"), 64)
            pe.wait_ge(sem("norm1"), 3)
            Xn = one["Xn"].rearrange("p (t n) -> p t n", t=TT)
            transposes_of(Xn, lambda k: f"h1_{k}", meta=one["Xnm"])
            for v in range(2):
                if v == 0:
                    pe.wait_ge(sem("relneg"), 1)
                ps = opened(f"line{v}")
                oh = cst("onehot").rearrange("p (v n) -> p v n", v=2)
                a = PARAM["rel"][0]
                closed(mm(ps[0:BH, 0:LINE], pbuf[0:33, a:a + BH], oh[0:33, v, :], start=True, stop=True), f"line{v}")
            for k in range(KD):
                freed(pe, f"h1_{k}")
            real = slice(META, ALL)
            every = slice(0, ALL)
            names = ["cq0", "cq1", "ckv", "dq0", "dq1", "dk0", "dk1", "sq0", "sq1", "sq2", "sk"]
            for n, what in enumerate(names):
                u = arrived(f"in1f{n // 4}")
                name = "p1_" + what
                ps = opened(name)
                cols = every if what in ("cq0", "cq1", "ckv", "dk0", "dk1", "sk") else real
                w = ALL if cols is every else SEQ
                closed(feature_product(u, n % 4, cols, ps[:, 0:w], True), name)
                unit_jobs[f"in1f{n // 4}"] = name
            ur = u
            psA, psB = opened("p1_krA"), opened("p1_krB")
            closed(feature_product(ur, 3, every, psA[64:96, 0:ALL], True, c0=0, m=32), "p1_krA")
            closed(feature_product(ur, 3, every, psB[64:96, 0:ALL], True, c0=32, m=32), "p1_krB")
            unit_jobs["in1f2"] = "p1_krB"
            u = arrived("in1t")
            token_product(u, lambda k, t: hT[:, k, 0:META], 384, "vt_m", 0, m=META)
            for t in range(TT):
                token_product(u, lambda k, t: hT[:, k, META + P * t:META + P * t + P], 384, f"vt_{t}", t)
            unit_jobs["in1t"] = "vt_1"
            pe.wait_ge(sem("ones"), 1)
            ps = opened("lat_q")
            pe.wait_ge(sem("lat_sq"), 3)
            sq = one["sqT"].rearrange("p (c n) -> p c n", c=3)
            mm(ps[:, 0:ALL], ones[:, :], sq[:, 0, :], start=True, stop=False)
            closed(mm(ps[:, 0:ALL], ones[:, :], sq[:, 1, :], start=False, stop=True), "lat_q")
            ps = opened("lat_kv")
            closed(mm(ps[:, 0:ALL], ones[:, :], sq[:, 2, :], start=True, stop=True), "lat_kv")
            u = arrived("mla")
            wq = u[:, 0:MH * 2 * P].rearrange("p (h k n) -> p h k n", h=MH, k=2)
            wk = u[:, MH * 2 * P:MH * 2 * P + MH * 64].rearrange("p (h n) -> p h n", h=MH)
            wv = u[:, MH * 2 * P + MH * 64:]
            cn = one["cnT"].rearrange("p (c n) -> p c n", c=3)
            pe.wait_ge(sem("lat_norm"), 3)
            for h in range(MH):
                ps = opened(f"mq_{h}")
                for k in range(2):
                    mm(ps[0:96, 0:SEQ], wq[:, h, k, 0:96], cn[:, k, real], start=(k == 0), stop=(k == 1))
                for k in range(2):
                    last = mm(ps[64:96, SEQ:2 * SEQ], wq[:, h, k, 96:128], cn[:, k, real], start=(k == 0), stop=(k == 1))
                closed(last, f"mq_{h}")
                ps = opened(f"mk_{h}")
                closed(mm(ps[0:64, 0:ALL], wk[:, h, :], cn[:, 2, :], start=True, stop=True), f"mk_{h}")
            for t in range(-1, TT):
                name = f"mv_{t}"
                ps = opened(name)
                m, cols = (META, slice(0, META)) if t < 0 else (P, slice(META + P * t, META + P * t + P))
                closed(mm(ps[0:m, 0:384], cn[:, 2, cols], wv, start=True, stop=True), name)
            unit_jobs["mla"] = "mv_1"
            freed(pe, f"mq_{MH - 1}")
            freed(pe, f"mk_{MH - 1}")
            freed(pe, "mv_1")
            freed(pe, "p1_sk")
            pe.wait_ge(sem("krot"), 1)
            attention(G1, {})
            y = att1["y"].rearrange("p (t n) -> p t n", t=TT)
            pe.wait_ge(sem("y1"), 2)
            freed(pe, "pv_" + G1[-1]["name"])
            transposes_of(y, lambda k: f"yT1_{k}")
            for k in range(KD):
                freed(pe, f"yT1_{k}")
            yT = ffn1["yT"].rearrange("p (k n) -> p k n", k=KD)
            for nh in range(2):
                u = arrived(f"out1_{nh}")
                for t in range(TT):
                    token_product(u, lambda k, t: yT[:, k, P * t:P * t + P], 512, f"o1_{nh}_{t}", t)
                unit_jobs[f"out1_{nh}"] = f"o1_{nh}_1"
            def norm_turn(tag, count, src):
                pe.wait_ge(sem(tag), count)
                transposes_of(src, lambda k: f"{tag}_{k}")
                for k in range(KD):
                    freed(pe, f"{tag}_{k}")

            norm_turn("norm2", 2, ffn1["Xn"].rearrange("p (t n) -> p t n", t=TT))
            tok = slice(0, SEQ)

            def down(units, tag, tiles, acts, ready):
                for uname, f0, nf in units:
                    u = arrived(uname)
                    w = u.rearrange("p (f n) -> p f n", n=D)
                    ready(f0, nf)
                    for f in range(f0, f0 + nf):
                        for t in range(TT):
                            for nh in range(2):
                                if f == 0:
                                    opened(f"{tag}_{t}_{nh}", 4 + 2 * t + nh)
                                ps = bank_of(f"{tag}_{t}_{nh}")
                                last = mm(ps, acts[:, f, P * t:P * t + P], w[:, f - f0, 512 * nh:512 * nh + 512],
                                          start=(f == 0), stop=(f == tiles - 1))
                                if f == tiles - 1:
                                    closed(last, f"{tag}_{t}_{nh}")
                    if f0 + nf == tiles:
                        unit_jobs[uname] = f"{tag}_1_1"
                    else:
                        unit_jobs[uname] = ("down_used", signal(last, "down_used"))

            aT = ffn1["aT"].rearrange("p (f n) -> p f n", f=FT1)
            turn[0], turn[1] = 0, 4

            def hidden1(f0, nf):
                for f in range(f0, f0 + nf):
                    freed(pe, f"gu_{f}")

            def hidden2(f0, nf):
                pe.wait_ge(sem("hidden2"), (f0 + nf) // 2)

            for n in range(FT1 // 2):
                u = arrived(f"gu{n}").rearrange("p (f s k n) -> p f s k n", f=2, s=2, k=KD)
                for j in range(2):
                    name = f"gu_{2 * n + j}"
                    ps = opened(name)
                    for s in range(2):
                        for k in range(KD):
                            last = mm(ps[:, SEQ * s:SEQ * s + SEQ], u[:, j, s, k, :], hT[:, k, tok],
                                      start=(k == 0), stop=(k == KD - 1))
                    closed(last, name)
                unit_jobs[f"gu{n}"] = name
                if n % 2 == 1 or n == FT1 // 2 - 1:
                    down([(f"dn1_{n // 2}", 4 * (n // 2), 4 if n % 2 == 1 else 2)], "d1", FT1, aT, hidden1)
            turn[0], turn[1] = 0, 8
            norm_turn("norm3", 2, two["Xn"].rearrange("p (t n) -> p t n", t=TT))

            def tokens_of(buf):
                return lambda k, t: buf[:, k, P * t:P * t + P]

            def two_tokens(uname, tag, src=tokens_of(hT), wait=None):
                u = arrived(uname)
                for t in range(TT):
                    token_product(u, src, 512, f"{tag}_{t}", t)
                unit_jobs[uname] = f"{tag}_1"

            sm = par("small")
            for t in range(TT):
                token_product(sm, tokens_of(hT), 64, f"small_{t}", t)
            for n in range(2):
                two_tokens(f"qnsa{n}", f"nq{n}")
            two_tokens("ksw", "nk")
            two_tokens("vsw", "nv")
            u = arrived("kvc")
            for n in range(2):
                name = f"kvc_{n}"
                ps = opened(name)
                for j in range(2):
                    last = feature_product(u, 2 * n + j, tok, ps[:, SEQ * j:SEQ * j + SEQ], True)
                closed(last, name)
            unit_jobs["kvc"] = "kvc_1"

            def conv_half(uname, which, first, n):
                if n == 0:
                    held[0] = arrived(uname)
                u = held[0]
                name = f"cv_{which}{first // 2 + n}"
                ps = opened(name)
                for j in range(2):
                    last = feature_product(u, 2 * n + j, tok, ps[:, SEQ * j:SEQ * j + SEQ], True)
                closed(last, name)
                unit_jobs[uname] = name

            held = [None]
            for uname, first in (("dk0", 0), ("dk1", 4)):
                for n in range(2):
                    conv_half(uname, "k", first, n)

            def z_tile(n, t):
                if t == 0:
                    held[0] = arrived(f"z{n}")
                token_product(held[0], tokens_of(hT), 512, f"z{n}_{t}", t)
                unit_jobs[f"z{n}"] = f"z{n}_{t}"

            Q = nsa["Q"].rearrange("p (t n) -> p t n", t=TT)
            pe.wait_ge(sem("nq_norm"), 2)
            for k in range(KD):
                name = f"nqT_{k}"
                ps = opened(name)
                for t in range(TT):
                    last = nc.tensor.transpose(ps[:, P * t:P * t + P], Q[:, t, P * k:P * k + P], ident)
                closed(last, name)
            ksw = nsa["ksw"].rearrange("p (t n) -> p t n", t=TT)
            pe.wait_ge(sem("nk_norm"), 2)
            for b in range(2):
                name = f"nkT_{b}"
                ps = opened(name)
                for s in range(2):
                    for t in range(TT):
                        src = ksw[:, t, 256 * b + P * s:256 * b + P * s + P]
                        at = SEQ * s + P * t
                        last = nc.tensor.transpose(ps[:, at:at + P], src, ident)
                closed(last, name)
            u = arrived("cmp").rearrange("p (s l n) -> p s l n", s=2, l=16)
            blk = nsa["blk"].rearrange("p (s l n) -> p s l n", s=2, l=16)
            freed(pe, "kvc_0")
            freed(pe, "kvc_1")
            ps = opened("hid")
            for s in range(2):
                for l in range(16):
                    last = mm(ps[:, 64 * s:64 * s + 60], u[:, s, l, :], blk[:, s, l, :], start=(l == 0), stop=(l == 15))
            closed(last, "hid")
            unit_jobs["cmp"] = "hid"
            freed(pe, "hid")
            ps = opened("kvc2")
            for s in range(2):
                for g in range(NSG):
                    slot = g if s else 2 * (g % 2) + g // 2
                    last = mm(ps[0:NC, 256 * s + 64 * slot:256 * s + 64 * slot + 64], hid[:, s, 15 * g:15 * g + 15],
                              par("w2k" if s == 0 else "w2v"), start=True, stop=True)
            closed(last, "kvc2")
            ps = opened("kcT")
            pe.wait_ge(sem("kc_norm"), 1)
            for s in range(2):
                last = nc.tensor.transpose(ps[:, 16 * s:16 * s + NC], kcn[0:NC, P * s:P * s + P], ident[0:NC, 0:NC])
            closed(last, "kcT")
            freed(pe, "kcT")
            for k in range(KD):
                freed(pe, f"nqT_{k}")
            freed(pe, "nkT_0")
            freed(pe, "nkT_1")
            freed(pe, "nv_0")
            freed(pe, "nv_1")
            pe.wait_ge(sem("alibi"), 16)
            extra = {}
            for i, what in zip(FILL, FILLERS):
                if what[0] == "z":
                    extra[i] = [lambda w=what: z_tile(w[1], w[2])]
                else:
                    extra[i] = [lambda w=what: conv_half(f"d{w[0]}{w[2] // 4}", w[0], w[2], w[3])]
            attention(G2, extra)
            cv = dnp["cv"].rearrange("p (w h n) -> p w h n", w=3, h=NH2)

            def cv_turn(w, tag):
                for t in range(TT):
                    for q in range(2):
                        name = f"{tag}_{t}_{q}"
                        ps = opened(name)
                        for n in range(GH):
                            last = nc.tensor.transpose(ps[:, P * n:P * n + P], cv[:, w, GH * q + n, P * t:P * t + P], ident)
                        closed(last, name)

            pe.wait_ge(sem("conv_done"), 24)
            cv_turn(0, "kt")
            cv_turn(1, "vt2")
            cv_turn(2, "qt2")
            pe.wait_ge(sem("gates"), 1)
            ps = opened("gc")
            for t in range(TT):
                mm(ps[:, 8 * t:8 * t + 8], cst("upper"), gl[:, t, :], start=True, stop=True)
            closed(mm(ps[:, 16:24], ones[:, :], gl[:, 0, :], start=True, stop=True), "gc")
            pairs = [(t, q) for t in range(TT) for q in range(2)]
            for t, q in pairs:
                name = f"gr_{t}_{q}"
                ps = opened(name)
                for n in range(GH):
                    last = mm(ps[:, P * n:P * n + P], gl[:, t, GH * q + n:GH * q + n + 1].to_broadcast([P, P]),
                              cst("upper"), start=True, stop=True)
                closed(last, name)
            Kt = dn["Kt"].rearrange("p (t h n) -> p t h n", t=TT, h=NH2)
            KnT = dn["KnT"].rearrange("p (h n) -> p h n", h=NH2)
            pe.wait_ge(sem("kn"), 4)
            for n in range(4):
                name = f"knT_{n}"
                ps = opened(name)
                for j in range(2):
                    for t in range(TT):
                        at = SEQ * j + P * t
                        last = nc.tensor.transpose(ps[:, at:at + P], Kt[:, t, 2 * n + j, :], ident)
                closed(last, name)
            for n in range(4):
                freed(pe, f"knT_{n}")
            for t, q in pairs:
                for what in ("qk", "kk", "br"):
                    name = f"{what}_{t}_{q}"
                    ps = opened(name)
                    for n in range(GH):
                        h = GH * q + n
                        c = slice(P * t, P * t + P)
                        if what == "br":
                            last = mm(ps[:, P * n:P * n + P], be[:, t, h:h + 1].to_broadcast([P, P]), ident,
                                      start=True, stop=True)
                        else:
                            rhs = cv[:, 2, h, c] if what == "qk" else KnT[:, h, c]
                            last = mm(ps[:, P * n:P * n + P], KnT[:, h, c], rhs, start=True, stop=True)
                    closed(last, name)
            Xi = dn["Xi"].rearrange("p (g n) -> p g n", g=4)
            Yi = dn["Yi"].rearrange("p (g n) -> p g n", g=4)
            M = dn["M"].rearrange("p (g n) -> p g n", g=4)
            LTk = dn["DT"].rearrange("p (g n) -> p g n", g=4)
            for g in range(4):
                name = f"x0_{g}"
                ps = opened(name)
                pe.wait_ge(sem("y_new"), g + 1)
                for n in range(GH):
                    last = nc.tensor.transpose(ps[:, P * n:P * n + P], Yi[:, g, P * n:P * n + P], ident)
                closed(last, name)
            for lv in range(1, LEVELS):
                for g in range(4):
                    name = f"m{lv}_{g}"
                    ps = opened(name)
                    if lv == 1:
                        freed(pe, f"x0_{g}")
                    else:
                        freed(pe, f"dx{lv - 1}_{g}")
                    pe.wait_ge(sem("lt_level"), 4 * (lv - 1) + g + 1)
                    for n in range(GH):
                        s = slice(P * n, P * n + P)
                        last = mm(ps[:, s], LTk[:, g, s], Xi[:, g, s], start=True, stop=True)
                    closed(last, name)
                for g in range(4):
                    freed(pe, f"m{lv}_{g}")
                    for what in (["dx", "dy"] if lv < LEVELS - 1 else ["dy"]):
                        name = f"{what}{lv}_{g}"
                        ps = opened(name)
                        if what == "dy" and lv > 1:
                            freed(pe, f"dy{lv - 1}_{g}")
                        if what == "dx" and lv > 1:
                            freed(pe, f"dy{lv - 1}_{g}")
                        for n in range(GH):
                            s = slice(P * n, P * n + P)
                            a, b = (Yi, M) if what == "dx" else (M, Yi)
                            last = mm(ps[:, s], a[:, g, s], b[:, g, s], start=True, stop=True)
                        closed(last, name)
            Y4 = dn["Yi"].rearrange("p (t h n) -> p t h n", t=TT, h=NH2)
            Vb = dn["Vb"].rearrange("p (t h n) -> p t h n", t=TT, h=NH2)
            QKD = dn["QKD"].rearrange("p (t h n) -> p t h n", t=TT, h=NH2)
            VN = cv[:, 0].rearrange("p h n -> p (h n)").rearrange("p (w h n) -> p w h n", w=2, h=NH2)
            S1 = cv[:, 1].rearrange("p h n -> p (h n)")[:, 0:1024].rearrange("p (h n) -> p h n", h=NH2)

            def heads_job(name, q, lhs, rhs):
                ps = opened(name)
                for n in range(GH):
                    h = GH * q + n
                    last = mm(ps[:, P * n:P * n + P], lhs(h), rhs(h), start=True, stop=True)
                closed(last, name)

            for t in range(TT):
                for q in range(2):
                    freed(pe, f"dy{LEVELS - 1}_{2 * t + q}")
                    if t == 1:
                        freed(pe, f"s1_{q}")
                        heads_job(f"ks_{q}", q, lambda h: KnT[:, h, P:SEQ], lambda h: S1[:, h, :])
                        pe.wait_ge(sem("vb1"), q + 1)
                    heads_job(f"vn_{t}_{q}", q, lambda h: Y4[:, t, h, :], lambda h: Vb[:, t, h, :])
                for q in range(2):
                    freed(pe, f"vn_{t}_{q}")
                    if t == 0:
                        pe.wait_ge(sem("vne"), q + 1)
                        heads_job(f"s1_{q}", q, lambda h: Kt[:, 0, h, :], lambda h: VN[:, 1, h, :])
                    heads_job(f"o_{t}_{q}", q, lambda h: QKD[:, t, h, :], lambda h: VN[:, 0, h, :])
                    if t == 1:
                        heads_job(f"os_{q}", q, lambda h: cv[:, 2, h, P:SEQ], lambda h: S1[:, h, :])
            for n in range(2):
                two_tokens(f"gn{n}", f"gn{n}")
            Onsa = nsa["O"].rearrange("p (t n) -> p t n", t=TT)
            transposes_of(Onsa, lambda k: f"onT_{k}")
            for k in range(KD):
                freed(pe, f"onT_{k}")
            onT = dn["Kt"].rearrange("p (k n) -> p k n", k=KD)
            for n in range(2):
                two_tokens(f"pn{n}", f"pn{n}", tokens_of(onT))
            for n in range(2):
                two_tokens(f"gd{n}", f"gd{n}")
            pe.wait_ge(sem("dn_out"), 2)
            Od = dn["Xi"].rearrange("p (t n) -> p t n", t=TT)
            transposes_of(Od, lambda k: f"odT_{k}")
            for k in range(KD):
                freed(pe, f"odT_{k}")
            odT = dn["KnT"].rearrange("p (k n) -> p k n", k=KD)
            for n in range(2):
                two_tokens(f"pd{n}", f"pd{n}", tokens_of(odT))
            mix = dn["Vb"].rearrange("p (t n) -> p t n", t=TT)
            pe.wait_ge(sem("mix"), 4)
            transposes_of(mix, lambda k: f"mixT_{k}")
            for k in range(KD):
                freed(pe, f"mixT_{k}")
            mixT = dn["Kt"].rearrange("p (k n) -> p k n", k=KD)
            for n in range(2):
                two_tokens(f"out2_{n}", f"o2_{n}", tokens_of(mixT))
            norm_turn("norm4", 2, dn["Vb"].rearrange("p (t n) -> p t n", t=TT))
            a2 = arena[:, 8192:8192 + FT2 * SEQ].rearrange("p (f n) -> p f n", f=FT2)
            turn[0], turn[1] = 0, 4
            for n in range(8):
                u = arrived(f"up{n}")
                for j in range(2):
                    name = f"up_{2 * n + j}"
                    ps = opened(name)
                    for s in range(2):
                        last = feature_product(u, 2 * j + s, tok, ps[:, SEQ * s:SEQ * s + SEQ], True)
                    closed(last, name)
                unit_jobs[f"up{n}"] = name
                if n >= 1:
                    down([(f"dn2_{n - 1}", 4 * (n - 1), 4)], "d2", FT2, a2, hidden2)
            down([("dn2_7", 28, 4)], "d2", FT2, a2, hidden2)

        @block.sync
        def _(sp):
            sp.dma_start(X[:, :, :], x.rearrange("(t p) n -> p t n", p=P)).then_inc(sem("x_in"), 16)
            sp.dma_start(one["Xm"][0:META, :], meta).then_inc(sem("x_in"), 16)
            sp.wait_ge(sem("x_in"), 32)
            for i, name in enumerate(order):
                if i >= SLOTS:
                    before = unit_jobs[order[i - SLOTS]]
                    if isinstance(before, tuple):
                        sp.wait_ge(sem(before[0]), before[1])
                    else:
                        full(sp, before)
                w = WIDTHS[name]
                src = weights[STARTS[name]:STARTS[name] + P * w].rearrange("(p n) -> p n", p=P)
                sp.dma_start(ring[:, i % SLOTS, 0:w], src).then_inc(sem(f"unit_in{i % SLOTS}"), 16)
            for t in range(TT):
                for nh in range(2):
                    freed(sp, f"d2_{t}_{nh}")
            sp.dma_start(out.rearrange("(t p) n -> p t n", p=P), X[:, :, :]).then_inc(sem("stored"), 16)
            sp.wait_ge(sem("stored"), 16)

        @block.scalar
        def _(act):
            A = nc.scalar.activation
            act.dma_start(cbuf[:, :], consts[:, 0:NCHELD]).then_inc(sem("const_in"), 16)
            act.dma_start(att1["causal"], consts[:, NCHELD:NEARLY]).then_inc(sem("const_in"), 16)
            act.dma_start(att1["S"][:, 0:NCONST - NEARLY], consts[:, NEARLY:NCONST]).then_inc(sem("const_in"), 16)
            act.dma_start(pbuf[:, :], params[:, 0:NHELD]).then_inc(sem("const_in"), 16)
            act.dma_start(att1["final"], params[:, NHELD:NPARAM]).then_inc(sem("final_in"), 16)

            def square_sums(src, col, junk, rows=P):
                return A(junk, src, ACT.Square, accum_out=st[0:rows, col:col + 1])

            def turned_out(name_of, dst, width, gain):
                for k in range(KD):
                    full(act, name_of(k))
                    g = gain(k)
                    if g is None:
                        ins = A(dst[:, k, 0:width], bank_of(name_of(k))[:, 0:width], ACT.Copy)
                    else:
                        ins = A(dst[:, k, 0:width], bank_of(name_of(k))[:, 0:width], ACT.Copy, scale=g)
                    release(ins, name_of(k))

            def norm_sums(tag, base, junk):
                for t in range(TT):
                    signal(square_sums(X[:, t, :], base + t, junk[:, t, :]), tag)

            def exponentials(g):
                S, E, PT, PTm = slabs(g)
                tag = "probs1" if g["kind"] in ("mla", "dif", "swa") else "probs2"
                G = G1 if tag == "probs1" else G2
                if g["i"] >= 2:
                    prev = G[g["i"] - 2]
                    full(act, last_turn(prev))
                for n in range(len(g["maps"])):
                    act.wait_ge(sem("peak" + tag[-1]), g["first"] + n + 1)
                    col = g["first"] + n
                    signal(A(map_slot(g, E, n), map_slot(g, S, n), ACT.Exp, bias=npeaks[:, col:col + 1],
                             accum_out=sums[:, col:col + 1]), tag)
                if g["kind"] == "swa":
                    c0, c1 = g["first"], g["last"]
                    act.wait_ge(sem("sink_in"), g["swas"])
                    signal(A(difsum[:, c0:c1], difsum[:, c0:c1], ACT.Exp), "sink_exp")

            def probs_out(g):
                S, E, PT, PTm = slabs(g)
                G = G1 if g["kind"] in ("mla", "dif", "swa") else G2
                nm = len(g["hs"])
                if g["i"] >= 2:
                    full(act, "pv_" + G[g["i"] - 2]["name"])
                if g["meta"]:
                    name = f"tm_{g['name']}"
                    full(act, name)
                    release(A(PTm[0:g["meta"], 0:P * nm], bank_of(name)[0:g["meta"], 0:P * nm], ACT.Copy), name)
                if g["tiles"]:
                    per = 512 // (P * g["tiles"])
                    flat = PT.rearrange("p m n -> p (m n)")
                    for j in range((nm + per - 1) // per):
                        w = P * g["tiles"] * min(per, nm - per * j)
                        name = f"tt_{g['name']}_{j}"
                        full(act, name)
                        release(A(flat[:, 512 * j:512 * j + w], bank_of(name)[:, 0:w], ACT.Copy), name)

            def attention(G, between):
                exponentials(G[0])
                for i, g in enumerate(G):
                    if i + 1 < len(G):
                        exponentials(G[i + 1])
                    probs_out(g)
                    for step in between.get(i, ()):
                        step()

            act.wait_ge(sem("x_in"), 32)
            jn = one["Xn"].rearrange("p (t n) -> p t n", t=TT)
            norm_sums("sq1", 0, jn)
            signal(square_sums(one["Xm"][0:META, :], 2, one["Xnm"][0:META, :], META), "sq1")
            act.wait_ge(sem("const_in"), 64)
            act.wait_ge(sem("lamsum"), 2)
            signal(A(st[:, 12:14], st[:, 10:12], ACT.Exp), "lamexp")
            turned_out(lambda k: f"h1_{k}", hT, ALL, lambda k: par("attn_norm")[:, k:k + 1])
            for v in range(2):
                full(act, f"line{v}")
                release(A(scr[0:BH, LINE * v:LINE * v + LINE], bank_of(f"line{v}")[0:BH, 0:LINE], ACT.Copy), f"line{v}")
            for v in range(2):
                freed(act, f"line{v}")
            act.dma_start(line_dram.rearrange("q h n -> h q n"),
                          scr[0:BH, 0:2 * LINE].unsqueeze(1).to_broadcast([BH, P, 2 * LINE])).then_inc(sem("lines_out"), 16)
            act.wait_ge(sem("lines_out"), 16)

            def shifted(head0, heads, v, m0, n):
                return bass.AP(tensor=line_dram.tensor, offset=head0 * 2 * LINE + v * LINE + m0 + P - 1,
                               ap=[[BH * 2 * LINE - 1, P], [2 * LINE, heads], [1, n]])

            sz0 = one["sz0"].rearrange("p (h n) -> p h n", h=SH)
            sz1 = one["sz1"].rearrange("p (h n) -> p h n", h=SH)
            act.dma_start(one["dz"].rearrange("p (h n) -> p h n", h=DH), shifted(0, DH, 0, 0, ALL)).then_inc(sem("bias_in"), 16)
            act.dma_start(sz0[:, :, 0:META], shifted(DH, SH, 0, P, META)).then_inc(sem("bias_in"), 16)
            act.dma_start(sz0[:, :, META:144], shifted(DH, SH, 1, P + META, P)).then_inc(sem("bias_in"), 16)
            act.dma_start(sz1[:, :, 0:META], shifted(DH, SH, 0, 0, META)).then_inc(sem("bias_in"), 16)
            act.dma_start(sz1[:, :, META:ALL], shifted(DH, SH, 1, META, SEQ)).then_inc(sem("bias_in"), 16)
            cT = one["cT"].rearrange("p (c n) -> p c n", c=3)
            sqT = one["sqT"].rearrange("p (c n) -> p c n", c=3)
            for c, what in enumerate(["cq0", "cq1", "ckv"]):
                name = "p1_" + what
                full(act, name)
                signal(A(sqT[:, c, :], bank_of(name)[:, 0:ALL], ACT.Square), "lat_sq")
                release(A(cT[:, c, :], bank_of(name)[:, 0:ALL], ACT.Copy), name)
            dq = one["dqT"].rearrange("p (c n) -> p c n", c=2)
            dk = one["dkT"].rearrange("p (c n) -> p c n", c=2)
            sQ = one["sQT"].rearrange("p (c n) -> p c n", c=3)
            for c in range(2):
                full(act, f"p1_dq{c}")
                release(A(dq[:, c, :], bank_of(f"p1_dq{c}")[:, 0:SEQ], ACT.Copy, scale=DQK ** -0.5), f"p1_dq{c}")
            for c in range(2):
                full(act, f"p1_dk{c}")
                release(A(dk[:, c, :], bank_of(f"p1_dk{c}")[:, 0:ALL], ACT.Copy), f"p1_dk{c}")
            for c in range(3):
                full(act, f"p1_sq{c}")
                release(A(sQ[:, c, :], bank_of(f"p1_sq{c}")[:, 0:SEQ], ACT.Copy, scale=SD ** -0.5), f"p1_sq{c}")
            full(act, "p1_sk")
            release(A(one["sKT"], bank_of("p1_sk")[:, 0:ALL], ACT.Copy), "p1_sk")
            V = one["V"].rearrange("p (t n) -> p t n", t=3)
            for t, rows in (("m", META), (0, P), (1, P)):
                full(act, f"vt_{t}")
                ti = 0 if t == "m" else t + 1
                release(A(V[0:rows, ti, 384:768], bank_of(f"vt_{t}")[0:rows, 0:384], ACT.Copy), f"vt_{t}")
            rs = one["rs"].rearrange("p (c n) -> p c n", c=3)
            act.wait_ge(sem("lat_ms"), 1)
            signal(A(rs[:, 1:3, :], rs[:, 1:3, :], ACT.Ln), "lat_ln")
            act.wait_ge(sem("lat_ln"), 1)
            signal(A(rs[:, 1:3, :], rs[:, 1:3, :], ACT.Exp, scale=-0.5), "lat_guess")
            kT = one["kT"].rearrange("p (h n) -> p h n", h=MH)
            qT = one["qT"].rearrange("p (h n) -> p h n", h=MH)
            for h in range(MH):
                full(act, f"mq_{h}")
                signal(A(qT[0:64, h, :], bank_of(f"mq_{h}")[0:64, 0:SEQ], ACT.Copy), "q_nope")
                full(act, f"mk_{h}")
                release(A(kT[0:64, h, :], bank_of(f"mk_{h}")[0:64, 0:ALL], ACT.Copy), f"mk_{h}")
            for t, rows in ((-1, META), (0, P), (1, P)):
                full(act, f"mv_{t}")
                release(A(V[0:rows, t + 1, 0:384], bank_of(f"mv_{t}")[0:rows, 0:384], ACT.Copy), f"mv_{t}")
            attention(G1, {})
            act.wait_ge(sem("y1"), 2)
            turned_out(lambda k: f"yT1_{k}", ffn1["yT"].rearrange("p (k n) -> p k n", k=KD), SEQ,
                       lambda k: st[:, 20:21] if k in (3, 4) else None)
            for nh in range(2):
                for t in range(TT):
                    freed(act, f"o1_{nh}_{t}")
            norm_sums("sq2", 0, ffn1["Xn"].rearrange("p (t n) -> p t n", t=TT))
            turned_out(lambda k: f"norm2_{k}", hT, SEQ, lambda k: par("ffn_norm")[:, k:k + 1])
            sg = ffn1["sg"].rearrange("p (s n) -> p s n", s=4)
            for f in range(FT1):
                full(act, f"gu_{f}")
                if f >= 4:
                    freed(act, f"gu_{f - 4}")
                signal(A(sg[:, f % 4, :], bank_of(f"gu_{f}")[:, 0:SEQ], ACT.Silu), "silu1")
            for t in range(TT):
                for nh in range(2):
                    freed(act, f"d1_{t}_{nh}")
            norm_sums("sq3", 0, two["Xn"].rearrange("p (t n) -> p t n", t=TT))
            act.wait_ge(sem("x2"), 2)
            norm_sums("sq3b", 0, two["Xn"].rearrange("p (t n) -> p t n", t=TT))
            turned_out(lambda k: f"norm3_{k}", hT, SEQ, lambda k: par("norm_mix")[:, k:k + 1])
            act.wait_ge(sem("small_in"), 1)
            signal(A(sig[:, :], sig[:, :], ACT.Exp, scale=-1.0), "small_exp")
            signal(A(soft[:, 16:32], soft[:, 16:32], ACT.Exp, scale=-1.0), "small_exp")
            signal(A(soft[:, 48:56], par("a_log"), ACT.Exp), "small_exp")
            act.wait_ge(sem("small_exp"), 3)
            signal(A(soft[:, 16:32], soft[:, 16:32], ACT.Ln, bias=1.0), "small_ln")
            Q = nsa["Q"].rearrange("p (t n) -> p t n", t=TT)
            ksw = nsa["ksw"].rearrange("p (t n) -> p t n", t=TT)
            VV = nsa["VV"].rearrange("p (t n) -> p t n", t=TT)
            for n in range(2):
                for t in range(TT):
                    name = f"nq{n}_{t}"
                    full(act, name)
                    release(A(Q[:, t, 512 * n:512 * n + 512], bank_of(name), ACT.Copy), name)
            for tag, dst in (("nk", ksw), ("nv", VV)):
                for t in range(TT):
                    full(act, f"{tag}_{t}")
                    release(A(dst[:, t, :], bank_of(f"{tag}_{t}"), ACT.Copy), f"{tag}_{t}")
            turned_out(lambda k: f"nqT_{k}", nsa["qT"].rearrange("p (k n) -> p k n", k=KD), SEQ, lambda k: par("nsa_q"))
            KT = nsa["KT"].rearrange("p (h n) -> p h n", h=4)
            for b in range(2):
                full(act, f"nkT_{b}")
                release(A(KT[:, 2 * b:2 * b + 2, :], bank_of(f"nkT_{b}"), ACT.Copy, scale=par("k_slc" if b == 0 else "k_win")),
                        f"nkT_{b}")
            full(act, "hid")
            hid_in = bank_of("hid")[:, 0:128].rearrange("p (s n) -> p s n", s=2)[:, :, 0:60]
            release(A(hid[:, :, :], hid_in, ACT.Gelu_apprx_tanh), "hid")
            full(act, "kcT")
            release(A(kcT[:, :, 0:NC],
                      bank_of("kcT")[:, 0:32].rearrange("p (s n) -> p s n", s=2)[:, :, 0:NC], ACT.Copy, scale=par("k_cmp")), "kcT")

            cv = dnp["cv"].rearrange("p (w h n) -> p w h n", w=3, h=NH2)

            def silu_conv(w, first, half):
                for n in range(2):
                    h = first + 2 * half + n
                    done = 8 * w + h + 1
                    act.wait_ge(sem("conv_raw"), done)
                    signal(A(cv[:, w, h, :], cv[:, w, h, :], ACT.Silu), "conv_done")

            def z_out(n, t):
                Z = dnp["Z"].rearrange("p (t n) -> p t n", t=TT)
                name = f"z{n}_{t}"
                full(act, name)
                release(A(Z[:, t, 512 * n:512 * n + 512], bank_of(name), ACT.Silu), name)

            for first in (0, 4):
                for half in range(2):
                    silu_conv(0, first, half)
            extra = {}
            for i, what in zip(FILL, FILLERS):
                if what[0] == "z":
                    extra[i] = [lambda w=what: z_out(w[1], w[2])]
                else:
                    extra[i + 1] = [lambda w=what: silu_conv(w[1], w[2], w[3])]
            attention(G2, extra)
            for t in range(TT):
                for q in range(2):
                    name = f"qt2_{t}_{q}"
                    full(act, name)
                    sqb = dn["M"].rearrange("p (g n) -> p g n", g=4)[:, 2 * t + q, :]
                    release(A(sqb, bank_of(name), ACT.Square), name)
            E4 = dn["DT"].rearrange("p (g n) -> p g n", g=4)
            full(act, "gc")
            act.wait_ge(sem("gc_out"), 1)
            signal(A(gcb[:, 32:40], gcb[:, 8:16], ACT.Exp), "gc_exp")
            signal(A(gcb[:, 40:48], gcb[:, 24:32], ACT.Exp), "gc_exp")
            for g in range(4):
                freed(act, f"gr_{g // 2}_{g % 2}")
                signal(A(E4[:, g, :], E4[:, g, :], ACT.Exp), "dec_exp")
            KnT = dn["KnT"].rearrange("p (h n) -> p h n", h=NH2)
            for n in range(4):
                full(act, f"knT_{n}")
                release(A(KnT[:, 2 * n:2 * n + 2, :], bank_of(f"knT_{n}"), ACT.Copy), f"knT_{n}")
            Xi = dn["Xi"].rearrange("p (g n) -> p g n", g=4)
            M = dn["M"].rearrange("p (g n) -> p g n", g=4)
            for g in range(4):
                full(act, f"x0_{g}")
                release(A(Xi[:, g, :], bank_of(f"x0_{g}"), ACT.Copy), f"x0_{g}")
            for lv in range(1, LEVELS):
                for g in range(4):
                    name = f"m{lv}_{g}"
                    full(act, name)
                    if lv > 1:
                        full(act, f"dy{lv - 1}_{g}")
                    release(A(M[:, g, :], bank_of(name), ACT.Copy), name)
            VN = cv[:, 0].rearrange("p h n -> p (h n)").rearrange("p (w h n) -> p w h n", w=2, h=NH2)
            S1 = cv[:, 1].rearrange("p h n -> p (h n)")[:, 0:1024].rearrange("p (h n) -> p h n", h=NH2)
            for q in range(2):
                full(act, f"vn_0_{q}")
                release(A(VN[:, 0, GH * q:GH * q + GH, :], bank_of(f"vn_0_{q}"), ACT.Copy), f"vn_0_{q}")
            for q in range(2):
                full(act, f"s1_{q}")
                ins = A(S1[:, GH * q:GH * q + GH, :], bank_of(f"s1_{q}"), ACT.Copy)
                release(ins, f"s1_{q}")
            for q in range(2):
                full(act, f"vn_1_{q}")
                full(act, f"o_0_{q}")
                release(A(VN[:, 0, GH * q:GH * q + GH, :], bank_of(f"vn_1_{q}"), ACT.Copy), f"vn_1_{q}")
            sgs = nsa["cv"][:, 4096:6144].rearrange("p (t n) -> p t n", t=TT)
            for n in range(2):
                for t in range(TT):
                    name = f"gn{n}_{t}"
                    full(act, name)
                    if n == 0 and t == 0:
                        full(act, "os_1")
                    release(A(sgs[:, t, 512 * n:512 * n + 512], bank_of(name), ACT.Sigmoid), name)
            turned_out(lambda k: f"onT_{k}", dn["Kt"].rearrange("p (k n) -> p k n", k=KD), SEQ, lambda k: None)
            sgd = dn["QKD"].rearrange("p (t n) -> p t n", t=TT)
            for n in range(2):
                for t in range(TT):
                    name = f"gd{n}_{t}"
                    full(act, name)
                    release(A(sgd[:, t, 512 * n:512 * n + 512], bank_of(name), ACT.Sigmoid), name)
            turned_out(lambda k: f"odT_{k}", dn["KnT"].rearrange("p (k n) -> p k n", k=KD), SEQ, lambda k: par("dn_out"))
            turned_out(lambda k: f"mixT_{k}", dn["Kt"].rearrange("p (k n) -> p k n", k=KD), SEQ, lambda k: None)
            for nh in range(2):
                for t in range(TT):
                    freed(act, f"o2_{nh}_{t}")
            norm_sums("sq4", 0, dn["Vb"].rearrange("p (t n) -> p t n", t=TT))
            turned_out(lambda k: f"norm4_{k}", hT, SEQ, lambda k: par("norm_mlp")[:, k:k + 1])
            a2 = arena[:, 8192:8192 + FT2 * SEQ].rearrange("p (f n) -> p f n", f=FT2)
            for j in range(FT2 // 2):
                name = f"up_{j}"
                full(act, name)
                release(A(a2[:, 2 * j:2 * j + 2, :], bank_of(name), ACT.Relu), name)

        @block.gpsimd
        def _(pool):
            nc.gpsimd.memset(ones[:, :], 1.0).then_inc(sem("ones"), 1)
            pool.wait_ge(sem("x2"), 2)
            al = nsa["alibi"].rearrange("p (h n) -> p h n", h=NSH)
            for h in range(NSH):
                slope = float(np.float32(2.0 ** (-8.0 * (h + 1) / NSH)))
                nc.gpsimd.tensor_scalar(al[:, h, :], cst("negdist"), slope, None, ALU.mult).then_inc(sem("alibi"), 1)
            E4 = dn["DT"].rearrange("p (g n) -> p g n", g=4)
            for g in range(4):
                pool.wait_ge(sem("dec_exp"), g + 1)
                v = E4[:, g, :].rearrange("p (n i) -> p n i", n=GH)
                nc.gpsimd.tensor_tensor(v, v, cst("upper").unsqueeze(1).to_broadcast([P, GH, P]), ALU.mult)\
                    .then_inc(sem("dec_masked"), 1)
            lev = cst("level").rearrange("p (l n) -> p l n", l=LEVELS)
            LT = dn["LT"].rearrange("p (g n) -> p g n", g=4)
            LTk = dn["DT"].rearrange("p (g n) -> p g n", g=4)
            for lv in range(1, LEVELS):
                for g in range(4):
                    if lv == 1:
                        pool.wait_ge(sem("y_new"), 4)
                    else:
                        full(pool, f"m{lv - 1}_{g}")
                    nc.gpsimd.tensor_tensor(
                        LTk[:, g, :].rearrange("p (n i) -> p n i", n=GH), LT[:, g, :].rearrange("p (n i) -> p n i", n=GH),
                        lev[:, lv, :].unsqueeze(1).to_broadcast([P, GH, P]), ALU.mult).then_inc(sem("lt_level"), 1)
            a2 = arena[:, 8192:8192 + FT2 * SEQ].rearrange("p (f n) -> p f n", f=FT2)
            for j in range(FT2 // 2):
                freed(pool, f"up_{j}")
                v = a2[:, 2 * j:2 * j + 2, :]
                nc.gpsimd.tensor_tensor(v, v, v, ALU.mult).then_inc(sem("hidden2"), 1)

        @block.vector
        def _(dve):
            V_ = nc.vector

            def link(ins):
                n = signal(ins, "vector_step")
                dve.wait_ge(sem("vector_step"), n)

            def step(ins):
                signal(ins, "vector_step")

            def settle():
                dve.wait_ge(sem("vector_step"), counts["vector_step"])

            def inv_sqrt(y, v, a, b):
                link(V_.tensor_scalar(y.bitcast(I32), v.bitcast(I32), -0.5, 1597463007.0, ALU.mult, ALU.add))
                link(V_.tensor_scalar(b, v, -0.5, None, ALU.mult))
                for _n in range(4):
                    newton(y, a, b)

            def newton(y, a, b):
                link(V_.tensor_tensor(a, y, y, ALU.mult))
                link(V_.tensor_tensor(a, a, b, ALU.mult))
                link(V_.scalar_tensor_tensor(out=y, in0=a, scalar=1.5, in1=y, op0=ALU.add, op1=ALU.mult))

            def inv_rms(dst, ssum, n, a, b, width):
                link(V_.tensor_scalar(ssum, ssum, 1.0 / n, EPS, ALU.mult, ALU.add))
                inv_sqrt(dst, ssum, a, b)

            def bc(ap, shape):
                return ap.unsqueeze(2).to_broadcast(shape)

            def norm_rows(tag, dst, sq_tag, count):
                dve.wait_ge(sem(sq_tag), count)
                inv_rms(st[:, 4:6], st[:, 0:2], D, st[:, 6:8], st[:, 8:10], 2)
                for t in range(TT):
                    signal(V_.tensor_scalar(dst[:, t, :], X[:, t, :], st[:, 4 + t:5 + t], None, ALU.mult), tag)

            def residual(names_):
                for t, nh, name in names_:
                    full(dve, name)
                    xs = X[:, t, 512 * nh:512 * nh + 512]
                    release(V_.tensor_tensor(xs, bank_of(name), xs, ALU.add), name)
                for t, nh, name in names_:
                    freed(dve, name)

            def peaks_of(g):
                S, E, PT, PTm = slabs(g)
                tag = "1" if g["kind"] in ("mla", "dif", "swa") else "2"
                G = G1 if tag == "1" else G2
                if g["i"] >= 2:
                    dve.wait_ge(sem("probs" + tag), G[g["i"] - 2]["last"])
                for n, (h, c) in enumerate(g["maps"]):
                    name = f"qk_{g['name']}_{n // g['per']}"
                    col = g["first"] + n
                    at = g["keys"] * (n % g["per"])
                    if n % g["per"] == 0:
                        full(dve, name)
                    ins = V_.tensor_tensor_reduce(out=map_slot(g, S, n), in0=bank_of(name)[:, at:at + g["keys"]],
                                                  in1=map_bias(g, h), scale=1.0, scalar=-3e38, op0=ALU.add, op1=ALU.max,
                                                  accum_out=peaks[:, col:col + 1])
                    if n % g["per"] == g["per"] - 1 or n == len(g["maps"]) - 1:
                        release(ins, name)
                    else:
                        step(ins)
                for n, (h, c) in enumerate(g["maps"]):
                    name = f"qk_{g['name']}_{n // g['per']}"
                    col = g["first"] + n
                    freed(dve, name)
                    if g["kind"] == "swa":
                        ins = V_.tensor_scalar(npeaks[:, col:col + 1], peaks[:, col:col + 1], par("sinks")[:, h:h + 1], -1.0,
                                               ALU.max, ALU.mult)
                    else:
                        ins = V_.tensor_scalar(npeaks[:, col:col + 1], peaks[:, col:col + 1], -1.0, None, ALU.mult)
                    signal(ins, "peak" + tag)
                if g["kind"] == "swa":
                    c0, c1, h0 = g["first"], g["last"], g["hs"][0]
                    dve.wait_ge(sem("peak1"), c1)
                    signal(V_.tensor_tensor(difsum[:, c0:c1], npeaks[:, c0:c1], par("sinks")[:, h0:h0 + c1 - c0], ALU.add),
                           "sink_in")

            def finish_one(g):
                y = att1["y"].rearrange("p (t n) -> p t n", t=TT)
                nm = len(g["hs"])
                c0 = g["first"]
                name = f"pv_{g['name']}"
                off = {"mla": 0, "dif": 384, "swa": 640}[g["kind"]] + 64 * g["hs"][0]
                yo = y[:, g["qt"], off:off + 64 * nm]
                if g["kind"] == "dif":
                    full(dve, name)
                    release(V_.tensor_copy(yo, bank_of(name)[:, 0:64 * nm]), name)
                    return
                dve.wait_ge(sem("probs1"), g["last"])
                link(V_.reciprocal(st[:, 24:24 + nm], sums[:, c0:c0 + nm]))
                full(dve, name)
                release(V_.tensor_tensor(yo.rearrange("p (h d) -> p h d", h=nm),
                                         bank_of(name)[:, 0:64 * nm].rearrange("p (h d) -> p h d", h=nm),
                                         bc(st[:, 24:24 + nm], [P, nm, 64]), ALU.mult), name)

            def sinks_in(g):
                c0, c1 = g["first"], g["last"]
                dve.wait_ge(sem("sink_exp"), g["swas"])
                link(V_.tensor_tensor(sums[:, c0:c1], sums[:, c0:c1], difsum[:, c0:c1], ALU.add))

            def difference(g):
                S, E, PT, PTm = slabs(g)
                c0 = g["first"]
                dve.wait_ge(sem("probs1"), g["last"])
                link(V_.reciprocal(difsum[:, c0:c0 + 4], sums[:, c0:c0 + 4]))
                v = difsum[:, c0:c0 + 4].rearrange("p (h c) -> p h c", c=2)[:, :, 1:2]
                link(V_.tensor_scalar(v, v, st[:, 16:17], None, ALU.mult))
                kk = g["keys"]
                for n in range(2):
                    a, b = map_slot(g, E, 2 * n), map_slot(g, E, 2 * n + 1)
                    link(V_.tensor_scalar(a, a, difsum[:, c0 + 2 * n:c0 + 2 * n + 1], None, ALU.mult))
                    ins = V_.scalar_tensor_tensor(out=a, in0=b, scalar=difsum[:, c0 + 2 * n + 1:c0 + 2 * n + 2], in1=a,
                                                  op0=ALU.mult, op1=ALU.add)
                    if n == 0:
                        step(ins)
                    else:
                        signal(ins, "differences")

            dve.wait_ge(sem("sq1"), 3)
            inv_rms(st[:, 4:6], st[:, 0:2], D, st[:, 6:8], st[:, 8:10], 2)
            inv_rms(st[0:META, 3:4], st[0:META, 2:3], D, st[0:META, 30:31], st[0:META, 31:32], 1)
            Xn = one["Xn"].rearrange("p (t n) -> p t n", t=TT)
            for t in range(TT):
                signal(V_.tensor_scalar(Xn[:, t, :], X[:, t, :], st[:, 4 + t:5 + t], None, ALU.mult), "norm1")
            signal(V_.tensor_scalar(one["Xnm"][0:META, :], one["Xm"][0:META, :], st[0:META, 3:4], None, ALU.mult), "norm1")
            dve.wait_ge(sem("const_in"), 64)
            a = PARAM["rel"][0]
            signal(V_.memset(pbuf[32:33, a:a + BH], NEG), "relneg")
            lam = par("lam").rearrange("p (r n) -> p r n", r=4)
            for n in range(2):
                ins = V_.tensor_tensor_reduce(out=scr[:, 32 * n:32 * n + DQK], in0=lam[:, 2 * n, :], in1=lam[:, 2 * n + 1, :],
                                              scale=1.0, scalar=0.0, op0=ALU.mult, op1=ALU.add,
                                              accum_out=st[:, 10 + n:11 + n])
                signal(ins, "lamsum")
            dve.wait_ge(sem("lamexp"), 1)
            link(V_.tensor_tensor(st[:, 15:16], st[:, 13:14], st[:, 12:13], ALU.subtract))
            link(V_.tensor_scalar(st[:, 16:17], st[:, 15:16], -LAM0, None, ALU.add))
            link(V_.tensor_scalar(st[:, 20:21], par("subln"), 1.0 - LAM0, None, ALU.mult))
            rot = one["rot"].rearrange("p (a n) -> p a n", a=4)
            kT = one["kT"].rearrange("p (h n) -> p h n", h=MH)
            qT = one["qT"].rearrange("p (h n) -> p h n", h=MH)
            cos, sin = cst("cos")[64:96, :], cst("sin")[64:96, :]
            full(dve, "p1_krA")
            release(V_.tensor_tensor(rot[64:96, 0, :], bank_of("p1_krA")[64:96, 0:ALL], cos, ALU.mult), "p1_krA")
            full(dve, "p1_krB")
            release(V_.tensor_tensor(rot[64:96, 1, :], bank_of("p1_krB")[64:96, 0:ALL], sin, ALU.mult), "p1_krB")
            freed(dve, "p1_krA")
            freed(dve, "p1_krB")
            link(V_.tensor_tensor(rot[64:96, 0, :], rot[64:96, 0, :], rot[64:96, 1, :], ALU.add))
            signal(V_.tensor_copy(kT[64:96, :, :], rot[64:96, 0, :].unsqueeze(1).to_broadcast([32, MH, ALL])), "krot")
            rs = one["rs"].rearrange("p (c n) -> p c n", c=3)
            cT = one["cT"].rearrange("p (c n) -> p c n", c=3)
            sqT = one["sqT"].rearrange("p (c n) -> p c n", c=3)
            cn = one["cnT"].rearrange("p (c n) -> p c n", c=3)
            for c, (name, n) in enumerate((("lat_q", MQR), ("lat_kv", MKR))):
                full(dve, name)
                release(V_.tensor_scalar(rs[:, 1 + c, :], bank_of(name)[:, 0:ALL], 1.0 / n, EPS, ALU.mult, ALU.add), name)
            freed(dve, "lat_q")
            freed(dve, "lat_kv")
            signal(V_.tensor_scalar(sqT[:, 0:2, :], rs[:, 1:3, :], -0.5, None, ALU.mult), "lat_ms")
            dve.wait_ge(sem("lat_guess"), 1)
            newton(rs[:, 1:3, :], cn[:, 0:2, :], sqT[:, 0:2, :])
            link(V_.tensor_scalar(rs[:, 1, :], rs[:, 1, :], (NOPE + ROPE) ** -0.5, None, ALU.mult))
            for c in range(3):
                g = par("q_norm")[:, c:c + 1] if c < 2 else par("kv_norm")
                signal(V_.scalar_tensor_tensor(out=cn[:, c, :], in0=cT[:, c, :], scalar=g, in1=rs[:, 1 + c // 2, :],
                                               op0=ALU.mult, op1=ALU.mult), "lat_norm")
            for h in range(MH):
                full(dve, f"mq_{h}")
                b_ = bank_of(f"mq_{h}")
                step(V_.tensor_tensor(rot[64:96, 2, 0:SEQ], b_[64:96, 0:SEQ], cos[:, META:ALL], ALU.mult))
                link(V_.tensor_tensor(rot[64:96, 3, 0:SEQ], b_[64:96, SEQ:2 * SEQ], sin[:, META:ALL], ALU.mult))
                dve.wait_ge(sem("q_nope"), h + 1)
                release(V_.tensor_tensor(qT[64:96, h, :], rot[64:96, 2, 0:SEQ], rot[64:96, 3, 0:SEQ], ALU.add), f"mq_{h}")
                freed(dve, f"mq_{h}")
            dve.wait_ge(sem("bias_in"), 80)
            peaks_of(G1[0])
            for i, g in enumerate(G1):
                if i + 1 < len(G1):
                    peaks_of(G1[i + 1])
                if g["kind"] == "dif":
                    difference(g)
                if i >= 1:
                    if G1[i - 1]["kind"] == "swa":
                        sinks_in(G1[i - 1])
                    finish_one(G1[i - 1])
            sinks_in(G1[-1])
            finish_one(G1[-1])
            freed(dve, "pv_" + G1[-1]["name"])
            y = att1["y"].rearrange("p (t n) -> p t n", t=TT)
            yd = [y[:, t, 384:640] for t in range(TT)]
            for t in range(TT):
                link(V_.tensor_tensor(scr[:, 256 * t:256 * t + 256], yd[t], yd[t], ALU.mult))
            link(V_.tensor_reduce(st[:, 32:40], scr[:, 0:512].rearrange("p (h d) -> p h d", d=DV), AXX, ALU.add))
            inv_rms(st[:, 40:48], st[:, 32:40], DV, st[:, 48:56], st[:, 56:64], 8)
            for t in range(TT):
                signal(V_.tensor_tensor(yd[t].rearrange("p (h d) -> p h d", d=DV), yd[t].rearrange("p (h d) -> p h d", d=DV),
                                        bc(st[:, 40 + 4 * t:44 + 4 * t], [P, DH, DV]), ALU.mult), "y1")
            residual([(t, nh, f"o1_{nh}_{t}") for nh in range(2) for t in range(TT)])
            norm_rows("norm2", ffn1["Xn"].rearrange("p (t n) -> p t n", t=TT), "sq2", 2)
            aT = ffn1["aT"].rearrange("p (f n) -> p f n", f=FT1)
            sg = ffn1["sg"].rearrange("p (s n) -> p s n", s=4)
            for f in range(FT1):
                dve.wait_ge(sem("silu1"), f + 1)
                full(dve, f"gu_{f}")
                ins = V_.tensor_tensor(aT[:, f, :], bank_of(f"gu_{f}")[:, SEQ:2 * SEQ], sg[:, f % 4, :], ALU.mult)
                release(ins, f"gu_{f}")
            residual([(t, nh, f"d1_{t}_{nh}") for t in range(TT) for nh in range(2)])
            dve.wait_ge(sem("sq3"), 2)
            dve.wait_ge(sem("final_in"), 16)
            inv_rms(st[:, 4:6], st[:, 0:2], D, st[:, 6:8], st[:, 8:10], 2)
            for t in range(TT):
                signal(V_.scalar_tensor_tensor(out=X[:, t, :], in0=X[:, t, :], scalar=st[:, 4 + t:5 + t], in1=att1["final"],
                                               op0=ALU.mult, op1=ALU.mult), "x2")
            norm_rows("norm3", two["Xn"].rearrange("p (t n) -> p t n", t=TT), "sq3b", 2)
            for t in range(TT):
                full(dve, f"small_{t}")
                ps = bank_of(f"small_{t}")
                step(V_.tensor_copy(sig[:, 16 + 48 * t:64 + 48 * t], ps[:, 16:64]))
                step(V_.tensor_copy(sig[:, 8 * t:8 * t + 8], ps[:, 0:8]))
                release(V_.tensor_tensor(soft[:, 8 * t:8 * t + 8], ps[:, 8:16], par("dt"), ALU.add), f"small_{t}")
            freed(dve, "small_0")
            freed(dve, "small_1")
            link(V_.tensor_scalar(soft[:, 32:48], soft[:, 0:16], -1.0, None, ALU.mult))
            signal(V_.tensor_tensor(soft[:, 16:32], soft[:, 0:16], soft[:, 32:48], ALU.max), "small_in")
            dve.wait_ge(sem("small_ln"), 1)
            link(V_.tensor_scalar(sig[:, :], sig[:, :], 1.0, None, ALU.add))
            link(V_.reciprocal(sig[:, :], sig[:, :]))
            link(V_.scalar_tensor_tensor(out=soft[:, 0:16], in0=soft[:, 0:16], scalar=0.0, in1=soft[:, 16:32],
                                         op0=ALU.max, op1=ALU.add))
            link(V_.tensor_scalar(soft[:, 48:56], soft[:, 48:56], -1.0, None, ALU.mult))
            signal(V_.tensor_tensor(gl[:, :, :], soft[:, 0:16].rearrange("p (t h) -> p t h", t=TT),
                                    soft[:, 48:56].unsqueeze(1).to_broadcast([P, TT, NH2]), ALU.mult), "gates")
            Q = nsa["Q"].rearrange("p (t n) -> p t n", t=TT)
            junk = nsa["O"]
            for n in range(2):
                for t in range(TT):
                    freed(dve, f"nq{n}_{t}")
            link(V_.tensor_tensor(junk, nsa["Q"], nsa["Q"], ALU.mult))
            link(V_.tensor_reduce(st[:, 64:96], junk.rearrange("p (h d) -> p h d", d=ND), AXX, ALU.add))
            inv_rms(st[:, 96:128], st[:, 64:96], ND, st[:, 128:160], st[:, 160:192], 32)
            link(V_.tensor_scalar(st[:, 96:128], st[:, 96:128], ND ** -0.5, None, ALU.mult))
            for t in range(TT):
                v = Q[:, t, :].rearrange("p (h d) -> p h d", d=ND)
                signal(V_.tensor_tensor(v, v, bc(st[:, 96 + 16 * t:112 + 16 * t], [P, NSH, ND]), ALU.mult), "nq_norm")
            for t in range(TT):
                freed(dve, f"nk_{t}")
            link(V_.tensor_tensor(junk[:, 0:1024], nsa["ksw"], nsa["ksw"], ALU.mult))
            link(V_.tensor_reduce(st[:, 64:80], junk[:, 0:1024].rearrange("p (h d) -> p h d", d=ND), AXX, ALU.add))
            inv_rms(st[:, 80:96], st[:, 64:80], ND, st[:, 128:144], st[:, 160:176], 16)
            for t in range(TT):
                v = nsa["ksw"][:, 512 * t:512 * t + 512].rearrange("p (h d) -> p h d", d=ND)
                signal(V_.tensor_tensor(v, v, bc(st[:, 80 + 8 * t:88 + 8 * t], [P, 8, ND]), ALU.mult), "nk_norm")
            cv = nsa["cv"].rearrange("p (w h n) -> p w h n", w=3, h=NH2)
            taps = par("conv").rearrange("p (h j) -> p h j", j=4)

            def convolve(which, w, first, n):
                name = f"cv_{which}{first // 2 + n}"
                full(dve, name)
                both = [(first + 2 * n + j, bank_of(name)[:, SEQ * j:SEQ * j + SEQ]) for j in range(2)]
                for h, raw in both:
                    step(V_.tensor_scalar(cv[:, w, h, :], raw, taps[:, 8 * w + h, 3:4], None, ALU.mult))
                settle()
                for back in (1, 2, 3):
                    for h, raw in both:
                        o = cv[:, w, h, back:SEQ]
                        ins = V_.scalar_tensor_tensor(out=o, in0=raw[:, 0:SEQ - back], scalar=taps[:, 8 * w + h, 3 - back:4 - back],
                                                      in1=o, op0=ALU.mult, op1=ALU.add)
                        if back < 3:
                            step(ins)
                        else:
                            signal(ins, "conv_raw")
                    if back < 3:
                        settle()
                release(V_.tensor_copy(scr[:, 800 + n:801 + n], bank_of(name)[:, 0:1]), name)

            for first in (0, 4):
                for n in range(2):
                    convolve("k", 0, first, n)
            blk = nsa["blk"].rearrange("p (s l g n) -> p s l g n", s=2, l=16, g=NSG)
            for s_ in range(2):
                name = f"kvc_{s_}"
                full(dve, name)
                for g in range(NSG):
                    r = 64 * (g % 2)
                    src = bank_of(name)[r:r + 64, SEQ * (g // 2):SEQ * (g // 2) + SEQ]
                    for odd in range(2):
                        o = 64 * odd
                        view = bass.AP(tensor=src.tensor, offset=src.offset + odd,
                                       ap=[src.ap[0], [2, 16], [CS, NC]])
                        pos = par("pos_k" if s_ == 0 else "pos_v")[o:o + 64, :]
                        ins = V_.tensor_tensor(blk[o:o + 64, s_, :, g, :], view, bc(pos, [64, 16, NC]), ALU.add)
                        if g == NSG - 1 and odd == 1:
                            release(ins, name)
                        else:
                            step(ins)
            full(dve, "kvc2")
            kv2 = bank_of("kvc2")
            link(V_.tensor_copy(kcn[0:NC, :], kv2[0:NC, 0:256]))
            release(V_.tensor_copy(vc[0:NC, :], kv2[0:NC, 256:512]), "kvc2")
            link(V_.tensor_tensor(scr[0:NC, 0:256], kcn[0:NC, :], kcn[0:NC, :], ALU.mult))
            link(V_.tensor_reduce(st[0:NC, 64:68], scr[0:NC, 0:256].rearrange("p (h d) -> p h d", d=ND), AXX, ALU.add))
            inv_rms(st[0:NC, 68:72], st[0:NC, 64:68], ND, st[0:NC, 72:76], st[0:NC, 76:80], 4)
            k4 = kcn[0:NC, :].rearrange("p (h d) -> p h d", d=ND)
            signal(V_.tensor_tensor(k4, k4, bc(st[0:NC, 68:72], [NC, NSG, ND]), ALU.mult), "kc_norm")

            def finish_two(g):
                c0 = g["first"]
                name = f"pv_{g['name']}"
                b_ = {"cmp": 0, "slc": 1, "win": 2}[g["kind"]]
                t = g["qt"]
                dve.wait_ge(sem("probs2"), g["last"])
                link(V_.reciprocal(st[:, 24:28], sums[:, c0:c0 + 4]))
                gates = sig[:, 16 + 48 * t:64 + 48 * t].rearrange("p (h b) -> p h b", b=3)[:, g["hs"][0]:g["hs"][0] + 4, b_]
                link(V_.tensor_tensor(st[:, 24:28], st[:, 24:28], gates, ALU.mult))
                if b_ == 0:
                    link(V_.tensor_scalar(st[:, 24:28], st[:, 24:28], cst("valid")[:, t:t + 1], None, ALU.mult))
                full(dve, name)
                o = nsa["O"].rearrange("p (t h d) -> p t h d", t=TT, h=NSH)[:, t, g["hs"][0]:g["hs"][0] + 4, :]
                ps = bank_of(name)[:, 0:256].rearrange("p (h d) -> p h d", h=4)
                f4 = bc(st[:, 24:28], [P, 4, ND])
                if b_ == 0:
                    release(V_.tensor_tensor(o, ps, f4, ALU.mult), name)
                    freed(dve, name)
                else:
                    tmp = scr[:, 0:256].rearrange("p (h d) -> p h d", h=4)
                    release(V_.tensor_tensor(tmp, ps, f4, ALU.mult), name)
                    freed(dve, name)
                    link(V_.tensor_tensor(o, o, tmp, ALU.add))

            extra = {i: what for i, what in zip(FILL, FILLERS) if what[0] != "z"}
            peaks_of(G2[0])
            for i, g in enumerate(G2):
                if i + 1 < len(G2):
                    peaks_of(G2[i + 1])
                if i >= 1:
                    finish_two(G2[i - 1])
                if i in extra:
                    convolve(*extra[i])
            finish_two(G2[-1])
            Kt = dn["Kt"].rearrange("p (t h n) -> p t h n", t=TT, h=NH2)
            Vb = dn["Vb"].rearrange("p (t h n) -> p t h n", t=TT, h=NH2)
            pairs = [(t, q) for t in range(TT) for q in range(2)]

            def four(ap, q):
                return ap[:, GH * q:GH * q + GH]

            def heads_of(bank):
                return bank.rearrange("p (h n) -> p h n", h=GH)

            for t, q in pairs:
                full(dve, f"kt_{t}_{q}")
                release(V_.tensor_copy(four(Kt[:, t], q), heads_of(bank_of(f"kt_{t}_{q}"))), f"kt_{t}_{q}")
            for t, q in pairs:
                freed(dve, f"kt_{t}_{q}")
            link(V_.tensor_tensor(dn["LT"], dn["Kt"], dn["Kt"], ALU.mult))
            link(V_.tensor_reduce(st[:, 64:80], dn["LT"].rearrange("p (h d) -> p h d", d=P), AXX, ALU.add))
            inv_rms(st[:, 80:96], st[:, 64:80], 1, st[:, 128:144], st[:, 160:176], 16)
            for t, q in pairs:
                v = four(Kt[:, t], q)
                signal(V_.tensor_tensor(v, v, bc(st[:, 80 + 8 * t + GH * q:84 + 8 * t + GH * q], [P, GH, P]), ALU.mult), "kn")
            for t, q in pairs:
                name = f"vt2_{t}_{q}"
                full(dve, name)
                release(V_.tensor_tensor(four(Vb[:, t], q), heads_of(bank_of(name)), bc(four(be[:, t], q), [P, GH, P]),
                                         ALU.mult), name)
            for t, q in pairs:
                freed(dve, f"qt2_{t}_{q}")
            link(V_.tensor_reduce(st[:, 64:80], dn["M"].rearrange("p (h d) -> p h d", d=P), AXX, ALU.add))
            rq = st[:, 96:112]
            inv_rms(rq, st[:, 64:80], 1, st[:, 128:144], st[:, 160:176], 16)
            link(V_.tensor_scalar(rq, rq, P ** -0.5, None, ALU.mult))
            full(dve, "gc")
            release(V_.tensor_copy(gcb[:, 0:24], bank_of("gc")[:, 0:24]), "gc")
            freed(dve, "gc")
            signal(V_.tensor_tensor(gcb[:, 24:32], gcb[:, 16:24], gcb[:, 0:8], ALU.subtract), "gc_out")
            E4 = dn["DT"].rearrange("p (g n) -> p g n", g=4)
            for t, q in pairs:
                name = f"gr_{t}_{q}"
                full(dve, name)
                for n in range(GH):
                    s_ = slice(P * n, P * n + P)
                    h = 8 * t + GH * q + n
                    ins = V_.tensor_scalar(E4[:, 2 * t + q, s_], bank_of(name)[:, s_], gcb[:, h:h + 1], 0.0, ALU.subtract, ALU.min)
                    if n == GH - 1:
                        release(ins, name)
                    else:
                        step(ins)
            QKD = dn["QKD"].rearrange("p (g n) -> p g n", g=4)
            LT = dn["LT"].rearrange("p (g n) -> p g n", g=4)
            Yi = dn["Yi"].rearrange("p (g n) -> p g n", g=4)
            Xi = dn["Xi"].rearrange("p (g n) -> p g n", g=4)
            lev0 = cst("level")[:, 0:P].unsqueeze(1).to_broadcast([P, GH, P])
            idb = ident.unsqueeze(1).to_broadcast([P, GH, P])
            for t, q in pairs:
                g = 2 * t + q
                dve.wait_ge(sem("dec_masked"), g + 1)
                full(dve, f"qk_{t}_{q}")
                release(V_.tensor_tensor(QKD[:, g, :], bank_of(f"qk_{t}_{q}"), E4[:, g, :], ALU.mult), f"qk_{t}_{q}")
                full(dve, f"br_{t}_{q}")
                release(V_.tensor_tensor(Yi[:, g, :], bank_of(f"br_{t}_{q}"), E4[:, g, :], ALU.mult), f"br_{t}_{q}")
                freed(dve, f"br_{t}_{q}")
                release(V_.tensor_tensor(LT[:, g, :], bank_of(f"kk_{t}_{q}"), Yi[:, g, :], ALU.mult), f"kk_{t}_{q}")
                freed(dve, f"kk_{t}_{q}")
                link(V_.tensor_tensor(heads_of(Yi[:, g, :]), heads_of(LT[:, g, :]), lev0, ALU.mult))
                signal(V_.tensor_tensor(heads_of(Yi[:, g, :]), idb, heads_of(Yi[:, g, :]), ALU.subtract), "y_new")
            for lv in range(1, LEVELS):
                for g in range(4):
                    for what in (["dx", "dy"] if lv < LEVELS - 1 else ["dy"]):
                        name = f"{what}{lv}_{g}"
                        full(dve, name)
                        tgt = (Xi if what == "dx" else Yi)[:, g, :]
                        release(V_.tensor_tensor(tgt, tgt, bank_of(name), ALU.subtract), name)
            VN = cv[:, 0].rearrange("p h n -> p (h n)").rearrange("p (w h n) -> p w h n", w=2, h=NH2)
            L4 = dn["LT"].rearrange("p (w h n) -> p w h n", w=2, h=NH2)
            O4 = dn["Xi"].rearrange("p (t h n) -> p t h n", t=TT, h=NH2)
            dve.wait_ge(sem("gc_exp"), 2)
            link(V_.tensor_tensor(gcb[:, 48:56], gcb[:, 32:40], be[:, 1, :], ALU.mult))
            for q in range(2):
                freed(dve, f"vn_0_{q}")
                signal(V_.tensor_tensor(four(VN[:, 1], q), four(VN[:, 0], q), bc(gcb[:, 40 + GH * q:44 + GH * q], [P, GH, P]),
                                        ALU.mult), "vne")
            for q in range(2):
                full(dve, f"o_0_{q}")
                release(V_.tensor_copy(four(O4[:, 0], q), heads_of(bank_of(f"o_0_{q}"))), f"o_0_{q}")
            for q in range(2):
                name = f"ks_{q}"
                full(dve, name)
                release(V_.tensor_tensor(four(L4[:, 0], q), heads_of(bank_of(name)), bc(gcb[:, 48 + GH * q:52 + GH * q], [P, GH, P]),
                                         ALU.mult), name)
                freed(dve, name)
                v = four(Vb[:, 1], q)
                signal(V_.tensor_tensor(v, v, four(L4[:, 0], q), ALU.subtract), "vb1")
            for q in range(2):
                name = f"os_{q}"
                full(dve, name)
                release(V_.tensor_tensor(four(L4[:, 1], q), heads_of(bank_of(name)), bc(gcb[:, 32 + GH * q:36 + GH * q], [P, GH, P]),
                                         ALU.mult), name)
                freed(dve, name)
                name = f"o_1_{q}"
                release(V_.tensor_tensor(four(O4[:, 1], q), heads_of(bank_of(name)), four(L4[:, 1], q), ALU.add), name)
            for q in range(2):
                freed(dve, f"o_0_{q}")
                freed(dve, f"o_1_{q}")
            link(V_.tensor_tensor(dn["LT"], dn["Xi"], dn["Xi"], ALU.mult))
            link(V_.tensor_reduce(st[:, 64:80], dn["LT"].rearrange("p (h d) -> p h d", d=P), AXX, ALU.add))
            link(V_.tensor_tensor(st[:, 64:80], st[:, 64:80], rq, ALU.mult))
            link(V_.tensor_tensor(st[:, 64:80], st[:, 64:80], rq, ALU.mult))
            inv_rms(st[:, 80:96], st[:, 64:80], P, st[:, 128:144], st[:, 160:176], 16)
            link(V_.tensor_tensor(st[:, 80:96], st[:, 80:96], rq, ALU.mult))
            for t in range(TT):
                for n in range(2):
                    freed(dve, f"z{n}_{t}")
                link(V_.tensor_tensor(O4[:, t], O4[:, t], bc(st[:, 80 + 8 * t:88 + 8 * t], [P, NH2, P]), ALU.mult))
                signal(V_.tensor_tensor(O4[:, t], O4[:, t], nsa["Z"].rearrange("p (t h n) -> p t h n", t=TT, h=NH2)[:, t],
                                        ALU.mult), "dn_out")
            sgs = nsa["cv"][:, 4096:6144].rearrange("p (t n) -> p t n", t=TT)
            sgd = dn["QKD"].rearrange("p (t n) -> p t n", t=TT)
            mix = dn["Vb"].rearrange("p (t n) -> p t n", t=TT)
            tmp = dn["LT"].rearrange("p (t n) -> p t n", t=TT)
            for n in range(2):
                for t in range(TT):
                    s_ = slice(512 * n, 512 * n + 512)
                    name = f"pn{n}_{t}"
                    freed(dve, f"gn{n}_{t}")
                    full(dve, name)
                    release(V_.tensor_tensor(mix[:, t, s_], bank_of(name), sgs[:, t, s_], ALU.mult), name)
            for n in range(2):
                for t in range(TT):
                    s_ = slice(512 * n, 512 * n + 512)
                    name = f"pd{n}_{t}"
                    freed(dve, f"gd{n}_{t}")
                    full(dve, name)
                    release(V_.tensor_tensor(tmp[:, t, s_], bank_of(name), sgd[:, t, s_], ALU.mult), name)
                    freed(dve, name)
                    signal(V_.tensor_tensor(mix[:, t, s_], mix[:, t, s_], tmp[:, t, s_], ALU.add), "mix")
            residual([(t, nh, f"o2_{nh}_{t}") for nh in range(2) for t in range(TT)])
            norm_rows("norm4", dn["Vb"].rearrange("p (t n) -> p t n", t=TT), "sq4", 2)
            residual([(t, nh, f"d2_{t}_{nh}") for t in range(TT) for nh in range(2)])


def shape_constants():
    c = np.zeros((P, NCONST), np.float32)

    def put(name, value, rows=slice(0, P)):
        a, w = CONST[name]
        c[rows, a:a + w] = np.asarray(value, np.float32).reshape(-1, w)

    j, i = np.arange(P)[:, None], np.arange(P)[None, :]
    put("ident", j == i)
    put("upper", j <= i)
    put("level", np.stack([((j >> l) % 2 == 0) & ((i >> l) == (j >> l) + 1) for l in range(LEVELS)], 1).reshape(P, -1))
    dist = P + j - (np.arange(ALL)[None, :] - META)
    put("causal", np.where(dist >= 0, 0.0, NEG))
    dist = P + j - np.arange(2 * P)[None, :]
    put("negdist", np.where(dist >= 0, -dist.astype(np.float64), NEG))
    inv = np.float32(10000.0) ** (-np.arange(0, ROPE, 2, dtype=np.float32) / np.float32(ROPE))
    ang = (np.arange(ALL, dtype=np.float32)[:, None] * inv[None, :].astype(np.float32)).astype(np.float32)
    cos, sin = np.cos(ang).T, np.sin(ang).T
    put("cos", np.concatenate([cos, cos]), slice(64, 96))
    put("sin", np.concatenate([-sin, sin]), slice(64, 96))
    slopes = (2.0 ** (-8.0 * np.arange(1, NSH + 1) / NSH)).astype(np.float32)
    pos = (np.arange(TT)[None, :, None, None] * P + np.arange(P)[:, None, None, None])
    end = (np.arange(NC) * CS + CL - 1)[None, None, None, :]
    put("cmpbias", np.where(pos - end >= 0, -slopes[None, None, :, None] * (pos - end).astype(np.float32), NEG))
    put("valid", (np.arange(TT)[None, :] * P + np.arange(P)[:, None]) >= CL - 1)
    n = (ALL - 1) - np.arange(LINE)
    half = BUCKETS // 2
    nf = np.maximum(n, half).astype(np.float32)
    large = half + (np.log(nf / np.float32(half)) / np.float32(math.log(128 / half)) * np.float32(BUCKETS - half)).astype(np.int32)
    bucket = np.where(n < half, n, np.minimum(large, BUCKETS - 1))
    hot = np.zeros((BUCKETS + 1, 2, LINE), np.float32)
    for v in range(2):
        row = np.where((n < 0) | ((n >= WIN) if v else False), BUCKETS, bucket)
        hot[row, v, np.arange(LINE)] = 1.0
    put("onehot", hot, slice(0, BUCKETS + 1))
    return c


def laid_params(a):
    p = np.zeros((P, NPARAM), np.float32)

    def put(name, value, rows=slice(0, P)):
        at, w = PARAM[name]
        p[rows, at:at + w] = value

    def columns(v):
        return v.reshape(-1, P).T

    def everywhere(v):
        return np.broadcast_to(v.reshape(1, -1), (P, v.size))

    put("attn_norm", columns(a["attn_norm"]))
    put("ffn_norm", columns(a["ffn_norm"]))
    put("norm_mix", columns(a["norm_mix_2"]))
    put("norm_mlp", columns(a["norm_mlp_2"]))
    put("q_norm", columns(a["mla_q_norm"]))
    put("kv_norm", columns(a["mla_kv_norm"]))
    for name, src in [("subln", "diff_subln"), ("nsa_q", "nsa_q_norm_2"), ("k_cmp", "nsa_k_norm_cmp_2"),
                      ("k_slc", "nsa_k_norm_slc_2"), ("k_win", "nsa_k_norm_win_2")]:
        put(name, columns(np.concatenate([a[src].reshape(-1)] * 2)))
    put("dn_out", columns(a["dn_out_norm_2"]))
    conv = a["dn_conv_2"].reshape(4, 3, NH2, P)[:, [1, 2, 0]]
    put("conv", conv.transpose(3, 1, 2, 0).reshape(P, -1))
    put("w2k", a["cmp_w2_k_2"][0])
    put("w2v", a["cmp_w2_v_2"][0])
    for name, src in [("pos_k", "cmp_pos_k_2"), ("pos_v", "cmp_pos_v_2")]:
        put(name, a[src].reshape(CL // 2, P).T)
    put("rel", a["rel_bias"], slice(0, BUCKETS))
    put("lam", everywhere(a["diff_lambda"]))
    put("sinks", everywhere(a["swa_sinks"]))
    put("a_log", everywhere(a["dn_a_log_2"]))
    put("dt", everywhere(a["dn_dt_bias_2"]))
    put("final", everywhere(a["final_norm"]))
    w = a["w_in_2"][0]
    small = np.concatenate([w[:, 4096:4112], w[:, 6672:6720]], 1)
    put("small", small.reshape(KD, P, 64).transpose(1, 0, 2).reshape(P, -1))
    return p


def laid_weights(a):
    flat = np.empty(TOTAL, np.float32)

    def put(name, value):
        value = value.reshape(P, -1)
        assert value.shape[1] == WIDTHS[name], (name, value.shape)
        flat[STARTS[name]:STARTS[name] + value.size] = value.reshape(-1)

    def features(w):
        k, m = w.shape
        return w.reshape(k // P, P, m // P, P).transpose(1, 2, 0, 3)

    def tokens(w):
        return w.reshape(-1, P, w.shape[1]).transpose(1, 0, 2)

    w = a["w_in"][0]
    cq, ckv, kr, dq, dk, dv, sq, sk, sv = np.split(w, np.cumsum([256, 128, 32, 256, 256, 256, 384, 128]), axis=1)
    sq = sq.reshape(D, 2, 3, 64).transpose(0, 2, 1, 3).reshape(D, 384)
    swapped = np.concatenate([kr[:, 16:], kr[:, :16]], 1)
    feat = np.concatenate([cq, ckv, dq, dk, sq, sk, kr, swapped, np.zeros((D, 64), np.float32)], 1)
    for n in range(3):
        put(f"in1f{n}", features(feat[:, 512 * n:512 * n + 512]))
    put("in1t", tokens(np.concatenate([dv, sv], 1)))
    wq = a["mla_w_qb"][0].reshape(2, P, MH, 96).transpose(1, 2, 0, 3)
    wq = np.concatenate([wq, wq[..., 80:96], wq[..., 64:80]], 3).reshape(P, -1)
    wkv = a["mla_w_kvb"][0].reshape(P, MH, 128)
    put("mla", np.concatenate([wq, wkv[:, :, :64].reshape(P, -1), wkv[:, :, 64:].reshape(P, -1)], 1))
    for n in range(2):
        put(f"out1_{n}", tokens(a["w_out"][0][:, 512 * n:512 * n + 512]))
    gate, up = features(a["w_gate"][0]), features(a["w_up"][0])
    down1 = a["w_down"][0].reshape(FT1, P, D).transpose(1, 0, 2)
    for n in range(FT1 // 2):
        put(f"gu{n}", np.stack([gate[:, 2 * n:2 * n + 2], up[:, 2 * n:2 * n + 2]], 2))
        if n % 2 == 1 or n == FT1 // 2 - 1:
            put(f"dn1_{n // 2}", down1[:, 4 * (n // 2):4 * (n // 2) + 4])
    w = a["w_in_2"][0]
    sizes = [1024, 1024, 1024, 1024, 8, 8, 1024, 256, 256, 256, 256, 256, 256, 48, 1024, 1024]
    (q, k, v, z, _b, _a, nq, kc, vc, ks, vs, kw, vw, _g, gd, gn) = np.split(w, np.cumsum(sizes)[:-1], axis=1)
    nq = nq.reshape(D, 2, 8, ND).transpose(0, 2, 1, 3).reshape(D, D)
    ks, kw = (m.reshape(D, 2, 2, ND).transpose(0, 2, 1, 3).reshape(D, 256) for m in (ks, kw))
    for tag, m in [("qnsa", nq), ("z", z), ("gn", gn), ("gd", gd), ("pn", a["w_proj_nsa_2"][0]), ("pd", a["w_proj_dn_2"][0])]:
        for n in range(2):
            put(f"{tag}{n}", tokens(m[:, 512 * n:512 * n + 512]))
    for n in range(2):
        put(f"out2_{n}", tokens(a["w_out_2"][0][:, 512 * n:512 * n + 512]))
    put("ksw", tokens(np.concatenate([ks, kw], 1)))
    put("vsw", tokens(np.concatenate([vs, vw], 1)))
    put("kvc", features(np.concatenate([kc, vc], 1)))
    for tag, m in [("dk", k), ("dv", v), ("dq", q)]:
        for n in range(2):
            put(f"{tag}{n}", features(m[:, 512 * n:512 * n + 512]))
    w1 = np.stack([a["cmp_w1_k_2"][0], a["cmp_w1_v_2"][0]]).reshape(2, CL // 2, P, P)
    put("cmp", w1.transpose(2, 0, 1, 3))
    up2 = features(a["w_up_2"][0])
    down2 = a["w_down_2"][0].reshape(FT2, P, D).transpose(1, 0, 2)
    for n in range(8):
        put(f"up{n}", up2[:, 4 * n:4 * n + 4])
        put(f"dn2_{n}", down2[:, 4 * n:4 * n + 4])
    return flat


def kernel(**inputs):
    import concourse.bacc as bacc
    from concourse.bass_utils import run_bass_kernel_spmd

    a = {k: np.asarray(v) for k, v in inputs.items()}
    arrays = {"consts": shape_constants(), "params": laid_params(a), "weights": laid_weights(a),
              "x": np.ascontiguousarray(a["x"][0]), "meta": np.ascontiguousarray(a["meta_tokens"])}
    nc = bacc.Bacc("TRN2", target_bir_lowering=False, num_devices=1)
    ins = {k: nc.dram_tensor(k, v.shape, F32, kind="ExternalInput").ap() for k, v in arrays.items()}
    out = nc.dram_tensor("out", (SEQ, D), F32, kind="ExternalOutput").ap()
    lines = nc.dram_tensor("lines", (P, BH, 2 * LINE), F32, kind="Internal").ap()
    build(nc, ins["consts"], ins["params"], ins["weights"], ins["x"], ins["meta"], out, lines)
    r = run_bass_kernel_spmd(nc, [arrays], core_ids=[0])
    return r.results[0]["out"].reshape(1, SEQ, D)
```

```python
import math
from contextlib import ExitStack

import numpy as np

import concourse.bass as bass
from concourse import mybir

F32 = mybir.dt.float32
I32 = mybir.dt.int32
F32R = mybir.dt.float32r
ALU = mybir.AluOpType
ACT = mybir.ActivationFunctionType
AXX = mybir.AxisListType.X

P = 128
D = 1024
KD = D // P
SEQ = 256
TT = SEQ // P
META = 16
ALL = META + SEQ
EPS = 1e-6
NEG = -1e30
MH, MQR, MKR, NOPE, ROPE, MV = 6, 256, 128, 64, 32, 64
DH, DQK, DV = 4, 32, 64
SH, SG, SD, WIN = 6, 2, 64, 128
BUCKETS, BH = 32, 10
FF1 = 2816
FT1 = FF1 // P
LAM0 = 0.8 - 0.6 * math.exp(0.0)
LINE = ALL + P - 1
NH2, GH = 8, 4
NSH, NSG, ND = 16, 4, 64
CL, CS, NC = 32, 16, 15
FF2 = 4096
FT2 = FF2 // P
LEVELS = 7
PIECE = 1024
RAW, SPLIT = 5, 6
AHEAD = 4

CONST = {}
PARAM = {}


def _place(table, names):
    at = 0
    for name, width in names:
        table[name] = (at, width)
        at += width
    return at


NCONST = _place(CONST, [("ident", P), ("upper", P), ("negdist", 2 * P),
                        ("cmpbias", TT * NSH * NC), ("valid", TT), ("causal", ALL),
                        ("onehot", 2 * LINE), ("cos", ALL), ("sin", ALL), ("level", LEVELS * P)])
NCHELD = CONST["causal"][0]
NEARLY = CONST["onehot"][0]
NLATE = CONST["level"][0]
NPARAM = _place(PARAM, [("attn_norm", KD), ("ffn_norm", KD), ("norm_mix", KD), ("norm_mlp", KD),
                        ("q_norm", MQR // P), ("kv_norm", 1), ("subln", 1), ("dn_out", 1), ("nsa_q", 1),
                        ("k_cmp", 1), ("k_slc", 1), ("k_win", 1), ("conv", 24 * 4), ("w2k", ND),
                        ("w2v", ND), ("pos_k", CL // 2), ("pos_v", CL // 2), ("rel", BH), ("lam", 4 * DQK),
                        ("sinks", SH), ("a_log", NH2), ("dt", NH2), ("final", D)])
NHELD = NPARAM - D

WIDTHS = {}


def _pieces(name, count, width=PIECE):
    for n in range(count):
        WIDTHS[f"{name}.{n}"] = width


FEATURES1 = ["cq0", "cq1", "ckv", "dq0", "dq1", "dk0", "dk1", "sq0", "sq1", "sq2", "sk", "krA", "krB"]
for _n in FEATURES1:
    WIDTHS["in1_" + _n] = PIECE
_pieces("in1t", 4, 2 * 384)
WIDTHS["mla.0"], WIDTHS["mla.1"], WIDTHS["mla.2"] = PIECE, 2 * 2 * P + MH * 64, MH * 64
_pieces("out1_0", 4)
_pieces("out1_1", 4)
for _f in range(FT1):
    WIDTHS[f"gate.{_f}"] = WIDTHS[f"up1.{_f}"] = PIECE
    if _f >= 5 and _f % 4 == 1:
        for _g in range(_f - 5, _f - 1):
            WIDTHS[f"down1.{_g}"] = PIECE
for _g in range(FT1 - 2, FT1):
    WIDTHS[f"down1.{_g}"] = PIECE
_pieces("small", 1, KD * 64)
for _n in ["kvc", "qnsa0", "qnsa1", "ksw", "cmp", "vsw", "dk0", "dk1", "dv0", "dv1", "dq0", "dq1", "z0", "z1",
           "gn0", "gn1", "gd0", "gd1", "pn0", "pn1", "pd0", "pd1", "out2_0", "out2_1"]:
    _pieces(_n, 4)
for _n in range(8):
    for _f in range(4 * _n, 4 * _n + 4):
        WIDTHS[f"up2.{_f}"] = PIECE
    if _n >= 1:
        for _f in range(4 * _n - 4, 4 * _n):
            WIDTHS[f"down2.{_f}"] = PIECE
for _f in range(28, 32):
    WIDTHS[f"down2.{_f}"] = PIECE
PIECES = list(WIDTHS)
WHOLE = {n for n in PIECES if n.split(".")[0] in ("mla", "cmp")}
BY_POOL = {n for n in PIECES if "." in n and n.split(".")[0] in ("dv1", "dq0", "dq1", "z0", "z1")}
INDEX = {n: i for i, n in enumerate(PIECES)}
PARTED = [n for n in PIECES if n not in WHOLE]
PART = {n: i for i, n in enumerate(PARTED)}
TURN = {n: sum((m in BY_POOL) == (n in BY_POOL) for m in PARTED[:i + 1]) for i, n in enumerate(PARTED)}
STARTS = {}
_at = 0
for _n, _w in WIDTHS.items():
    STARTS[_n] = _at
    _at += P * _w
TOTAL = _at


def build(nc, consts, params, weights, x, meta, out, line_dram):
    ctx = ExitStack()
    with ctx:
        def sb(name, shape, dt=F32):
            return ctx.enter_context(nc.sbuf_tensor(name, shape, dt))

        sems = {}

        def sem(name):
            if name not in sems:
                sems[name] = ctx.enter_context(nc.semaphore(name))
            return sems[name]

        psum = ctx.enter_context(nc.psum_tensor("psum", [P, 8, 512], F32))
        raw = sb("raw", [P, RAW, PIECE])
        parts = sb("parts", [P, SPLIT, 2, PIECE], F32R)
        cbuf = sb("cbuf", [P, NCHELD])
        pbuf = sb("pbuf", [P, NHELD])
        X = sb("X", [P, TT, D])
        hT = sb("hT", [P, 2, KD, ALL], F32R)
        ones = sb("ones", [P, P])
        st = sb("st", [P, 192])
        ARENA = 25472
        with nc.sbuf_tensor("arena", [P, ARENA], F32) as arena:
            pass
        arena_r = sb("arena_r", [P, ARENA], F32R)

        def cst(name, rows=P):
            a, w = CONST[name]
            if a >= NLATE:
                return dn["level"]
            if a >= NEARLY:
                return att1["S"][0:rows, a - NEARLY:a - NEARLY + w]
            if a >= NCHELD:
                return att1["causal"][0:rows, :]
            return cbuf[0:rows, a:a + w]

        def par(name, rows=P):
            a, w = PARAM[name]
            return pbuf[0:rows, a:a + w]

        ident = cbuf[:, 0:P]

        def lay(start, names):
            at, got = start, {}
            for name, width in names:
                got[name] = arena[:, at:at + width]
                at += width
            assert at <= ARENA, at
            return got

        def both(start, tiles, width):
            assert start + 2 * tiles * width <= ARENA
            return arena_r[:, start:start + 2 * tiles * width].rearrange("p (s k n) -> p s k n", s=2, k=tiles)

        KM = 4 * ALL
        one = lay(0, [("Xm", D), ("Xn", TT * D), ("Xnm", D), ("cT", 3 * ALL), ("cnT", 3 * ALL), ("sqT", 3 * ALL),
                      ("rs", 3 * ALL), ("qT", MH * SEQ), ("kT", MH * ALL), ("dqT", 2 * SEQ), ("dkT", 2 * ALL),
                      ("sQT", 3 * SEQ), ("sKT", ALL), ("V", 3 * 768), ("dz", DH * ALL), ("sz0", SH * 144),
                      ("sz1", SH * ALL), ("rot", 4 * ALL)])
        end = sum(w for w in [D, TT * D, D, 12 * ALL, MH * SEQ, MH * ALL, 2 * SEQ, 2 * ALL, 3 * SEQ, ALL, 3 * 768,
                              DH * ALL, SH * 144, SH * ALL, 4 * ALL])
        att1 = lay(end, [("S", 2 * KM), ("PTm", 2 * 512), ("final", D), ("causal", ALL)])
        att1 |= lay(0, [("PT", 2 * 4 * SEQ), ("y", TT * D)])
        yT = both(4096, KD, SEQ)
        ffn1 = lay(0, [("Xn", TT * D), ("sg", 4 * SEQ), ("v", 4 * SEQ)])
        aT = both(8192, FT1, SEQ)
        two = lay(0, [("Xn", TT * D)])
        nsa = lay(0, [("PT", 2 * 4 * SEQ), ("Q", TT * D), ("qT", KD * SEQ), ("ksw", TT * 512), ("KT", 4 * SEQ),
                      ("VV", TT * 512), ("blk", 2 * 16 * 60), ("alibi", NSH * SEQ), ("cv", 3 * NH2 * SEQ),
                      ("Z", TT * D), ("O", TT * D)])
        nsa["S"] = nsa["Q"]
        nsa["PTm"] = nsa["ksw"]
        dn = lay(0, [("Kt", 2048), ("KnT", 2048), ("Vb", 2048), ("DT", 2048), ("QKD", 2048), ("LT", 2048), ("Xi", 2048),
                     ("level", LEVELS * P)])
        dn["M"] = nsa["cv"][:, 0:2048]
        dn["Yi"] = nsa["cv"][:, 2048:4096]
        dnp = nsa
        onT = both(0, KD, SEQ)
        odT = both(15232, KD, SEQ)
        mixT = both(0, KD, SEQ)
        a2 = both(8192, FT2, SEQ)
        junk3 = [arena[:, at:at + TT * D].rearrange("p (t n) -> p t n", t=TT) for at in (4096, end)]
        relu2 = arena[:, 0:2048].rearrange("p (s n) -> p s n", s=4)

        bank_full = [sem(f"bank{b}_full") for b in range(8)]
        bank_free = [sem(f"bank{b}_free") for b in range(8)]
        used = [0] * 8
        jobs = {}
        turn = [0, 8]

        def bank_of(name):
            return psum[:, jobs[name][0], :]

        job_piece = {}
        keep_ahead = {}

        def full(eng, name):
            if eng in keep_ahead:
                keep_ahead[eng](job_piece[name] + AHEAD)
            b, n = jobs[name]
            eng.wait_ge(bank_full[b], n + 1)

        def freed(eng, name):
            if eng in keep_ahead:
                keep_ahead[eng](job_piece[name] + AHEAD)
            b, n = jobs[name]
            eng.wait_ge(bank_free[b], n + 1)

        def release(ins, name):
            ins.then_inc(bank_free[jobs[name][0]], 1)

        counts = {}

        def signal(ins, name, by=1):
            ins.then_inc(sem(name), by)
            counts[name] = counts.get(name, 0) + by
            return counts[name]

        piece_used = {}

        def used_up(eng, name):
            after = piece_used[name]
            if isinstance(after, tuple):
                eng.wait_ge(sem(after[0]), after[1])
            else:
                b, n = jobs[after]
                eng.wait_ge(bank_full[b], n + 1)

        def loaded(eng, name):
            i = INDEX[name]
            eng.wait_ge(sem(f"piece_in{i % RAW}"), 16 * (i // RAW + 1))
            return raw[:, i % RAW, 0:WIDTHS[name]]

        def split_slot(name):
            j = PART[name] % SPLIT
            return parts[:, j, 0, 0:WIDTHS[name]], parts[:, j, 1, 0:WIDTHS[name]]

        def slot_free(eng, name):
            j = PART[name]
            if j >= SPLIT:
                used_up(eng, PARTED[j - SPLIT])

        def groups_one():
            got = []
            for qt in range(TT):
                keys = META + P * (qt + 1)
                for name, hs in [("mla", range(0, 4)), ("mla", range(4, 6)), ("dif", range(0, 2)), ("dif", range(2, 4)),
                                 ("swa", range(0, 4)), ("swa", range(4, 6))]:
                    got.append(dict(kind=name, qt=qt, hs=list(hs), keys=keys, meta=META, tiles=qt + 1,
                                    name=f"{name}{qt}_{hs[0]}"))
            return got

        def groups_two():
            got = []
            for qt in range(TT):
                for g in range(NSG):
                    hs = list(range(4 * g, 4 * g + 4))
                    got.append(dict(kind="cmp", qt=qt, hs=hs, keys=NC, meta=NC, tiles=0, name=f"cmp{qt}_{g}"))
                    for kind in ("slc", "win"):
                        got.append(dict(kind=kind, qt=qt, hs=hs, keys=P * (qt + 1), meta=0, tiles=qt + 1,
                                        name=f"{kind}{qt}_{g}"))
            return got

        G1, G2 = groups_one(), groups_two()
        CONVOLVED = [(w, p, first, n) for w, p in (("v", 1), ("q", 2)) for first in (0, 4) for n in range(2)]
        EARLY = CONVOLVED[:1]
        FILLERS = CONVOLVED[1:]
        FILL = [0, 1, 3, 4, 7, 10, 13]
        n_maps = 0
        for i, g in enumerate(G1 + G2):
            if i == len(G1):
                n_maps = 0
            g["maps"] = [(h, c) for h in g["hs"] for c in range(2)] if g["kind"] == "dif" else [(h, 0) for h in g["hs"]]
            g["first"] = n_maps
            n_maps += len(g["maps"])
            g["last"] = n_maps
            g["per"] = 1 if g["kind"] == "dif" else min(len(g["maps"]), 512 // g["keys"])
        for G in (G1, G2):
            for i, g in enumerate(G):
                g["i"] = i
                g["difs"] = sum(q["kind"] == "dif" for q in G[:i + 1])
                g["swas"] = sum(q["kind"] == "swa" for q in G[:i + 1])

        def heads_v(g, h):
            if g["kind"] in ("mla", "dif", "swa"):
                V = one["V"].rearrange("p (t n) -> p t n", t=3)
                off = {"mla": 64 * h, "dif": 384 + 64 * h, "swa": 640 + 64 * (h // 3)}[g["kind"]]
                return [V[:, 1 + t, off:off + 64] for t in range(2)], V[0:META, 0, off:off + 64]
            if g["kind"] == "cmp":
                return [], vc[0:NC, 64 * (h // 4):64 * (h // 4) + 64]
            off = {"slc": 0, "win": 256}[g["kind"]] + 64 * (h // 4)
            V = nsa["VV"].rearrange("p (t n) -> p t n", t=TT)
            return [V[:, t, off:off + 64] for t in range(TT)], None

        def heads_qk(g, h, c):
            qs = slice(P * g["qt"], P * g["qt"] + P)
            ks = slice(0, g["keys"])
            if g["kind"] == "mla":
                return (one["qT"].rearrange("p (h n) -> p h n", h=MH)[0:96, h, qs],
                        one["kT"].rearrange("p (h n) -> p h n", h=MH)[0:96, h, ks])
            if g["kind"] == "dif":
                r = 32 * ((2 * h + c) % 4)
                return (one["dqT"].rearrange("p (h n) -> p h n", h=2)[r:r + 32, h // 2, qs],
                        one["dkT"].rearrange("p (h n) -> p h n", h=2)[r:r + 32, h // 2, ks])
            if g["kind"] == "swa":
                r = 64 * (h // 3)
                return (one["sQT"].rearrange("p (h n) -> p h n", h=3)[r:r + 64, h % 3, qs], one["sKT"][r:r + 64, ks])
            r = 64 * (h // 8)
            q = nsa["qT"].rearrange("p (h n) -> p h n", h=KD)[r:r + 64, h % 8, qs]
            if g["kind"] == "cmp":
                return q, kcT[r:r + 64, (h // 4) % 2, 0:NC]
            slot = {"slc": 0, "win": 2}[g["kind"]] + (h // 4) % 2
            return q, nsa["KT"].rearrange("p (h n) -> p h n", h=4)[r:r + 64, slot, ks]

        def map_bias(g, h):
            if g["kind"] == "mla":
                return cst("causal")[:, P * (1 - g["qt"]):ALL]
            if g["kind"] == "dif":
                return one["dz"].rearrange("p (h n) -> p h n", h=DH)[:, h, P * (1 - g["qt"]):ALL]
            if g["kind"] == "swa":
                return one["sz0" if g["qt"] == 0 else "sz1"].rearrange("p (h n) -> p h n", h=SH)[:, h, :]
            if g["kind"] == "cmp":
                return cst("cmpbias").rearrange("p (t h n) -> p t h n", t=TT, h=NSH)[:, g["qt"], h, :]
            return nsa["alibi"].rearrange("p (h n) -> p h n", h=NSH)[:, h, P * (1 - g["qt"]):2 * P]

        def slabs(g):
            own, width = (att1, ALL) if g["kind"] in ("mla", "dif", "swa") else (nsa, SEQ)
            par_ = g["i"] % 2
            S = own["S"].rearrange("p (b m n) -> p b m n", b=2, m=4)[:, par_]
            PT = own["PT"].rearrange("p (b m n) -> p b m n", b=2, m=4)[:, par_]
            PTm = own["PTm"].rearrange("p (b n) -> p b n", b=2)[:, par_]
            return S, S, PT, PTm

        sig = sb("sig", [P, 112])
        soft = sb("soft", [P, 96])
        gl = sb("gl", [P, TT, NH2])
        gcb = sb("gcb", [P, 64])
        hid = sb("hid", [P, 2, 60])
        kcT = sb("kcT", [P, 2, 16])
        vc = sb("vc", [16, 256])
        be = sig[:, 0:16].rearrange("p (t h) -> p t h", t=TT)
        sums = sb("sums", [P, 96])
        peaks = sb("peaks", [P, 96])
        npeaks = sb("npeaks", [P, 96])
        scr = sb("scr", [P, 514])
        kcn = nsa["O"][0:16, 0:256]
        difsum = sb("difsum", [P, 40])
        nsinks = sb("nsinks", [P, 8])

        def map_slot(g, buf, n):
            return buf[:, n, 0:g["keys"]]

        def probs_slot(g, n):
            return 2 * n if g["kind"] == "dif" else n

        def last_turn(g):
            per = 512 // (P * g["tiles"]) if g["tiles"] else 0
            return f"tt_{g['name']}_{(len(g['hs']) - 1) // per}" if per else f"tm_{g['name']}"

        block = ctx.enter_context(nc.Block())

        @block.tensor
        def _(pe):
            mm = nc.tensor.matmul
            taken = [1 - AHEAD]

            def opened(name, bank=None):
                if bank is None:
                    bank = turn[0] % turn[1]
                    turn[0] += 1
                if used[bank]:
                    pe.wait_ge(bank_free[bank], used[bank])
                jobs[name] = (bank, used[bank])
                used[bank] += 1
                return psum[:, bank, :]

            def closed(ins, name):
                ins.then_inc(bank_full[jobs[name][0]], 1)
                job_piece[name] = taken[0]

            def whole(name):
                taken[0] = INDEX[name.split(".")[0] + ".0"]
                return loaded(pe, name)

            def split(name):
                taken[0] = INDEX[name] + 1
                pe.wait_ge(sem("split_pool" if name in BY_POOL else "split_vector"), TURN[name])
                return split_slot(name)

            def done_with(name, last):
                piece_used[name] = ("piece_used", signal(last, "piece_used"))

            def three(ps, stationary, moving, start, stop):
                (a, b), (c, d) = stationary, moving
                mm(ps, a, c, start=start, stop=False)
                mm(ps, a, d, start=False, stop=False)
                return mm(ps, b, c, start=False, stop=stop)

            arrivals = {}

            def need(k):
                if k in arrivals:
                    freed(pe, arrivals.pop(k))

            def transposes_of(src, name_of, gain_tiles=KD, meta=None):
                for k in range(gain_tiles):
                    name = name_of(k)
                    ps = opened(name)
                    at = 0
                    if meta is not None:
                        nc.tensor.transpose(ps[:, 0:META], meta[0:META, P * k:P * k + P], ident[0:META, 0:META])
                        at = META
                    for t in range(TT):
                        last = nc.tensor.transpose(ps[:, at + P * t:at + P * t + P], src[:, t, P * k:P * k + P], ident)
                    closed(last, name)
                    arrivals[k] = name

            def feature_product(name, cols, ps, acts=hT):
                w = [half.rearrange("p (k n) -> p k n", k=KD) for half in split(name)]
                for k in range(KD):
                    need(k)
                    last = three(ps, [h[:, k, :] for h in w], [acts[:, s, k, cols] for s in range(2)],
                                 k == 0, k == KD - 1)
                return last

            def token_products(unit, tiles, acts, width=512):
                for job, cols in tiles:
                    opened(job)
                for j in range(4):
                    name = f"{unit}.{j}"
                    w = [half.rearrange("p (k n) -> p k n", k=2) for half in split(name)]
                    for job, cols in tiles:
                        for k in range(2):
                            need(2 * j + k)
                            last = three(bank_of(job)[:, 0:width], [acts[:, s, 2 * j + k, cols] for s in range(2)],
                                         [h[:, k, :] for h in w], j == 0 and k == 0, j == 3 and k == 1)
                        if j == 3:
                            closed(last, job)
                    if j == 3:
                        piece_used[name] = tiles[-1][0]
                    else:
                        done_with(name, last)

            def scores(g):
                for n, (h, c) in enumerate(g["maps"]):
                    name = f"qk_{g['name']}_{n // g['per']}"
                    if n % g["per"] == 0:
                        ps = opened(name)
                    q, k = heads_qk(g, h, c)
                    at = g["keys"] * (n % g["per"])
                    last = mm(ps[:, at:at + g["keys"]], q, k, start=True, stop=True)
                    if n % g["per"] == g["per"] - 1 or n == len(g["maps"]) - 1:
                        closed(last, name)

            def turned(g):
                S, E, PT, PTm = slabs(g)
                block_no = "1" if g["kind"] in ("mla", "dif", "swa") else "2"
                if g["kind"] == "dif":
                    pe.wait_ge(sem("differences"), g["difs"])
                else:
                    pe.wait_ge(sem("probs" + block_no), g["last"])
                nm = len(g["hs"])
                if g["meta"]:
                    name = f"tm_{g['name']}"
                    ps = opened(name)
                    for n in range(nm):
                        last = nc.tensor.transpose(ps[0:g["meta"], P * n:P * n + P], E[:, probs_slot(g, n), 0:g["meta"]], ident)
                    closed(last, name)
                per = 512 // (P * g["tiles"]) if g["tiles"] else 0
                for n in range(nm if per else 0):
                    name = f"tt_{g['name']}_{n // per}"
                    if n % per == 0:
                        ps = opened(name)
                    for t in range(g["tiles"]):
                        at = P * ((n % per) * g["tiles"] + t)
                        last = nc.tensor.transpose(ps[:, at:at + P], E[:, probs_slot(g, n), g["meta"] + P * t:g["meta"] + P * t + P],
                                                   ident)
                    if n % per == per - 1 or n == nm - 1:
                        closed(last, name)

            def weighted(g):
                S, E, PT, PTm = slabs(g)
                name = f"pv_{g['name']}"
                nm = len(g["hs"])
                if g["meta"]:
                    freed(pe, f"tm_{g['name']}")
                if g["tiles"]:
                    per = 512 // (P * g["tiles"])
                    for j in range((nm + per - 1) // per):
                        freed(pe, f"tt_{g['name']}_{j}")
                ps = opened(name)
                for n, h in enumerate(g["hs"]):
                    vt, vm = heads_v(g, h)
                    o = ps[:, 64 * n:64 * n + 64]
                    if g["meta"]:
                        last = mm(o, PTm[0:g["meta"], P * n:P * n + P], vm, start=True, stop=g["tiles"] == 0)
                    for t in range(g["tiles"]):
                        at = P * (n * g["tiles"] + t)
                        flat = PT.rearrange("p m n -> p (m n)")
                        last = mm(o, flat[:, at:at + P], vt[t], start=(t == 0 and not g["meta"]),
                                  stop=(t == g["tiles"] - 1))
                closed(last, name)

            def attention(G, between):
                scores(G[0])
                for i, g in enumerate(G):
                    if i + 1 < len(G):
                        scores(G[i + 1])
                    for step in between.get(i, ()):
                        step()
                    turned(g)
                    if i >= 1:
                        weighted(G[i - 1])
                weighted(G[-1])

            pe.wait_ge(sem("const_in"), 64)
            pe.wait_ge(sem("norm1"), 2)
            pe.wait_ge(sem("norm1_act"), 1)
            Xn = one["Xn"].rearrange("p (t n) -> p t n", t=TT)
            transposes_of(Xn, lambda k: f"h1_{k}", meta=one["Xnm"])
            for v in range(2):
                if v == 0:
                    pe.wait_ge(sem("relneg"), 1)
                ps = opened(f"line{v}")
                oh = cst("onehot").rearrange("p (v n) -> p v n", v=2)
                a = PARAM["rel"][0]
                closed(mm(ps[0:BH, 0:LINE], pbuf[0:33, a:a + BH], oh[0:33, v, :], start=True, stop=True), f"line{v}")
            def latent_sums():
                pe.wait_ge(sem("ones"), 1)
                ps = opened("lat_q")
                pe.wait_ge(sem("lat_sq"), 3)
                sq = one["sqT"].rearrange("p (c n) -> p c n", c=3)
                mm(ps[:, 0:ALL], ones[:, :], sq[:, 0, :], start=True, stop=False)
                closed(mm(ps[:, 0:ALL], ones[:, :], sq[:, 1, :], start=False, stop=True), "lat_q")
                ps = opened("lat_kv")
                closed(mm(ps[:, 0:ALL], ones[:, :], sq[:, 2, :], start=True, stop=True), "lat_kv")

            real = slice(META, ALL)
            every = slice(0, ALL)
            for what in FEATURES1:
                name = "p1_" + what
                ps = opened(name)
                cols = real if what[:2] in ("dq", "sq") else every
                w = ALL if cols is every else SEQ
                closed(feature_product("in1_" + what, cols, ps[:, 0:w]), name)
                piece_used["in1_" + what] = name
                if what == "dq1":
                    latent_sums()
            token_products("in1t", [("vt_m", slice(0, P))] + [(f"vt_{t}", slice(META + P * t, META + P * t + P))
                                                            for t in range(TT)], hT, 384)
            u0, u1, wv = whole("mla.0"), whole("mla.1"), whole("mla.2")
            wq = [w.rearrange("p (h k n) -> p h k n", k=2, n=P) for w in (u0, u1[:, 0:2 * 2 * P])]
            wk = u1[:, 2 * 2 * P:].rearrange("p (h n) -> p h n", h=MH)
            cn = one["cnT"].rearrange("p (c n) -> p c n", c=3)
            pe.wait_ge(sem("lat_norm"), 3)
            for h in range(MH):
                ps = opened(f"mq_{h}")
                for k in range(2):
                    mm(ps[0:96, 0:SEQ], wq[h // 4][:, h % 4, k, 0:96], cn[:, k, real], start=(k == 0), stop=(k == 1))
                for k in range(2):
                    last = mm(ps[64:96, SEQ:2 * SEQ], wq[h // 4][:, h % 4, k, 96:128], cn[:, k, real], start=(k == 0), stop=(k == 1))
                closed(last, f"mq_{h}")
                ps = opened(f"mk_{h}")
                closed(mm(ps[0:64, 0:ALL], wk[:, h, :], cn[:, 2, :], start=True, stop=True), f"mk_{h}")
            for t in range(-1, TT):
                name = f"mv_{t}"
                ps = opened(name)
                m, cols = (META, slice(0, META)) if t < 0 else (P, slice(META + P * t, META + P * t + P))
                closed(mm(ps[0:m, 0:384], cn[:, 2, cols], wv, start=True, stop=True), name)
            piece_used["mla.0"] = piece_used["mla.1"] = piece_used["mla.2"] = "mv_1"
            freed(pe, f"mq_{MH - 1}")
            freed(pe, f"mk_{MH - 1}")
            freed(pe, "mv_1")
            freed(pe, "p1_sk")
            pe.wait_ge(sem("krot"), 1)
            attention(G1, {})
            y = att1["y"].rearrange("p (t n) -> p t n", t=TT)
            pe.wait_ge(sem("y1"), 2)
            freed(pe, "pv_" + G1[-1]["name"])
            transposes_of(y, lambda k: f"yT1_{k}")
            tiles2 = [slice(P * t, P * t + P) for t in range(TT)]
            for nh in range(2):
                token_products(f"out1_{nh}", [(f"o1_{nh}_{t}", tiles2[t]) for t in range(TT)], yT)
            def norm_turn(tag, count, src):
                pe.wait_ge(sem(tag), count)
                pe.wait_ge(sem(tag + "_act"), 1)
                transposes_of(src, lambda k: f"{tag}_{k}")

            norm_turn("norm2", 1, ffn1["Xn"].rearrange("p (t n) -> p t n", t=TT))
            tok = slice(0, SEQ)

            def down(what, f0, nf, tag, tiles, acts, ready):
                ready(f0, nf)

                def halves(f, t):
                    w = split(f"{what}.{f}")
                    for nh in range(2):
                        job = f"{tag}_{t}_{nh}"
                        if f == 0:
                            opened(job, 4 + 2 * t + nh)
                        last = three(bank_of(job), [acts[:, s, f, tiles2[t]] for s in range(2)],
                                     [h[:, 512 * nh:512 * nh + 512] for h in w], f == 0, f == tiles - 1)
                        if f == tiles - 1:
                            closed(last, job)
                    return last

                if f0 + nf == tiles:
                    for t in range(TT):
                        for f in range(f0, f0 + nf):
                            last = halves(f, t)
                            if t == 0:
                                continue
                            if f == tiles - 1:
                                piece_used[f"{what}.{f}"] = f"{tag}_1_1"
                            else:
                                done_with(f"{what}.{f}", last)
                    return
                for f in range(f0, f0 + nf):
                    for t in range(TT):
                        last = halves(f, t)
                    done_with(f"{what}.{f}", last)

            turn[0], turn[1] = 0, 4

            def hidden1(f0, nf):
                pe.wait_ge(sem("hidden1"), f0 + nf)

            def hidden2(f0, nf):
                pe.wait_ge(sem("hidden2"), (f0 + nf) // 2)

            for f in range(FT1):
                name = f"gu_{f}"
                ps = opened(name)
                done_with(f"gate.{f}", feature_product(f"gate.{f}", tok, ps[:, 0:SEQ]))
                closed(feature_product(f"up1.{f}", tok, ps[:, SEQ:2 * SEQ]), name)
                piece_used[f"up1.{f}"] = name
                if f >= 5 and f % 4 == 1:
                    down("down1", f - 5, 4, "d1", FT1, aT, hidden1)
            down("down1", FT1 - 2, 2, "d1", FT1, aT, hidden1)
            turn[0], turn[1] = 0, 8
            norm_turn("norm3", 1, two["Xn"].rearrange("p (t n) -> p t n", t=TT))

            def two_tokens(uname, tag, acts=hT):
                token_products(uname, [(f"{tag}_{t}", tiles2[t]) for t in range(TT)], acts)

            w = [half.rearrange("p (k n) -> p k n", k=KD) for half in split("small.0")]
            for t in range(TT):
                ps = opened(f"small_{t}")
                for k in range(KD):
                    need(k)
                    last = three(ps[:, 0:64], [hT[:, s, k, tiles2[t]] for s in range(2)], [h[:, k, :] for h in w],
                                 k == 0, k == KD - 1)
                closed(last, f"small_{t}")
            piece_used["small.0"] = "small_1"
            def feature_pair(uname, n, name):
                ps = opened(name)
                for j in range(2):
                    piece = f"{uname}.{2 * n + j}"
                    last = feature_product(piece, tok, ps[:, SEQ * j:SEQ * j + SEQ])
                    if j == 0:
                        done_with(piece, last)
                closed(last, name)
                piece_used[piece] = name

            def conv_half(which, place, first, n):
                feature_pair(f"d{which}{first // 4}", n, f"cv_{which}{first // 2 + n}")

            def z_half(n):
                two_tokens(f"z{n}", f"z{n}")

            for n in range(2):
                feature_pair("kvc", n, f"kvc_{n}")
            for n in range(2):
                two_tokens(f"qnsa{n}", f"nq{n}")
            two_tokens("ksw", "nk")
            u = [whole(f"cmp.{n}").rearrange("p (l n) -> p l n", n=P) for n in range(4)]
            blk = nsa["blk"].rearrange("p (s l n) -> p s l n", s=2, l=16)
            freed(pe, "kvc_0")
            freed(pe, "kvc_1")
            ps = opened("hid")
            for s in range(2):
                for l in range(16):
                    last = mm(ps[:, 64 * s:64 * s + 60], u[2 * s + l // 8][:, l % 8, :], blk[:, s, l, :], start=(l == 0), stop=(l == 15))
            closed(last, "hid")
            for n in range(4):
                piece_used[f"cmp.{n}"] = "hid"
            two_tokens("vsw", "nv")
            freed(pe, "hid")
            ps = opened("kvc2")
            for s in range(2):
                for g in range(NSG):
                    slot = g if s else 2 * (g % 2) + g // 2
                    last = mm(ps[0:NC, 256 * s + 64 * slot:256 * s + 64 * slot + 64], hid[:, s, 15 * g:15 * g + 15],
                              par("w2k" if s == 0 else "w2v"), start=True, stop=True)
            closed(last, "kvc2")
            Q = nsa["Q"].rearrange("p (t n) -> p t n", t=TT)
            pe.wait_ge(sem("nq_norm"), 2)
            for k in range(KD):
                name = f"nqT_{k}"
                ps = opened(name)
                for t in range(TT):
                    last = nc.tensor.transpose(ps[:, P * t:P * t + P], Q[:, t, P * k:P * k + P], ident)
                closed(last, name)
            for n in range(2):
                conv_half("k", 0, 0, n)
            ps = opened("kcT")
            pe.wait_ge(sem("kc_norm"), 1)
            for s in range(2):
                last = nc.tensor.transpose(ps[:, 16 * s:16 * s + NC], kcn[0:NC, P * s:P * s + P], ident[0:NC, 0:NC])
            closed(last, "kcT")
            ksw = nsa["ksw"].rearrange("p (t n) -> p t n", t=TT)
            pe.wait_ge(sem("nk_norm"), 2)
            for b in range(2):
                name = f"nkT_{b}"
                ps = opened(name)
                for s in range(2):
                    for t in range(TT):
                        src = ksw[:, t, 256 * b + P * s:256 * b + P * s + P]
                        at = SEQ * s + P * t
                        last = nc.tensor.transpose(ps[:, at:at + P], src, ident)
                closed(last, name)
            for n in range(2):
                conv_half("k", 0, 4, n)
            for what in EARLY:
                conv_half(*what)
            freed(pe, "kcT")
            for k in range(KD):
                freed(pe, f"nqT_{k}")
            freed(pe, "nkT_0")
            freed(pe, "nkT_1")
            freed(pe, "nv_0")
            freed(pe, "nv_1")
            pe.wait_ge(sem("alibi"), 16)
            extra = {i: [lambda w=what: conv_half(*w)] for i, what in zip(FILL, FILLERS)}
            attention(G2, extra)
            cv = dnp["cv"].rearrange("p (w h n) -> p w h n", w=3, h=NH2)

            def cv_turn(w, tag):
                for t in range(TT):
                    for q in range(2):
                        name = f"{tag}_{t}_{q}"
                        ps = opened(name)
                        for n in range(GH):
                            last = nc.tensor.transpose(ps[:, P * n:P * n + P], cv[:, w, GH * q + n, P * t:P * t + P], ident)
                        closed(last, name)

            pe.wait_ge(sem("conv_done"), 24)
            cv_turn(0, "kt")
            cv_turn(1, "vt2")
            z_half(0)
            cv_turn(2, "qt2")
            pe.wait_ge(sem("gates"), 1)
            ps = opened("gc")
            for t in range(TT):
                mm(ps[:, 8 * t:8 * t + 8], cst("upper"), gl[:, t, :], start=True, stop=True)
            closed(mm(ps[:, 16:24], ones[:, :], gl[:, 0, :], start=True, stop=True), "gc")
            pairs = [(t, q) for t in range(TT) for q in range(2)]
            for t, q in pairs:
                name = f"gr_{t}_{q}"
                ps = opened(name)
                for n in range(GH):
                    last = mm(ps[:, P * n:P * n + P], gl[:, t, GH * q + n:GH * q + n + 1].to_broadcast([P, P]),
                              cst("upper"), start=True, stop=True)
                closed(last, name)
            Kt = dn["Kt"].rearrange("p (t h n) -> p t h n", t=TT, h=NH2)
            KnT = dn["KnT"].rearrange("p (h n) -> p h n", h=NH2)
            z_half(1)
            pe.wait_ge(sem("kn"), 4)
            for n in range(4):
                name = f"knT_{n}"
                ps = opened(name)
                for j in range(2):
                    for t in range(TT):
                        at = SEQ * j + P * t
                        last = nc.tensor.transpose(ps[:, at:at + P], Kt[:, t, 2 * n + j, :], ident)
                closed(last, name)
            for n in range(4):
                freed(pe, f"knT_{n}")
            for t, q in pairs:
                for what in ("qk", "kk", "br"):
                    name = f"{what}_{t}_{q}"
                    ps = opened(name)
                    for n in range(GH):
                        h = GH * q + n
                        c = slice(P * t, P * t + P)
                        if what == "br":
                            last = mm(ps[:, P * n:P * n + P], be[:, t, h:h + 1].to_broadcast([P, P]), ident,
                                      start=True, stop=True)
                        else:
                            rhs = cv[:, 2, h, c] if what == "qk" else KnT[:, h, c]
                            last = mm(ps[:, P * n:P * n + P], KnT[:, h, c], rhs, start=True, stop=True)
                    closed(last, name)
            Xi = dn["Xi"].rearrange("p (g n) -> p g n", g=4)
            Yi = dn["Yi"].rearrange("p (g n) -> p g n", g=4)
            M = dn["M"].rearrange("p (g n) -> p g n", g=4)
            LTk = dn["DT"].rearrange("p (g n) -> p g n", g=4)
            for g in range(4):
                name = f"x0_{g}"
                ps = opened(name)
                pe.wait_ge(sem("y_new"), g + 1)
                for n in range(GH):
                    last = nc.tensor.transpose(ps[:, P * n:P * n + P], Yi[:, g, P * n:P * n + P], ident)
                closed(last, name)
            for lv in range(1, LEVELS):
                for g in range(4):
                    name = f"m{lv}_{g}"
                    ps = opened(name)
                    if lv == 1:
                        freed(pe, f"x0_{g}")
                    else:
                        freed(pe, f"dx{lv - 1}_{g}")
                    pe.wait_ge(sem("lt_level"), 4 * (lv - 1) + g + 1)
                    for n in range(GH):
                        s = slice(P * n, P * n + P)
                        last = mm(ps[:, s], LTk[:, g, s], Xi[:, g, s], start=True, stop=True)
                    closed(last, name)
                for g in range(4):
                    freed(pe, f"m{lv}_{g}")
                    for what in (["dx", "dy"] if lv < LEVELS - 1 else ["dy"]):
                        name = f"{what}{lv}_{g}"
                        ps = opened(name)
                        if what == "dy" and lv > 1:
                            freed(pe, f"dy{lv - 1}_{g}")
                        if what == "dx" and lv > 1:
                            freed(pe, f"dy{lv - 1}_{g}")
                        for n in range(GH):
                            s = slice(P * n, P * n + P)
                            a, b = (Yi, M) if what == "dx" else (M, Yi)
                            last = mm(ps[:, s], a[:, g, s], b[:, g, s], start=True, stop=True)
                        closed(last, name)
            Y4 = dn["Yi"].rearrange("p (t h n) -> p t h n", t=TT, h=NH2)
            Vb = dn["Vb"].rearrange("p (t h n) -> p t h n", t=TT, h=NH2)
            QKD = dn["QKD"].rearrange("p (t h n) -> p t h n", t=TT, h=NH2)
            VN = cv[:, 0].rearrange("p h n -> p (h n)").rearrange("p (w h n) -> p w h n", w=2, h=NH2)
            S1 = dn["DT"][:, 0:1024].rearrange("p (h n) -> p h n", h=NH2)

            def heads_job(name, q, lhs, rhs):
                ps = opened(name)
                for n in range(GH):
                    h = GH * q + n
                    last = mm(ps[:, P * n:P * n + P], lhs(h), rhs(h), start=True, stop=True)
                closed(last, name)

            for t in range(TT):
                for q in range(2):
                    freed(pe, f"dy{LEVELS - 1}_{2 * t + q}")
                    if t == 1:
                        freed(pe, f"s1_{q}")
                        heads_job(f"ks_{q}", q, lambda h: KnT[:, h, P:SEQ], lambda h: S1[:, h, :])
                        pe.wait_ge(sem("vb1"), q + 1)
                    heads_job(f"vn_{t}_{q}", q, lambda h: Y4[:, t, h, :], lambda h: Vb[:, t, h, :])
                for q in range(2):
                    freed(pe, f"vn_{t}_{q}")
                    if t == 0:
                        pe.wait_ge(sem("vne"), q + 1)
                        heads_job(f"s1_{q}", q, lambda h: Kt[:, 0, h, :], lambda h: VN[:, 1, h, :])
                    heads_job(f"o_{t}_{q}", q, lambda h: QKD[:, t, h, :], lambda h: VN[:, 0, h, :])
                    if t == 1:
                        heads_job(f"os_{q}", q, lambda h: cv[:, 2, h, P:SEQ], lambda h: S1[:, h, :])
            for tag in ("gn", "gd"):
                for n in range(2):
                    two_tokens(f"{tag}{n}", f"{tag}{n}")
            Onsa = nsa["O"].rearrange("p (t n) -> p t n", t=TT)
            transposes_of(Onsa, lambda k: f"onT_{k}")
            two_tokens("pn0", "pn0", onT)
            pe.wait_ge(sem("dn_out"), 2)
            Od = dn["Xi"].rearrange("p (t n) -> p t n", t=TT)
            transposes_of(Od, lambda k: f"odT_{k}")
            two_tokens("pn1", "pn1", onT)
            for n in range(2):
                two_tokens(f"pd{n}", f"pd{n}", odT)
            mix = dn["Vb"].rearrange("p (t n) -> p t n", t=TT)
            pe.wait_ge(sem("mix"), 4)
            transposes_of(mix, lambda k: f"mixT_{k}")
            for n in range(2):
                two_tokens(f"out2_{n}", f"o2_{n}", mixT)
            norm_turn("norm4", 1, dn["Vb"].rearrange("p (t n) -> p t n", t=TT))
            turn[0], turn[1] = 0, 4
            for n in range(8):
                for j in (2 * n, 2 * n + 1):
                    name = f"up_{j}"
                    ps = opened(name)
                    done_with(f"up2.{2 * j}", feature_product(f"up2.{2 * j}", tok, ps[:, 0:SEQ]))
                    closed(feature_product(f"up2.{2 * j + 1}", tok, ps[:, SEQ:2 * SEQ]), name)
                    piece_used[f"up2.{2 * j + 1}"] = name
                if n >= 1:
                    down("down2", 4 * (n - 1), 4, "d2", FT2, a2, hidden2)
            down("down2", 28, 4, "d2", FT2, a2, hidden2)

        @block.sync
        def _(sp):
            for t in range(TT):
                sp.dma_start(X[:, t, :], x[P * t:P * t + P, :]).then_inc(sem(f"x{t}_in"), 16)
            sp.dma_start(one["Xm"][0:META, :], meta).then_inc(sem("meta_in"), 16)
            for name in ("x0_in", "x1_in", "meta_in"):
                sp.wait_ge(sem(name), 16)
            for i, name in enumerate(PIECES):
                if i >= RAW:
                    before = PIECES[i - RAW]
                    if before in WHOLE:
                        used_up(sp, before)
                    else:
                        sp.wait_ge(sem("split_pool" if before in BY_POOL else "split_vector"), TURN[before])
                w = WIDTHS[name]
                src = weights[STARTS[name]:STARTS[name] + P * w].rearrange("(p n) -> p n", p=P)
                sp.dma_start(raw[:, i % RAW, 0:w], src).then_inc(sem(f"piece_in{i % RAW}"), 16)
            for t in range(TT):
                for nh in range(2):
                    freed(sp, f"d2_{t}_{nh}")
                sp.dma_start(out[P * t:P * t + P, :], X[:, t, :]).then_inc(sem("stored"), 16)
            sp.wait_ge(sem("stored"), 16 * TT)

        @block.scalar
        def _(act):
            A = nc.scalar.activation
            act.dma_start(cbuf[:, :], consts[:, 0:NCHELD]).then_inc(sem("const_in"), 16)
            act.dma_start(att1["causal"], consts[:, NCHELD:NEARLY]).then_inc(sem("const_in"), 16)
            act.dma_start(att1["S"][:, 0:NLATE - NEARLY], consts[:, NEARLY:NLATE]).then_inc(sem("const_in"), 16)
            act.dma_start(pbuf[:, :], params[:, 0:NHELD]).then_inc(sem("const_in"), 16)
            act.dma_start(att1["final"], params[:, NHELD:NPARAM]).then_inc(sem("final_in"), 16)

            at = [0]

            def first_parts(n):
                for name in PIECES[at[0]:n]:
                    at[0] += 1
                    if name in WHOLE or name in BY_POOL:
                        continue
                    whole_piece = loaded(act, name)
                    slot_free(act, name)
                    signal(A(split_slot(name)[0], whole_piece, ACT.Copy), "first_parts")

            keep_ahead[act] = first_parts

            def square_sums(src, col, junk, rows=P):
                return A(junk, src, ACT.Square, accum_out=st[0:rows, col:col + 1])

            def turned_out(name_of, dst, width, gain=lambda k: None, parted=True):
                for k in range(KD):
                    name = name_of(k)
                    full(act, name)
                    g = gain(k)
                    src = bank_of(name)[:, 0:width]
                    out_ = dst[:, 0, k, 0:width] if parted else dst[:, k, 0:width]
                    ins = A(out_, src, ACT.Copy) if g is None else A(out_, src, ACT.Copy, scale=g)
                    if parted:
                        signal(ins, "turned_first")
                    else:
                        release(ins, name)

            def half_sums(tag, job, junk):
                for nh in range(2):
                    for t in range(TT):
                        freed(act, job(t, nh))
                        s_ = slice(512 * nh, 512 * nh + 512)
                        signal(square_sums(X[:, t, s_], 2 * nh + t, junk[:, t, s_]), tag)

            def second_tile(which, dst):
                act.wait_ge(sem("rms" + which), 1)
                signal(A(dst[:, 1, :], X[:, 1, :], ACT.Copy, scale=st[:, 5:6]), "norm" + which + "_act")

            def exponentials(g):
                S, E, PT, PTm = slabs(g)
                tag = "probs1" if g["kind"] in ("mla", "dif", "swa") else "probs2"
                act.wait_ge(sem("peak" + tag[-1]), g["i"] + 1)
                for n in range(len(g["maps"])):
                    col = g["first"] + n
                    signal(A(map_slot(g, E, n), map_slot(g, S, n), ACT.Exp, bias=npeaks[:, col:col + 1],
                             accum_out=sums[:, col:col + 1]), tag)
                if g["kind"] == "swa":
                    c0, c1 = g["first"], g["last"]
                    act.wait_ge(sem("sink_in"), g["swas"])
                    signal(A(difsum[:, c0:c1], difsum[:, c0:c1], ACT.Exp), "sink_exp")

            def probs_out(g):
                S, E, PT, PTm = slabs(g)
                G = G1 if g["kind"] in ("mla", "dif", "swa") else G2
                nm = len(g["hs"])
                if g["i"] >= 2:
                    full(act, "pv_" + G[g["i"] - 2]["name"])
                if g["meta"]:
                    name = f"tm_{g['name']}"
                    full(act, name)
                    release(A(PTm[0:g["meta"], 0:P * nm], bank_of(name)[0:g["meta"], 0:P * nm], ACT.Copy), name)
                if g["tiles"]:
                    per = 512 // (P * g["tiles"])
                    flat = PT.rearrange("p m n -> p (m n)")
                    for j in range((nm + per - 1) // per):
                        w = P * g["tiles"] * min(per, nm - per * j)
                        name = f"tt_{g['name']}_{j}"
                        full(act, name)
                        release(A(flat[:, 512 * j:512 * j + w], bank_of(name)[:, 0:w], ACT.Copy), name)

            def attention(G, between):
                exponentials(G[0])
                for i, g in enumerate(G):
                    if i + 1 < len(G):
                        exponentials(G[i + 1])
                    probs_out(g)
                    for step in between.get(i, ()):
                        step()

            jn = one["Xn"].rearrange("p (t n) -> p t n", t=TT)
            for t in range(TT):
                act.wait_ge(sem(f"x{t}_in"), 16)
                signal(square_sums(X[:, t, :], t, jn[:, t, :]), "sq1")
            act.wait_ge(sem("meta_in"), 16)
            act.wait_ge(sem("meta_column"), 1)
            signal(square_sums(one["Xm"][0:META, :], 2, one["Xnm"][0:META, :], META), "sq1")
            first_parts(1)
            second_tile("1", jn)
            act.wait_ge(sem("const_in"), 64)
            act.wait_ge(sem("lamsum"), 2)
            signal(A(st[:, 12:14], st[:, 10:12], ACT.Exp), "lamexp")
            turned_out(lambda k: f"h1_{k}", hT, ALL, lambda k: par("attn_norm")[:, k:k + 1])
            for v in range(2):
                full(act, f"line{v}")
                release(A(att1["PTm"][0:BH, LINE * v:LINE * v + LINE], bank_of(f"line{v}")[0:BH, 0:LINE], ACT.Copy), f"line{v}")
            for v in range(2):
                freed(act, f"line{v}")
            act.dma_start(line_dram.rearrange("q h n -> h q n"),
                          att1["PTm"][0:BH, 0:2 * LINE].unsqueeze(1).to_broadcast([BH, P, 2 * LINE])).then_inc(sem("lines_out"), 16)
            cT = one["cT"].rearrange("p (c n) -> p c n", c=3)
            sqT = one["sqT"].rearrange("p (c n) -> p c n", c=3)
            for c, what in enumerate(["cq0", "cq1", "ckv"]):
                name = "p1_" + what
                full(act, name)
                signal(A(sqT[:, c, :], bank_of(name)[:, 0:ALL], ACT.Square), "lat_sq")
                release(A(cT[:, c, :], bank_of(name)[:, 0:ALL], ACT.Copy), name)
            dq = one["dqT"].rearrange("p (c n) -> p c n", c=2)
            dk = one["dkT"].rearrange("p (c n) -> p c n", c=2)
            sQ = one["sQT"].rearrange("p (c n) -> p c n", c=3)
            for c in range(2):
                full(act, f"p1_dq{c}")
                release(A(dq[:, c, :], bank_of(f"p1_dq{c}")[:, 0:SEQ], ACT.Copy, scale=DQK ** -0.5), f"p1_dq{c}")
            rs = one["rs"].rearrange("p (c n) -> p c n", c=3)
            act.wait_ge(sem("lat_ms"), 1)
            signal(A(rs[:, 1:3, :], rs[:, 1:3, :], ACT.Ln), "lat_ln")
            act.wait_ge(sem("lat_ln"), 1)
            signal(A(rs[:, 1:3, :], rs[:, 1:3, :], ACT.Exp, scale=-0.5), "lat_guess")
            for c in range(2):
                full(act, f"p1_dk{c}")
                release(A(dk[:, c, :], bank_of(f"p1_dk{c}")[:, 0:ALL], ACT.Copy), f"p1_dk{c}")
            for c in range(3):
                full(act, f"p1_sq{c}")
                release(A(sQ[:, c, :], bank_of(f"p1_sq{c}")[:, 0:SEQ], ACT.Copy, scale=SD ** -0.5), f"p1_sq{c}")
            full(act, "p1_sk")
            release(A(one["sKT"], bank_of("p1_sk")[:, 0:ALL], ACT.Copy), "p1_sk")
            V = one["V"].rearrange("p (t n) -> p t n", t=3)
            for t, rows in (("m", META), (0, P), (1, P)):
                full(act, f"vt_{t}")
                ti = 0 if t == "m" else t + 1
                release(A(V[0:rows, ti, 384:768], bank_of(f"vt_{t}")[0:rows, 0:384], ACT.Copy), f"vt_{t}")
            kT = one["kT"].rearrange("p (h n) -> p h n", h=MH)
            qT = one["qT"].rearrange("p (h n) -> p h n", h=MH)
            for h in range(MH):
                full(act, f"mq_{h}")
                signal(A(qT[0:64, h, :], bank_of(f"mq_{h}")[0:64, 0:SEQ], ACT.Copy), "q_nope")
                full(act, f"mk_{h}")
                release(A(kT[0:64, h, :], bank_of(f"mk_{h}")[0:64, 0:ALL], ACT.Copy), f"mk_{h}")
            for t, rows in ((-1, META), (0, P), (1, P)):
                full(act, f"mv_{t}")
                release(A(V[0:rows, t + 1, 0:384], bank_of(f"mv_{t}")[0:rows, 0:384], ACT.Copy), f"mv_{t}")
            attention(G1, {})
            act.wait_ge(sem("y1"), 2)
            freed(act, "pv_" + G1[-1]["name"])
            turned_out(lambda k: f"yT1_{k}", yT, SEQ,
                       lambda k: st[:, 20:21] if k in (3, 4) else None)
            half_sums("sq2", lambda t, nh: f"o1_{nh}_{t}", ffn1["Xn"].rearrange("p (t n) -> p t n", t=TT))
            second_tile("2", ffn1["Xn"].rearrange("p (t n) -> p t n", t=TT))
            turned_out(lambda k: f"norm2_{k}", hT, SEQ, lambda k: par("ffn_norm")[:, k:k + 1])
            sg = ffn1["sg"].rearrange("p (s n) -> p s n", s=4)
            v1 = ffn1["v"].rearrange("p (s n) -> p s n", s=4)
            for f in range(FT1):
                full(act, f"gu_{f}")
                if f >= 4:
                    freed(act, f"gu_{f - 4}")
                signal(A(sg[:, f % 4, :], bank_of(f"gu_{f}")[:, 0:SEQ], ACT.Silu), "silu1")
                freed(act, f"gu_{f}")
                signal(A(aT[:, 0, f, :], v1[:, f % 4, :], ACT.Copy), "hidden1_first")
            for t in range(TT):
                for nh in range(2):
                    freed(act, f"d1_{t}_{nh}")
                signal(square_sums(X[:, t, :], t, junk3[0][:, t, :]), "sq3")
            for t in range(TT):
                act.wait_ge(sem("gained"), t + 1)
                signal(square_sums(two["Xn"].rearrange("p (t n) -> p t n", t=TT)[:, t, :], 2 + t, junk3[1][:, t, :]), "sq3")
            act.wait_ge(sem("rms3"), 1)
            Xn = two["Xn"].rearrange("p (t n) -> p t n", t=TT)
            signal(A(Xn[:, 1, :], Xn[:, 1, :], ACT.Copy, scale=st[:, 7:8]), "norm3_act")
            turned_out(lambda k: f"norm3_{k}", hT, SEQ, lambda k: par("norm_mix")[:, k:k + 1])
            first_parts(job_piece["small_1"] + AHEAD)
            act.wait_ge(sem("small_in"), 1)
            signal(A(sig[:, :], sig[:, :], ACT.Exp, scale=-1.0), "small_exp")
            signal(A(soft[:, 16:32], soft[:, 16:32], ACT.Exp, scale=-1.0), "small_exp")
            signal(A(soft[:, 48:56], par("a_log"), ACT.Exp), "small_exp")
            act.wait_ge(sem("small_exp"), 3)
            signal(A(soft[:, 16:32], soft[:, 16:32], ACT.Ln, bias=1.0), "small_ln")
            act.wait_ge(sem("x2"), 2)
            Q = nsa["Q"].rearrange("p (t n) -> p t n", t=TT)
            ksw = nsa["ksw"].rearrange("p (t n) -> p t n", t=TT)
            VV = nsa["VV"].rearrange("p (t n) -> p t n", t=TT)
            cv = dnp["cv"].rearrange("p (w h n) -> p w h n", w=3, h=NH2)

            def silu_conv(w, first, half):
                first_parts(job_piece[f"cv_{'kvq'[w]}{first // 2 + half}"] + AHEAD)
                for n in range(2):
                    h = first + 2 * half + n
                    done = 8 * w + h + 1
                    act.wait_ge(sem("conv_raw"), done)
                    signal(A(cv[:, w, h, :], cv[:, w, h, :], ACT.Silu), "conv_done")

            def z_out(n):
                Z = dnp["Z"].rearrange("p (t n) -> p t n", t=TT)
                for t in range(TT):
                    name = f"z{n}_{t}"
                    full(act, name)
                    release(A(Z[:, t, 512 * n:512 * n + 512], bank_of(name), ACT.Silu), name)

            for n in range(2):
                for t in range(TT):
                    name = f"nq{n}_{t}"
                    full(act, name)
                    signal(A(nsa["O"][:, D * t + 512 * n:D * t + 512 * n + 512], bank_of(name), ACT.Square), "q_squares")
                    release(A(Q[:, t, 512 * n:512 * n + 512], bank_of(name), ACT.Copy), name)
            for t in range(TT):
                full(act, f"nk_{t}")
                signal(A(nsa["Z"][:, 1024 + 512 * t:1536 + 512 * t], bank_of(f"nk_{t}"), ACT.Square), "k_squares")
                release(A(ksw[:, t, :], bank_of(f"nk_{t}"), ACT.Copy), f"nk_{t}")
            full(act, "hid")
            hid_in = bank_of("hid")[:, 0:128].rearrange("p (s n) -> p s n", s=2)[:, :, 0:60]
            release(A(hid[:, :, :], hid_in, ACT.Gelu_apprx_tanh), "hid")
            for t in range(TT):
                full(act, f"nv_{t}")
                release(A(VV[:, t, :], bank_of(f"nv_{t}"), ACT.Copy), f"nv_{t}")
            turned_out(lambda k: f"nqT_{k}", nsa["qT"].rearrange("p (k n) -> p k n", k=KD), SEQ, lambda k: par("nsa_q"),
                       parted=False)
            full(act, "kcT")
            release(A(kcT[:, :, 0:NC],
                      bank_of("kcT")[:, 0:32].rearrange("p (s n) -> p s n", s=2)[:, :, 0:NC], ACT.Copy, scale=par("k_cmp")), "kcT")
            KT = nsa["KT"].rearrange("p (h n) -> p h n", h=4)
            for b in range(2):
                full(act, f"nkT_{b}")
                release(A(KT[:, 2 * b:2 * b + 2, :], bank_of(f"nkT_{b}"), ACT.Copy, scale=par("k_slc" if b == 0 else "k_win")),
                        f"nkT_{b}")
            for half in range(4):
                silu_conv(0, 4 * (half // 2), half % 2)
            for what in EARLY:
                silu_conv(*what[1:])
            extra = {i + 1: [lambda w=what: silu_conv(*w[1:])] for i, what in zip(FILL, FILLERS)}
            attention(G2, extra)
            full(act, "pv_" + G2[-1]["name"])
            act.dma_start(dn["level"], consts[:, NLATE:NCONST]).then_inc(sem("level_in"), 16)
            for t in range(TT):
                for q in range(2):
                    name = f"kt_{t}_{q}"
                    full(act, name)
                    sqb = dn["LT"].rearrange("p (g n) -> p g n", g=4)[:, 2 * t + q, :]
                    signal(A(sqb, bank_of(name), ACT.Square), "key_squares")
            z_out(0)
            for t in range(TT):
                for q in range(2):
                    name = f"qt2_{t}_{q}"
                    full(act, name)
                    sqb = dn["M"].rearrange("p (g n) -> p g n", g=4)[:, 2 * t + q, :]
                    release(A(sqb, bank_of(name), ACT.Square), name)
            E4 = dn["DT"].rearrange("p (g n) -> p g n", g=4)
            full(act, "gc")
            act.wait_ge(sem("gc_out"), 1)
            signal(A(gcb[:, 32:40], gcb[:, 8:16], ACT.Exp), "gc_exp")
            signal(A(gcb[:, 40:48], gcb[:, 24:32], ACT.Exp), "gc_exp")
            for g in range(4):
                freed(act, f"gr_{g // 2}_{g % 2}")
                signal(A(E4[:, g, :], E4[:, g, :], ACT.Exp), "dec_exp")
            z_out(1)
            KnT = dn["KnT"].rearrange("p (h n) -> p h n", h=NH2)
            for n in range(4):
                full(act, f"knT_{n}")
                release(A(KnT[:, 2 * n:2 * n + 2, :], bank_of(f"knT_{n}"), ACT.Copy), f"knT_{n}")
            Xi = dn["Xi"].rearrange("p (g n) -> p g n", g=4)
            M = dn["M"].rearrange("p (g n) -> p g n", g=4)
            for g in range(4):
                full(act, f"x0_{g}")
                release(A(Xi[:, g, :], bank_of(f"x0_{g}"), ACT.Copy), f"x0_{g}")
            for lv in range(1, LEVELS):
                for g in range(4):
                    name = f"m{lv}_{g}"
                    full(act, name)
                    if lv > 1:
                        full(act, f"dy{lv - 1}_{g}")
                    release(A(M[:, g, :], bank_of(name), ACT.Copy), name)
            VN = cv[:, 0].rearrange("p h n -> p (h n)").rearrange("p (w h n) -> p w h n", w=2, h=NH2)
            S1 = dn["DT"][:, 0:1024].rearrange("p (h n) -> p h n", h=NH2)
            for q in range(2):
                full(act, f"vn_0_{q}")
                release(A(VN[:, 0, GH * q:GH * q + GH, :], bank_of(f"vn_0_{q}"), ACT.Copy), f"vn_0_{q}")
            for q in range(2):
                full(act, f"s1_{q}")
                ins = A(S1[:, GH * q:GH * q + GH, :], bank_of(f"s1_{q}"), ACT.Copy)
                release(ins, f"s1_{q}")
            for q in range(2):
                full(act, f"vn_1_{q}")
                full(act, f"o_0_{q}")
                release(A(VN[:, 0, GH * q:GH * q + GH, :], bank_of(f"vn_1_{q}"), ACT.Copy), f"vn_1_{q}")
            sgs = nsa["cv"][:, 4096:6144].rearrange("p (t n) -> p t n", t=TT)
            for n in range(2):
                for t in range(TT):
                    name = f"gn{n}_{t}"
                    full(act, name)
                    if n == 0 and t == 0:
                        full(act, "os_1")
                    release(A(sgs[:, t, 512 * n:512 * n + 512], bank_of(name), ACT.Sigmoid), name)
            sgd = dn["QKD"].rearrange("p (t n) -> p t n", t=TT)
            for n in range(2):
                for t in range(TT):
                    name = f"gd{n}_{t}"
                    full(act, name)
                    release(A(sgd[:, t, 512 * n:512 * n + 512], bank_of(name), ACT.Sigmoid), name)
            turned_out(lambda k: f"onT_{k}", onT, SEQ)
            turned_out(lambda k: f"odT_{k}", odT, SEQ, lambda k: par("dn_out"))
            turned_out(lambda k: f"mixT_{k}", mixT, SEQ)
            half_sums("sq4", lambda t, nh: f"o2_{nh}_{t}", dn["Vb"].rearrange("p (t n) -> p t n", t=TT))
            second_tile("4", dn["Vb"].rearrange("p (t n) -> p t n", t=TT))
            turned_out(lambda k: f"norm4_{k}", hT, SEQ, lambda k: par("norm_mlp")[:, k:k + 1])
            for j in range(FT2 // 2):
                name = f"up_{j}"
                full(act, name)
                if j >= 4:
                    act.wait_ge(sem("hidden2"), j - 3)
                release(A(relu2[:, j % 4, :], bank_of(name), ACT.Relu), name)
                freed(act, name)
                signal(A(a2[:, 0, 2 * j:2 * j + 2, :], relu2[:, j % 4, :], ACT.Square), "hidden2_first")
            first_parts(len(PIECES))

        @block.gpsimd
        def _(pool):
            nc.gpsimd.memset(ones[:, :], 1.0).then_inc(sem("ones"), 1)
            pool.wait_ge(sem("lines_out"), 16)

            def shifted(head0, heads, v, m0, n):
                return bass.AP(tensor=line_dram.tensor, offset=head0 * 2 * LINE + v * LINE + m0 + P - 1,
                               ap=[[BH * 2 * LINE - 1, P], [2 * LINE, heads], [1, n]])

            sz0 = one["sz0"].rearrange("p (h n) -> p h n", h=SH)
            sz1 = one["sz1"].rearrange("p (h n) -> p h n", h=SH)
            pool.dma_start(one["dz"].rearrange("p (h n) -> p h n", h=DH), shifted(0, DH, 0, 0, ALL)).then_inc(sem("bias_in"), 16)
            pool.dma_start(sz0[:, :, 0:META], shifted(DH, SH, 0, P, META)).then_inc(sem("bias_in"), 16)
            pool.dma_start(sz0[:, :, META:144], shifted(DH, SH, 1, P + META, P)).then_inc(sem("bias_in"), 16)
            pool.dma_start(sz1[:, :, 0:META], shifted(DH, SH, 0, 0, META)).then_inc(sem("bias_in"), 16)
            pool.dma_start(sz1[:, :, META:ALL], shifted(DH, SH, 1, META, SEQ)).then_inc(sem("bias_in"), 16)
            pool.wait_ge(sem("x2"), 2)
            al = nsa["alibi"].rearrange("p (h n) -> p h n", h=NSH)
            for h in range(NSH):
                slope = float(np.float32(2.0 ** (-8.0 * (h + 1) / NSH)))
                nc.gpsimd.tensor_scalar(al[:, h, :], cst("negdist"), slope, None, ALU.mult).then_inc(sem("alibi"), 1)
            for name in PARTED:
                if name in BY_POOL:
                    whole_piece = loaded(pool, name)
                    slot_free(pool, name)
                    first, second = split_slot(name)
                    nc.gpsimd.tensor_copy(first, whole_piece).then_inc(sem("pool_first"), 1)
                    pool.wait_ge(sem("pool_first"), TURN[name])
                    nc.gpsimd.tensor_tensor(second, whole_piece, first.bitcast(F32), ALU.subtract)\
                        .then_inc(sem("split_pool"), 1)
            E4 = dn["DT"].rearrange("p (g n) -> p g n", g=4)
            for g in range(4):
                pool.wait_ge(sem("dec_exp"), g + 1)
                v = E4[:, g, :].rearrange("p (n i) -> p n i", n=GH)
                nc.gpsimd.tensor_tensor(v, v, cst("upper").unsqueeze(1).to_broadcast([P, GH, P]), ALU.mult)\
                    .then_inc(sem("dec_masked"), 1)
            pool.wait_ge(sem("level_in"), 16)
            lev = cst("level").rearrange("p (l n) -> p l n", l=LEVELS)
            LT = dn["LT"].rearrange("p (g n) -> p g n", g=4)
            LTk = dn["DT"].rearrange("p (g n) -> p g n", g=4)
            for lv in range(1, LEVELS):
                for g in range(4):
                    if lv == 1:
                        pool.wait_ge(sem("y_new"), 4)
                    else:
                        full(pool, f"m{lv - 1}_{g}")
                    nc.gpsimd.tensor_tensor(
                        LTk[:, g, :].rearrange("p (n i) -> p n i", n=GH), LT[:, g, :].rearrange("p (n i) -> p n i", n=GH),
                        lev[:, lv, :].unsqueeze(1).to_broadcast([P, GH, P]), ALU.mult).then_inc(sem("lt_level"), 1)
            for j in range(FT2 // 2):
                v = relu2[:, j % 4, :]
                pool.wait_ge(sem("hidden2_first"), j + 1)
                nc.gpsimd.tensor_tensor(v, v, v, ALU.mult).then_inc(sem("squares2"), 1)
                pool.wait_ge(sem("squares2"), j + 1)
                nc.gpsimd.tensor_tensor(a2[:, 1, 2 * j:2 * j + 2, :], v, a2[:, 0, 2 * j:2 * j + 2, :].bitcast(F32), ALU.subtract)\
                    .then_inc(sem("hidden2"), 1)

        @block.vector
        def _(dve):
            V_ = nc.vector

            def link(ins):
                n = signal(ins, "vector_step")
                dve.wait_ge(sem("vector_step"), n)

            def step(ins):
                signal(ins, "vector_step")

            def settle():
                dve.wait_ge(sem("vector_step"), counts["vector_step"])

            at = [0]

            def second_parts(n):
                for name in PIECES[at[0]:n]:
                    at[0] += 1
                    if name in WHOLE or name in BY_POOL:
                        continue
                    first, second = split_slot(name)
                    dve.wait_ge(sem("first_parts"), TURN[name])
                    whole_piece = loaded(dve, name)
                    signal(V_.tensor_tensor(second, whole_piece, first.bitcast(F32), ALU.subtract), "split_vector")

            keep_ahead[dve] = second_parts

            def turned_rest(name_of, dst, width, gain=lambda k: None):
                for k in range(KD):
                    name = name_of(k)
                    full(dve, name)
                    turned[0] += 1
                    dve.wait_ge(sem("turned_first"), turned[0])
                    first, second = dst[:, 0, k, 0:width].bitcast(F32), dst[:, 1, k, 0:width]
                    src = bank_of(name)[:, 0:width]
                    g = gain(k)
                    if g is None:
                        release(V_.tensor_tensor(second, src, first, ALU.subtract), name)
                    else:
                        release(V_.scalar_tensor_tensor(out=second, in0=src, scalar=g, in1=first,
                                                        op0=ALU.mult, op1=ALU.subtract), name)

            turned = [0]

            def inv_sqrt(y, v, a, b, tag=None):
                step(V_.tensor_scalar(y.bitcast(I32), v.bitcast(I32), -0.5, 1597463007.0, ALU.mult, ALU.add))
                link(V_.tensor_scalar(b, v, -0.5, None, ALU.mult))
                for _n in range(3):
                    newton(y, a, b, tag if _n == 2 else None)

            def newton(y, a, b, tag=None):
                link(V_.tensor_tensor(a, y, y, ALU.mult))
                link(V_.tensor_tensor(a, a, b, ALU.mult))
                last = V_.scalar_tensor_tensor(out=y, in0=a, scalar=1.5, in1=y, op0=ALU.add, op1=ALU.mult)
                if tag is None:
                    link(last)
                else:
                    dve.wait_ge(sem(tag), signal(last, tag))

            def inv_rms(dst, ssum, n, a, b, tag=None):
                link(V_.tensor_scalar(ssum, ssum, 1.0 / n, EPS, ALU.mult, ALU.add))
                inv_sqrt(dst, ssum, a, b, tag)

            def bc(ap, shape):
                return ap.unsqueeze(2).to_broadcast(shape)

            def norm_rows(tag, dst, sq_tag):
                dve.wait_ge(sem(sq_tag), 2 * TT)
                link(V_.tensor_tensor(st[:, 0:2], st[:, 0:2], st[:, 2:4], ALU.add))
                inv_rms(st[:, 4:6], st[:, 0:2], D, st[:, 6:8], st[:, 8:10], "rms" + tag[-1])
                signal(V_.tensor_scalar(dst[:, 0, :], X[:, 0, :], st[:, 4:5], None, ALU.mult), tag)

            def residual(names_, last=False):
                for t, nh, name in names_:
                    full(dve, name)
                    xs = X[:, t, 512 * nh:512 * nh + 512]
                    release(V_.tensor_tensor(xs, bank_of(name), xs, ALU.add), name)
                if not last:
                    for t, nh, name in names_:
                        freed(dve, name)

            def peaks_of(g):
                S, E, PT, PTm = slabs(g)
                tag = "1" if g["kind"] in ("mla", "dif", "swa") else "2"
                G = G1 if tag == "1" else G2
                if g["i"] >= 2:
                    full(dve, last_turn(G[g["i"] - 2]))
                for n, (h, c) in enumerate(g["maps"]):
                    name = f"qk_{g['name']}_{n // g['per']}"
                    col = g["first"] + n
                    at = g["keys"] * (n % g["per"])
                    if n % g["per"] == 0:
                        full(dve, name)
                    ins = V_.tensor_tensor_reduce(out=map_slot(g, S, n), in0=bank_of(name)[:, at:at + g["keys"]],
                                                  in1=map_bias(g, h), scale=1.0, scalar=-3e38, op0=ALU.add, op1=ALU.max,
                                                  accum_out=peaks[:, col:col + 1])
                    if n % g["per"] == g["per"] - 1 or n == len(g["maps"]) - 1:
                        release(ins, name)
                    else:
                        step(ins)
                for n in range(0, len(g["maps"]), g["per"]):
                    freed(dve, f"qk_{g['name']}_{n // g['per']}")
                if g["per"] > 1:
                    settle()
                c0, c1, h0 = g["first"], g["last"], g["hs"][0]
                if g["kind"] == "swa":
                    sinks = par("sinks")[:, h0:h0 + c1 - c0]
                    signal(V_.scalar_tensor_tensor(out=npeaks[:, c0:c1], in0=peaks[:, c0:c1], scalar=-1.0,
                                                   in1=nsinks[:, h0:h0 + c1 - c0], op0=ALU.mult, op1=ALU.min), "peak" + tag)
                    dve.wait_ge(sem("peak1"), g["i"] + 1)
                    signal(V_.tensor_tensor(difsum[:, c0:c1], npeaks[:, c0:c1], sinks, ALU.add), "sink_in")
                else:
                    signal(V_.tensor_scalar(npeaks[:, c0:c1], peaks[:, c0:c1], -1.0, None, ALU.mult), "peak" + tag)

            def finish_one(g):
                y = att1["y"].rearrange("p (t n) -> p t n", t=TT)
                nm = len(g["hs"])
                c0 = g["first"]
                name = f"pv_{g['name']}"
                off = {"mla": 0, "dif": 384, "swa": 640}[g["kind"]] + 64 * g["hs"][0]
                yo = y[:, g["qt"], off:off + 64 * nm]
                if g["kind"] == "dif":
                    full(dve, name)
                    release(V_.tensor_copy(yo, bank_of(name)[:, 0:64 * nm]), name)
                    return
                dve.wait_ge(sem("probs1"), g["last"])
                link(V_.reciprocal(st[:, 24:24 + nm], sums[:, c0:c0 + nm]))
                full(dve, name)
                release(V_.tensor_tensor(yo.rearrange("p (h d) -> p h d", h=nm),
                                         bank_of(name)[:, 0:64 * nm].rearrange("p (h d) -> p h d", h=nm),
                                         bc(st[:, 24:24 + nm], [P, nm, 64]), ALU.mult), name)

            def sinks_in(g):
                c0, c1 = g["first"], g["last"]
                dve.wait_ge(sem("sink_exp"), g["swas"])
                link(V_.tensor_tensor(sums[:, c0:c1], sums[:, c0:c1], difsum[:, c0:c1], ALU.add))

            def difference(g):
                S, E, PT, PTm = slabs(g)
                c0 = g["first"]
                dve.wait_ge(sem("probs1"), g["last"])
                link(V_.reciprocal(difsum[:, c0:c0 + 4], sums[:, c0:c0 + 4]))
                v = difsum[:, c0:c0 + 4].rearrange("p (h c) -> p h c", c=2)[:, :, 1:2]
                link(V_.tensor_scalar(v, v, st[:, 16:17], None, ALU.mult))
                kk = g["keys"]
                for n in range(2):
                    a, b = map_slot(g, E, 2 * n), map_slot(g, E, 2 * n + 1)
                    link(V_.tensor_scalar(a, a, difsum[:, c0 + 2 * n:c0 + 2 * n + 1], None, ALU.mult))
                    ins = V_.scalar_tensor_tensor(out=a, in0=b, scalar=difsum[:, c0 + 2 * n + 1:c0 + 2 * n + 2], in1=a,
                                                  op0=ALU.mult, op1=ALU.add)
                    if n == 0:
                        step(ins)
                    else:
                        signal(ins, "differences")

            signal(V_.memset(st[:, 2:3], 1.0), "meta_column")
            dve.wait_ge(sem("sq1"), 3)
            inv_rms(st[:, 4:7], st[:, 0:3], D, st[:, 24:27], st[:, 27:30], "rms1")
            Xn = one["Xn"].rearrange("p (t n) -> p t n", t=TT)
            signal(V_.tensor_scalar(Xn[:, 0, :], X[:, 0, :], st[:, 4:5], None, ALU.mult), "norm1")
            signal(V_.tensor_scalar(one["Xnm"][0:META, :], one["Xm"][0:META, :], st[0:META, 6:7], None, ALU.mult), "norm1")
            dve.wait_ge(sem("const_in"), 64)
            a = PARAM["rel"][0]
            signal(V_.memset(pbuf[32:33, a:a + BH], NEG), "relneg")
            lam = par("lam").rearrange("p (r n) -> p r n", r=4)
            for n in range(2):
                ins = V_.tensor_tensor_reduce(out=scr[:, 32 * n:32 * n + DQK], in0=lam[:, 2 * n, :], in1=lam[:, 2 * n + 1, :],
                                              scale=1.0, scalar=0.0, op0=ALU.mult, op1=ALU.add,
                                              accum_out=st[:, 10 + n:11 + n])
                signal(ins, "lamsum")
            dve.wait_ge(sem("lamexp"), 1)
            link(V_.tensor_tensor(st[:, 15:16], st[:, 13:14], st[:, 12:13], ALU.subtract))
            link(V_.tensor_scalar(st[:, 16:17], st[:, 15:16], -LAM0, None, ALU.add))
            link(V_.tensor_scalar(st[:, 20:21], par("subln"), 1.0 - LAM0, None, ALU.mult))
            link(V_.tensor_scalar(nsinks[:, 0:SH], par("sinks"), -1.0, None, ALU.mult))
            turned_rest(lambda k: f"h1_{k}", hT, ALL, lambda k: par("attn_norm")[:, k:k + 1])
            rot = one["rot"].rearrange("p (a n) -> p a n", a=4)
            kT = one["kT"].rearrange("p (h n) -> p h n", h=MH)
            qT = one["qT"].rearrange("p (h n) -> p h n", h=MH)
            cos, sin = cst("cos")[64:96, :], cst("sin")[64:96, :]
            rs = one["rs"].rearrange("p (c n) -> p c n", c=3)
            cT = one["cT"].rearrange("p (c n) -> p c n", c=3)
            sqT = one["sqT"].rearrange("p (c n) -> p c n", c=3)
            cn = one["cnT"].rearrange("p (c n) -> p c n", c=3)
            for c, (name, n) in enumerate((("lat_q", MQR), ("lat_kv", MKR))):
                full(dve, name)
                release(V_.tensor_scalar(rs[:, 1 + c, :], bank_of(name)[:, 0:ALL], 1.0 / n, EPS, ALU.mult, ALU.add), name)
            freed(dve, "lat_q")
            freed(dve, "lat_kv")
            signal(V_.tensor_scalar(sqT[:, 0:2, :], rs[:, 1:3, :], -0.5, None, ALU.mult), "lat_ms")
            dve.wait_ge(sem("lat_guess"), 1)
            newton(rs[:, 1:3, :], cn[:, 0:2, :], sqT[:, 0:2, :])
            link(V_.tensor_scalar(rs[:, 1, :], rs[:, 1, :], (NOPE + ROPE) ** -0.5, None, ALU.mult))
            for c in range(3):
                g = par("q_norm")[:, c:c + 1] if c < 2 else par("kv_norm")
                signal(V_.scalar_tensor_tensor(out=cn[:, c, :], in0=cT[:, c, :], scalar=g, in1=rs[:, 1 + c // 2, :],
                                               op0=ALU.mult, op1=ALU.mult), "lat_norm")
            full(dve, "p1_krA")
            release(V_.tensor_tensor(rot[64:96, 0, :], bank_of("p1_krA")[64:96, 0:ALL], cos, ALU.mult), "p1_krA")
            full(dve, "p1_krB")
            release(V_.tensor_tensor(rot[64:96, 1, :], bank_of("p1_krB")[64:96, 0:ALL], sin, ALU.mult), "p1_krB")
            freed(dve, "p1_krA")
            freed(dve, "p1_krB")
            link(V_.tensor_tensor(rot[64:96, 0, :], rot[64:96, 0, :], rot[64:96, 1, :], ALU.add))
            signal(V_.tensor_copy(kT[64:96, :, :], rot[64:96, 0, :].unsqueeze(1).to_broadcast([32, MH, ALL])), "krot")
            for h in range(MH):
                full(dve, f"mq_{h}")
                b_ = bank_of(f"mq_{h}")
                step(V_.tensor_tensor(rot[64:96, 2, 0:SEQ], b_[64:96, 0:SEQ], cos[:, META:ALL], ALU.mult))
                link(V_.tensor_tensor(rot[64:96, 3, 0:SEQ], b_[64:96, SEQ:2 * SEQ], sin[:, META:ALL], ALU.mult))
                dve.wait_ge(sem("q_nope"), h + 1)
                release(V_.tensor_tensor(qT[64:96, h, :], rot[64:96, 2, 0:SEQ], rot[64:96, 3, 0:SEQ], ALU.add), f"mq_{h}")
                freed(dve, f"mq_{h}")
            dve.wait_ge(sem("bias_in"), 80)

            def sublayer_norm(t):
                for h in (0, 2):
                    freed(dve, f"pv_dif{t}_{h}")
                yd = att1["y"].rearrange("p (t n) -> p t n", t=TT)[:, t, 384:640].rearrange("p (h d) -> p h d", d=DV)
                sq = scr[:, 256 * t:256 * t + 256].rearrange("p (h d) -> p h d", d=DV)
                link(V_.tensor_tensor(sq, yd, yd, ALU.mult))
                link(V_.tensor_reduce(st[:, 32:36], sq, AXX, ALU.add))
                inv_rms(st[:, 40:44], st[:, 32:36], DV, st[:, 48:52], st[:, 56:60])
                signal(V_.tensor_tensor(yd, yd, bc(st[:, 40:44], [P, DH, DV]), ALU.mult), "y1")

            peaks_of(G1[0])
            for i, g in enumerate(G1):
                if i + 1 < len(G1):
                    peaks_of(G1[i + 1])
                if g["kind"] == "dif":
                    difference(g)
                if i >= 1:
                    if G1[i - 1]["kind"] == "swa":
                        sinks_in(G1[i - 1])
                    finish_one(G1[i - 1])
                if g["kind"] == "swa" and g["hs"][0] == 0:
                    sublayer_norm(g["qt"])
            sinks_in(G1[-1])
            finish_one(G1[-1])
            turned_rest(lambda k: f"yT1_{k}", yT, SEQ, lambda k: st[:, 20:21] if k in (3, 4) else None)
            residual([(t, nh, f"o1_{nh}_{t}") for nh in range(2) for t in range(TT)])
            norm_rows("norm2", ffn1["Xn"].rearrange("p (t n) -> p t n", t=TT), "sq2")
            turned_rest(lambda k: f"norm2_{k}", hT, SEQ, lambda k: par("ffn_norm")[:, k:k + 1])
            sg = ffn1["sg"].rearrange("p (s n) -> p s n", s=4)
            v1 = ffn1["v"].rearrange("p (s n) -> p s n", s=4)

            def hidden_rest(f):
                dve.wait_ge(sem("hidden1_first"), f + 1)
                signal(V_.tensor_tensor(aT[:, 1, f, :], v1[:, f % 4, :], aT[:, 0, f, :].bitcast(F32), ALU.subtract), "hidden1")

            for f in range(FT1):
                full(dve, f"gu_{f}")
                dve.wait_ge(sem("silu1"), f + 1)
                release(V_.tensor_tensor(v1[:, f % 4, :], bank_of(f"gu_{f}")[:, SEQ:2 * SEQ], sg[:, f % 4, :], ALU.mult),
                        f"gu_{f}")
                hidden_rest(f)
            dve.wait_ge(sem("final_in"), 16)
            Xn = two["Xn"].rearrange("p (t n) -> p t n", t=TT)
            for t in range(TT):
                residual([(t, nh, f"d1_{t}_{nh}") for nh in range(2)])
                signal(V_.tensor_tensor(Xn[:, t, :], X[:, t, :], att1["final"], ALU.mult), "gained")
            dve.wait_ge(sem("sq3"), 2)
            link(V_.tensor_scalar(st[:, 0:2], st[:, 0:2], 1.0 / D, EPS, ALU.mult, ALU.add))
            link(V_.tensor_scalar(st[:, 24:26], st[:, 0:2], EPS, None, ALU.mult))
            dve.wait_ge(sem("sq3"), 4)
            link(V_.scalar_tensor_tensor(out=st[:, 2:4], in0=st[:, 2:4], scalar=1.0 / D, in1=st[:, 24:26],
                                         op0=ALU.mult, op1=ALU.add))
            inv_sqrt(st[:, 4:8], st[:, 0:4], st[:, 24:28], st[:, 28:32], "rms3")
            dve.wait_ge(sem("gained"), 2)
            signal(V_.tensor_scalar(Xn[:, 0, :], Xn[:, 0, :], st[:, 6:7], None, ALU.mult), "norm3")
            for t in range(TT):
                signal(V_.scalar_tensor_tensor(out=X[:, t, :], in0=X[:, t, :], scalar=st[:, 4 + t:5 + t], in1=att1["final"],
                                               op0=ALU.mult, op1=ALU.mult), "x2")
            turned_rest(lambda k: f"norm3_{k}", hT, SEQ, lambda k: par("norm_mix")[:, k:k + 1])
            for t in range(TT):
                full(dve, f"small_{t}")
                ps = bank_of(f"small_{t}")
                step(V_.tensor_copy(sig[:, 16 + 48 * t:64 + 48 * t], ps[:, 16:64]))
                step(V_.tensor_copy(sig[:, 8 * t:8 * t + 8], ps[:, 0:8]))
                release(V_.tensor_tensor(soft[:, 8 * t:8 * t + 8], ps[:, 8:16], par("dt"), ALU.add), f"small_{t}")
            freed(dve, "small_0")
            freed(dve, "small_1")
            link(V_.tensor_scalar(soft[:, 32:48], soft[:, 0:16], -1.0, None, ALU.mult))
            signal(V_.tensor_tensor(soft[:, 16:32], soft[:, 0:16], soft[:, 32:48], ALU.max), "small_in")
            dve.wait_ge(sem("small_ln"), 1)
            link(V_.tensor_scalar(sig[:, :], sig[:, :], 1.0, None, ALU.add))
            link(V_.reciprocal(sig[:, :], sig[:, :]))
            link(V_.scalar_tensor_tensor(out=soft[:, 0:16], in0=soft[:, 0:16], scalar=0.0, in1=soft[:, 16:32],
                                         op0=ALU.max, op1=ALU.add))
            link(V_.tensor_scalar(soft[:, 48:56], soft[:, 48:56], -1.0, None, ALU.mult))
            signal(V_.tensor_tensor(gl[:, :, :], soft[:, 0:16].rearrange("p (t h) -> p t h", t=TT),
                                    soft[:, 48:56].unsqueeze(1).to_broadcast([P, TT, NH2]), ALU.mult), "gates")
            blk = nsa["blk"].rearrange("p (s l g n) -> p s l g n", s=2, l=16, g=NSG)
            for s_ in range(2):
                name = f"kvc_{s_}"
                full(dve, name)
                for g in range(NSG):
                    r = 64 * (g % 2)
                    src = bank_of(name)[r:r + 64, SEQ * (g // 2):SEQ * (g // 2) + SEQ]
                    for odd in range(2):
                        o = 64 * odd
                        view = bass.AP(tensor=src.tensor, offset=src.offset + odd,
                                       ap=[src.ap[0], [2, 16], [CS, NC]])
                        pos = par("pos_k" if s_ == 0 else "pos_v")[o:o + 64, :]
                        ins = V_.tensor_tensor(blk[o:o + 64, s_, :, g, :], view, bc(pos, [64, 16, NC]), ALU.add)
                        if g == NSG - 1 and odd == 1:
                            release(ins, name)
                        else:
                            step(ins)
            Q = nsa["Q"].rearrange("p (t n) -> p t n", t=TT)
            junk = nsa["O"]
            for n in range(2):
                for t in range(TT):
                    freed(dve, f"nq{n}_{t}")
            dve.wait_ge(sem("q_squares"), 4)
            link(V_.tensor_reduce(st[:, 64:96], junk.rearrange("p (h d) -> p h d", d=ND), AXX, ALU.add))
            inv_rms(st[:, 96:128], st[:, 64:96], ND, st[:, 128:160], st[:, 160:192])
            link(V_.tensor_scalar(st[:, 96:128], st[:, 96:128], ND ** -0.5, None, ALU.mult))
            for t in range(TT):
                v = Q[:, t, :].rearrange("p (h d) -> p h d", d=ND)
                signal(V_.tensor_tensor(v, v, bc(st[:, 96 + 16 * t:112 + 16 * t], [P, NSH, ND]), ALU.mult), "nq_norm")
            full(dve, "kvc2")
            kv2 = bank_of("kvc2")
            link(V_.tensor_copy(kcn[0:NC, :], kv2[0:NC, 0:256]))
            release(V_.tensor_copy(vc[0:NC, :], kv2[0:NC, 256:512]), "kvc2")
            link(V_.tensor_tensor(scr[0:NC, 0:256], kcn[0:NC, :], kcn[0:NC, :], ALU.mult))
            link(V_.tensor_reduce(st[0:NC, 64:68], scr[0:NC, 0:256].rearrange("p (h d) -> p h d", d=ND), AXX, ALU.add))
            inv_rms(st[0:NC, 68:72], st[0:NC, 64:68], ND, st[0:NC, 72:76], st[0:NC, 76:80])
            k4 = kcn[0:NC, :].rearrange("p (h d) -> p h d", d=ND)
            signal(V_.tensor_tensor(k4, k4, bc(st[0:NC, 68:72], [NC, NSG, ND]), ALU.mult), "kc_norm")
            for t in range(TT):
                freed(dve, f"nk_{t}")
            dve.wait_ge(sem("k_squares"), 2)
            dve.wait_ge(sem("kc_norm"), 1)
            link(V_.tensor_reduce(st[:, 64:80], nsa["Z"][:, 1024:2048].rearrange("p (h d) -> p h d", d=ND), AXX, ALU.add))
            inv_rms(st[:, 80:96], st[:, 64:80], ND, st[:, 128:144], st[:, 160:176])
            for t in range(TT):
                v = nsa["ksw"][:, 512 * t:512 * t + 512].rearrange("p (h d) -> p h d", d=ND)
                signal(V_.tensor_tensor(v, v, bc(st[:, 80 + 8 * t:88 + 8 * t], [P, 8, ND]), ALU.mult), "nk_norm")
            cv = nsa["cv"].rearrange("p (w h n) -> p w h n", w=3, h=NH2)
            taps = par("conv").rearrange("p (h j) -> p h j", j=4)

            def convolve(which, w, first, n):
                name = f"cv_{which}{first // 2 + n}"
                full(dve, name)
                both = [(first + 2 * n + j, bank_of(name)[:, SEQ * j:SEQ * j + SEQ]) for j in range(2)]
                for h, raw in both:
                    step(V_.tensor_scalar(cv[:, w, h, :], raw, taps[:, 8 * w + h, 3:4], None, ALU.mult))
                settle()
                for back in (1, 2, 3):
                    for h, raw in both:
                        o = cv[:, w, h, back:SEQ]
                        ins = V_.scalar_tensor_tensor(out=o, in0=raw[:, 0:SEQ - back], scalar=taps[:, 8 * w + h, 3 - back:4 - back],
                                                      in1=o, op0=ALU.mult, op1=ALU.add)
                        if back < 3:
                            step(ins)
                        else:
                            signal(ins, "conv_raw")
                    if back < 3:
                        settle()
                release(V_.tensor_copy(scr[:, 512 + n:513 + n], bank_of(name)[:, 0:1]), name)

            for n in range(4):
                convolve("k", 0, 4 * (n // 2), n % 2)
            for what in EARLY:
                convolve(*what)

            def finish_two(g):
                c0 = g["first"]
                name = f"pv_{g['name']}"
                b_ = {"cmp": 0, "slc": 1, "win": 2}[g["kind"]]
                t = g["qt"]
                dve.wait_ge(sem("probs2"), g["last"])
                link(V_.reciprocal(st[:, 24:28], sums[:, c0:c0 + 4]))
                gates = sig[:, 16 + 48 * t:64 + 48 * t].rearrange("p (h b) -> p h b", b=3)[:, g["hs"][0]:g["hs"][0] + 4, b_]
                link(V_.tensor_tensor(st[:, 24:28], st[:, 24:28], gates, ALU.mult))
                if b_ == 0:
                    link(V_.tensor_scalar(st[:, 24:28], st[:, 24:28], cst("valid")[:, t:t + 1], None, ALU.mult))
                full(dve, name)
                o = nsa["O"].rearrange("p (t h d) -> p t h d", t=TT, h=NSH)[:, t, g["hs"][0]:g["hs"][0] + 4, :]
                ps = bank_of(name)[:, 0:256].rearrange("p (h d) -> p h d", h=4)
                f4 = bc(st[:, 24:28], [P, 4, ND])
                if b_ == 0:
                    release(V_.tensor_tensor(o, ps, f4, ALU.mult), name)
                    freed(dve, name)
                else:
                    tmp = scr[:, 0:256].rearrange("p (h d) -> p h d", h=4)
                    release(V_.tensor_tensor(tmp, ps, f4, ALU.mult), name)
                    freed(dve, name)
                    link(V_.tensor_tensor(o, o, tmp, ALU.add))

            extra = dict(zip(FILL, FILLERS))
            peaks_of(G2[0])
            for i, g in enumerate(G2):
                if i + 1 < len(G2):
                    peaks_of(G2[i + 1])
                if i in extra:
                    convolve(*extra[i])
                if i >= 1:
                    finish_two(G2[i - 1])
            finish_two(G2[-1])
            Kt = dn["Kt"].rearrange("p (t h n) -> p t h n", t=TT, h=NH2)
            Vb = dn["Vb"].rearrange("p (t h n) -> p t h n", t=TT, h=NH2)
            pairs = [(t, q) for t in range(TT) for q in range(2)]

            def four(ap, q):
                return ap[:, GH * q:GH * q + GH]

            def heads_of(bank):
                return bank.rearrange("p (h n) -> p h n", h=GH)

            for t, q in pairs:
                full(dve, f"kt_{t}_{q}")
                dve.wait_ge(sem("key_squares"), 2 * t + q + 1)
                release(V_.tensor_copy(four(Kt[:, t], q), heads_of(bank_of(f"kt_{t}_{q}"))), f"kt_{t}_{q}")
            for t, q in pairs:
                freed(dve, f"kt_{t}_{q}")
            link(V_.tensor_reduce(st[:, 64:80], dn["LT"].rearrange("p (h d) -> p h d", d=P), AXX, ALU.add))
            inv_rms(st[:, 80:96], st[:, 64:80], 1, st[:, 128:144], st[:, 160:176])
            for t, q in pairs:
                v = four(Kt[:, t], q)
                signal(V_.tensor_tensor(v, v, bc(st[:, 80 + 8 * t + GH * q:84 + 8 * t + GH * q], [P, GH, P]), ALU.mult), "kn")
            for t, q in pairs:
                name = f"vt2_{t}_{q}"
                full(dve, name)
                release(V_.tensor_tensor(four(Vb[:, t], q), heads_of(bank_of(name)), bc(four(be[:, t], q), [P, GH, P]),
                                         ALU.mult), name)
            for t, q in pairs:
                freed(dve, f"qt2_{t}_{q}")
            link(V_.tensor_reduce(st[:, 64:80], dn["M"].rearrange("p (h d) -> p h d", d=P), AXX, ALU.add))
            rq = st[:, 96:112]
            inv_rms(rq, st[:, 64:80], 1, st[:, 128:144], st[:, 160:176])
            link(V_.tensor_scalar(rq, rq, P ** -0.5, None, ALU.mult))
            full(dve, "gc")
            release(V_.tensor_copy(gcb[:, 0:24], bank_of("gc")[:, 0:24]), "gc")
            freed(dve, "gc")
            signal(V_.tensor_tensor(gcb[:, 24:32], gcb[:, 16:24], gcb[:, 0:8], ALU.subtract), "gc_out")
            E4 = dn["DT"].rearrange("p (g n) -> p g n", g=4)
            for t, q in pairs:
                name = f"gr_{t}_{q}"
                full(dve, name)
                for n in range(GH):
                    s_ = slice(P * n, P * n + P)
                    h = 8 * t + GH * q + n
                    ins = V_.tensor_scalar(E4[:, 2 * t + q, s_], bank_of(name)[:, s_], gcb[:, h:h + 1], 0.0, ALU.subtract, ALU.min)
                    if n == GH - 1:
                        release(ins, name)
                    else:
                        step(ins)
            QKD = dn["QKD"].rearrange("p (g n) -> p g n", g=4)
            LT = dn["LT"].rearrange("p (g n) -> p g n", g=4)
            Yi = dn["Yi"].rearrange("p (g n) -> p g n", g=4)
            Xi = dn["Xi"].rearrange("p (g n) -> p g n", g=4)
            lev0 = cst("level")[:, 0:P].unsqueeze(1).to_broadcast([P, GH, P])
            dve.wait_ge(sem("level_in"), 16)
            idb = ident.unsqueeze(1).to_broadcast([P, GH, P])
            for t, q in pairs:
                g = 2 * t + q
                dve.wait_ge(sem("dec_masked"), g + 1)
                full(dve, f"qk_{t}_{q}")
                release(V_.tensor_tensor(QKD[:, g, :], bank_of(f"qk_{t}_{q}"), E4[:, g, :], ALU.mult), f"qk_{t}_{q}")
                full(dve, f"br_{t}_{q}")
                release(V_.tensor_tensor(Yi[:, g, :], bank_of(f"br_{t}_{q}"), E4[:, g, :], ALU.mult), f"br_{t}_{q}")
                freed(dve, f"br_{t}_{q}")
                release(V_.tensor_tensor(LT[:, g, :], bank_of(f"kk_{t}_{q}"), Yi[:, g, :], ALU.mult), f"kk_{t}_{q}")
                freed(dve, f"kk_{t}_{q}")
                link(V_.tensor_tensor(heads_of(Yi[:, g, :]), heads_of(LT[:, g, :]), lev0, ALU.mult))
                signal(V_.tensor_tensor(heads_of(Yi[:, g, :]), idb, heads_of(Yi[:, g, :]), ALU.subtract), "y_new")
            for lv in range(1, LEVELS):
                for g in range(4):
                    for what in (["dx", "dy"] if lv < LEVELS - 1 else ["dy"]):
                        name = f"{what}{lv}_{g}"
                        full(dve, name)
                        tgt = (Xi if what == "dx" else Yi)[:, g, :]
                        release(V_.tensor_tensor(tgt, tgt, bank_of(name), ALU.subtract), name)
            VN = cv[:, 0].rearrange("p h n -> p (h n)").rearrange("p (w h n) -> p w h n", w=2, h=NH2)
            L4 = dn["LT"].rearrange("p (w h n) -> p w h n", w=2, h=NH2)
            O4 = dn["Xi"].rearrange("p (t h n) -> p t h n", t=TT, h=NH2)
            dve.wait_ge(sem("gc_exp"), 2)
            link(V_.tensor_tensor(gcb[:, 48:56], gcb[:, 32:40], be[:, 1, :], ALU.mult))
            for q in range(2):
                freed(dve, f"vn_0_{q}")
                signal(V_.tensor_tensor(four(VN[:, 1], q), four(VN[:, 0], q), bc(gcb[:, 40 + GH * q:44 + GH * q], [P, GH, P]),
                                        ALU.mult), "vne")
            for q in range(2):
                full(dve, f"o_0_{q}")
                release(V_.tensor_copy(four(O4[:, 0], q), heads_of(bank_of(f"o_0_{q}"))), f"o_0_{q}")
            for q in range(2):
                name = f"ks_{q}"
                full(dve, name)
                release(V_.tensor_tensor(four(L4[:, 0], q), heads_of(bank_of(name)), bc(gcb[:, 48 + GH * q:52 + GH * q], [P, GH, P]),
                                         ALU.mult), name)
                freed(dve, name)
                v = four(Vb[:, 1], q)
                signal(V_.tensor_tensor(v, v, four(L4[:, 0], q), ALU.subtract), "vb1")
            for q in range(2):
                name = f"os_{q}"
                full(dve, name)
                release(V_.tensor_tensor(four(L4[:, 1], q), heads_of(bank_of(name)), bc(gcb[:, 32 + GH * q:36 + GH * q], [P, GH, P]),
                                         ALU.mult), name)
                freed(dve, name)
                name = f"o_1_{q}"
                release(V_.tensor_tensor(four(O4[:, 1], q), heads_of(bank_of(name)), four(L4[:, 1], q), ALU.add), name)
            for q in range(2):
                freed(dve, f"o_0_{q}")
                freed(dve, f"o_1_{q}")
            second_parts(INDEX["gn1.3"] + 1)
            link(V_.tensor_tensor(dn["LT"], dn["Xi"], dn["Xi"], ALU.mult))
            link(V_.tensor_reduce(st[:, 64:80], dn["LT"].rearrange("p (h d) -> p h d", d=P), AXX, ALU.add))
            link(V_.tensor_tensor(st[:, 64:80], st[:, 64:80], rq, ALU.mult))
            link(V_.tensor_tensor(st[:, 64:80], st[:, 64:80], rq, ALU.mult))
            inv_rms(st[:, 80:96], st[:, 64:80], P, st[:, 128:144], st[:, 160:176])
            link(V_.tensor_tensor(st[:, 80:96], st[:, 80:96], rq, ALU.mult))
            for t in range(TT):
                for n in range(2):
                    freed(dve, f"z{n}_{t}")
                link(V_.tensor_tensor(O4[:, t], O4[:, t], bc(st[:, 80 + 8 * t:88 + 8 * t], [P, NH2, P]), ALU.mult))
                signal(V_.tensor_tensor(O4[:, t], O4[:, t], nsa["Z"].rearrange("p (t h n) -> p t h n", t=TT, h=NH2)[:, t],
                                        ALU.mult), "dn_out")
            turned_rest(lambda k: f"onT_{k}", onT, SEQ)
            sgs = nsa["cv"][:, 4096:6144].rearrange("p (t n) -> p t n", t=TT)
            sgd = dn["QKD"].rearrange("p (t n) -> p t n", t=TT)
            mix = dn["Vb"].rearrange("p (t n) -> p t n", t=TT)
            tmp = dn["LT"].rearrange("p (t n) -> p t n", t=TT)
            def attention_share(n):
                for t in range(TT):
                    s_ = slice(512 * n, 512 * n + 512)
                    name = f"pn{n}_{t}"
                    freed(dve, f"gn{n}_{t}")
                    full(dve, name)
                    release(V_.tensor_tensor(mix[:, t, s_], bank_of(name), sgs[:, t, s_], ALU.mult), name)

            attention_share(0)
            turned_rest(lambda k: f"odT_{k}", odT, SEQ, lambda k: par("dn_out"))
            attention_share(1)
            for n in range(2):
                for t in range(TT):
                    s_ = slice(512 * n, 512 * n + 512)
                    name = f"pd{n}_{t}"
                    freed(dve, f"gd{n}_{t}")
                    full(dve, name)
                    release(V_.tensor_tensor(tmp[:, t, s_], bank_of(name), sgd[:, t, s_], ALU.mult), name)
                    freed(dve, name)
                    signal(V_.tensor_tensor(mix[:, t, s_], mix[:, t, s_], tmp[:, t, s_], ALU.add), "mix")
            turned_rest(lambda k: f"mixT_{k}", mixT, SEQ)
            residual([(t, nh, f"o2_{nh}_{t}") for nh in range(2) for t in range(TT)])
            norm_rows("norm4", dn["Vb"].rearrange("p (t n) -> p t n", t=TT), "sq4")
            turned_rest(lambda k: f"norm4_{k}", hT, SEQ, lambda k: par("norm_mlp")[:, k:k + 1])
            residual([(t, nh, f"d2_{t}_{nh}") for t in range(TT) for nh in range(2)])


def shape_constants():
    c = np.zeros((P, NCONST), np.float32)

    def put(name, value, rows=slice(0, P)):
        a, w = CONST[name]
        c[rows, a:a + w] = np.asarray(value, np.float32).reshape(-1, w)

    j, i = np.arange(P)[:, None], np.arange(P)[None, :]
    put("ident", j == i)
    put("upper", j <= i)
    put("level", np.stack([((j >> l) % 2 == 0) & ((i >> l) == (j >> l) + 1) for l in range(LEVELS)], 1).reshape(P, -1))
    dist = P + j - (np.arange(ALL)[None, :] - META)
    put("causal", np.where(dist >= 0, 0.0, NEG))
    dist = P + j - np.arange(2 * P)[None, :]
    put("negdist", np.where(dist >= 0, -dist.astype(np.float64), NEG))
    inv = np.float32(10000.0) ** (-np.arange(0, ROPE, 2, dtype=np.float32) / np.float32(ROPE))
    ang = (np.arange(ALL, dtype=np.float32)[:, None] * inv[None, :].astype(np.float32)).astype(np.float32)
    cos, sin = np.cos(ang).T, np.sin(ang).T
    put("cos", np.concatenate([cos, cos]), slice(64, 96))
    put("sin", np.concatenate([-sin, sin]), slice(64, 96))
    slopes = (2.0 ** (-8.0 * np.arange(1, NSH + 1) / NSH)).astype(np.float32)
    pos = (np.arange(TT)[None, :, None, None] * P + np.arange(P)[:, None, None, None])
    end = (np.arange(NC) * CS + CL - 1)[None, None, None, :]
    put("cmpbias", np.where(pos - end >= 0, -slopes[None, None, :, None] * (pos - end).astype(np.float32), NEG))
    put("valid", (np.arange(TT)[None, :] * P + np.arange(P)[:, None]) >= CL - 1)
    n = (ALL - 1) - np.arange(LINE)
    half = BUCKETS // 2
    nf = np.maximum(n, half).astype(np.float32)
    large = half + (np.log(nf / np.float32(half)) / np.float32(math.log(128 / half)) * np.float32(BUCKETS - half)).astype(np.int32)
    bucket = np.where(n < half, n, np.minimum(large, BUCKETS - 1))
    hot = np.zeros((BUCKETS + 1, 2, LINE), np.float32)
    for v in range(2):
        row = np.where((n < 0) | ((n >= WIN) if v else False), BUCKETS, bucket)
        hot[row, v, np.arange(LINE)] = 1.0
    put("onehot", hot, slice(0, BUCKETS + 1))
    return c


def laid_params(a):
    p = np.zeros((P, NPARAM), np.float32)

    def put(name, value, rows=slice(0, P)):
        at, w = PARAM[name]
        p[rows, at:at + w] = value

    def columns(v):
        return v.reshape(-1, P).T

    def everywhere(v):
        return np.broadcast_to(v.reshape(1, -1), (P, v.size))

    put("attn_norm", columns(a["attn_norm"]))
    put("ffn_norm", columns(a["ffn_norm"]))
    put("norm_mix", columns(a["norm_mix_2"]))
    put("norm_mlp", columns(a["norm_mlp_2"]))
    put("q_norm", columns(a["mla_q_norm"]))
    put("kv_norm", columns(a["mla_kv_norm"]))
    for name, src in [("subln", "diff_subln"), ("nsa_q", "nsa_q_norm_2"), ("k_cmp", "nsa_k_norm_cmp_2"),
                      ("k_slc", "nsa_k_norm_slc_2"), ("k_win", "nsa_k_norm_win_2")]:
        put(name, columns(np.concatenate([a[src].reshape(-1)] * 2)))
    put("dn_out", columns(a["dn_out_norm_2"]))
    conv = a["dn_conv_2"].reshape(4, 3, NH2, P)[:, [1, 2, 0]]
    put("conv", conv.transpose(3, 1, 2, 0).reshape(P, -1))
    put("w2k", a["cmp_w2_k_2"][0])
    put("w2v", a["cmp_w2_v_2"][0])
    for name, src in [("pos_k", "cmp_pos_k_2"), ("pos_v", "cmp_pos_v_2")]:
        put(name, a[src].reshape(CL // 2, P).T)
    put("rel", a["rel_bias"], slice(0, BUCKETS))
    put("lam", everywhere(a["diff_lambda"]))
    put("sinks", everywhere(a["swa_sinks"]))
    put("a_log", everywhere(a["dn_a_log_2"]))
    put("dt", everywhere(a["dn_dt_bias_2"]))
    put("final", everywhere(a["final_norm"]))
    return p


def laid_weights(a):
    flat = np.empty(TOTAL, np.float32)

    def put(name, value):
        value = value.reshape(P, -1)
        names = [name] if name in WIDTHS else [n for n in PIECES if n.rsplit(".", 1)[0] == name]
        cuts = np.cumsum([WIDTHS[n] for n in names])
        assert value.shape[1] == cuts[-1], (name, value.shape)
        for n, part in zip(names, np.split(value, cuts[:-1], axis=1)):
            flat[STARTS[n]:STARTS[n] + part.size] = part.reshape(-1)

    def features(w):
        k, m = w.shape
        return w.reshape(k // P, P, m // P, P).transpose(1, 2, 0, 3)

    def tokens(w):
        return w.reshape(-1, P, w.shape[1]).transpose(1, 0, 2)

    w = a["w_in"][0]
    cq, ckv, kr, dq, dk, dv, sq, sk, sv = np.split(w, np.cumsum([256, 128, 32, 256, 256, 256, 384, 128]), axis=1)
    sq = sq.reshape(D, 2, 3, 64).transpose(0, 2, 1, 3).reshape(D, 384)
    swapped = np.concatenate([kr[:, 16:], kr[:, :16]], 1)
    feat = features(np.concatenate([cq, ckv, dq, dk, sq, sk] + [kr] * 4 + [swapped] * 4, 1))
    for n, what in enumerate(FEATURES1):
        put("in1_" + what, feat[:, n])
    put("in1t", tokens(np.concatenate([dv, sv], 1)))
    wq = a["mla_w_qb"][0].reshape(2, P, MH, 96).transpose(1, 2, 0, 3)
    wq = np.concatenate([wq, wq[..., 80:96], wq[..., 64:80]], 3).reshape(P, -1)
    wkv = a["mla_w_kvb"][0].reshape(P, MH, 128)
    put("mla", np.concatenate([wq, wkv[:, :, :64].reshape(P, -1), wkv[:, :, 64:].reshape(P, -1)], 1))
    for n in range(2):
        put(f"out1_{n}", tokens(a["w_out"][0][:, 512 * n:512 * n + 512]))
    gate, up = features(a["w_gate"][0]), features(a["w_up"][0])
    down1 = a["w_down"][0].reshape(FT1, P, D).transpose(1, 0, 2)
    for f in range(FT1):
        put(f"gate.{f}", gate[:, f])
        put(f"up1.{f}", up[:, f])
        put(f"down1.{f}", down1[:, f])
    w = a["w_in_2"][0]
    sizes = [1024, 1024, 1024, 1024, 8, 8, 1024, 256, 256, 256, 256, 256, 256, 48, 1024, 1024]
    (q, k, v, z, _b, _a, nq, kc, vc, ks, vs, kw, vw, _g, gd, gn) = np.split(w, np.cumsum(sizes)[:-1], axis=1)
    nq = nq.reshape(D, 2, 8, ND).transpose(0, 2, 1, 3).reshape(D, D)
    ks, kw = (m.reshape(D, 2, 2, ND).transpose(0, 2, 1, 3).reshape(D, 256) for m in (ks, kw))
    for tag, m in [("qnsa", nq), ("z", z), ("gn", gn), ("gd", gd), ("pn", a["w_proj_nsa_2"][0]), ("pd", a["w_proj_dn_2"][0])]:
        for n in range(2):
            put(f"{tag}{n}", tokens(m[:, 512 * n:512 * n + 512]))
    for n in range(2):
        put(f"out2_{n}", tokens(a["w_out_2"][0][:, 512 * n:512 * n + 512]))
    put("ksw", tokens(np.concatenate([ks, kw], 1)))
    put("vsw", tokens(np.concatenate([vs, vw], 1)))
    put("kvc", features(np.concatenate([kc, vc], 1)))
    for tag, m in [("dk", k), ("dv", v), ("dq", q)]:
        for n in range(2):
            put(f"{tag}{n}", features(m[:, 512 * n:512 * n + 512]))
    w1 = np.stack([a["cmp_w1_k_2"][0], a["cmp_w1_v_2"][0]]).reshape(2, CL // 2, P, P)
    put("cmp", w1.transpose(2, 0, 1, 3))
    up2 = features(a["w_up_2"][0])
    down2 = a["w_down_2"][0].reshape(FT2, P, D).transpose(1, 0, 2)
    put("small", tokens(np.concatenate([_b, _a, _g], 1)))
    for f in range(FT2):
        put(f"up2.{f}", up2[:, f])
        put(f"down2.{f}", down2[:, f])
    return flat


def kernel(**inputs):
    import concourse.bacc as bacc
    from concourse.bass_utils import run_bass_kernel_spmd

    a = {k: np.asarray(v) for k, v in inputs.items()}
    arrays = {"consts": shape_constants(), "params": laid_params(a), "weights": laid_weights(a),
              "x": np.ascontiguousarray(a["x"][0]), "meta": np.ascontiguousarray(a["meta_tokens"])}
    nc = bacc.Bacc("TRN2", target_bir_lowering=False, num_devices=1)
    ins = {k: nc.dram_tensor(k, v.shape, F32, kind="ExternalInput").ap() for k, v in arrays.items()}
    out = nc.dram_tensor("out", (SEQ, D), F32, kind="ExternalOutput").ap()
    lines = nc.dram_tensor("lines", (P, BH, 2 * LINE), F32, kind="Internal").ap()
    build(nc, ins["consts"], ins["params"], ins["weights"], ins["x"], ins["meta"], out, lines)
    r = run_bass_kernel_spmd(nc, [arrays], core_ids=[0])
    return r.results[0]["out"].reshape(1, SEQ, D)
```
